# Optimizing a Trainium2 kernel written in Bass

```python
import math
import jax, jax.numpy as jnp
from jax import lax
import numpy as np

D_MODEL = 1024
BATCH = 1
SEQ = 512
DEPTH = 2
DEC_BATCH = 8
DEC_SEQ = 4
PAST_LEN = 1024
PAGE_SIZE = 128

N_BRANCH = 4
D_BR = D_MODEL // N_BRANCH
HEAD_DIM = 64
N_HEADS = D_BR // HEAD_DIM
CONV_W = 3
POOL_WINDOWS = (2, 4, 8, 16)
POOL_GROUP = D_BR // len(POOL_WINDOWS)
POOL_CTX = max(POOL_WINDOWS) - 1
RANK_W = D_MODEL // 16
RANK_A = D_MODEL // 16
RANK_G = D_MODEL // 8
D_CONV_IN = 3 * D_BR
D_RWKV_IN = 3 * D_BR + RANK_W + RANK_A + RANK_G
D_POOL_IN = D_BR
D_SB_IN = 3 * D_BR
D_IN = D_CONV_IN + D_RWKV_IN + D_POOL_IN + D_SB_IN
IN_SPLITS = (D_CONV_IN, D_CONV_IN + D_RWKV_IN, D_CONV_IN + D_RWKV_IN + D_POOL_IN)
RWKV_SPLITS = (D_BR, 2 * D_BR, 3 * D_BR, 3 * D_BR + RANK_W, 3 * D_BR + RANK_W + RANK_A)
D_FF = ((8 * D_MODEL // 3 + 127) // 128) * 128
N_MOD = 9
SB_BLOCK = 128
SB_BIAS_INIT = -8.0
EPS = 1e-6
LNX_EPS = 64e-5

kernel_name = 'hybrid_conv_rwkv7_pool_stickbreak_step'

def rmsnorm(x, g):
    xf = x.astype(jnp.float32)
    y = xf * lax.rsqrt(jnp.mean(xf * xf, axis=-1, keepdims=True) + EPS)
    return (y * g.astype(jnp.float32)).astype(x.dtype)

def heads(t):
    return t.reshape(t.shape[:-1] + (N_HEADS, HEAD_DIM)).astype(jnp.float32)

def swiglu(u, w_up, w_down):
    h = u @ w_up
    a, b = jnp.split(h, 2, axis=-1)
    return (jax.nn.silu(a) * b) @ w_down

def short_conv_mixer(p, conv_prev, conv_w):
    b_gate, c_gate, xv = jnp.split(p, 3, axis=-1)
    z = c_gate * xv
    z_ext = jnp.concatenate([conv_prev.astype(z.dtype), z], axis=1)
    T = z.shape[1]
    y = conv_w[0] * z_ext[:, 0:T]
    for i in range(1, CONV_W):
        y = y + conv_w[i] * z_ext[:, i:i + T]
    return b_gate * y, z_ext[:, -(CONV_W - 1):]

def rwkv7_mixer(p, shift_prev, wkv_prev, mu, w0, w_w2, a0, w_a2, w_g2, k_k, k_a, r_k, lnx_g, lnx_b):
    B, T, _ = p.shape
    p_prev = jnp.concatenate([shift_prev[:, None, :].astype(p.dtype), p[:, :-1]], axis=1)
    xs = p + (p_prev - p) * mu
    r, k, v, wd, ad, gd = jnp.split(xs, RWKV_SPLITS, axis=-1)
    w_log = -jax.nn.softplus(-(w0 + jnp.tanh(wd) @ w_w2)) - 0.5
    decay = jnp.exp(-jnp.exp(w_log.astype(jnp.float32)))
    a = jax.nn.sigmoid(a0 + ad @ w_a2)
    g = jax.nn.sigmoid(gd) @ w_g2
    kk = heads(k * k_k)
    kk = kk / jnp.maximum(jnp.sqrt(jnp.sum(kk * kk, axis=-1, keepdims=True)), 1e-12)
    k = k * (1.0 + (a - 1.0) * k_a)
    r_h, w_h, k_h, v_h, a_h = heads(r), heads(decay), heads(k), heads(v), heads(a)

    def step(S, inp):
        r_t, w_t, k_t, v_t, kk_t, a_t = inp
        sa = jnp.einsum('bhij,bhj->bhi', S, -kk_t)
        S = (S * w_t[:, :, None, :] + sa[..., None] * (kk_t * a_t)[:, :, None, :]
             + v_t[..., None] * k_t[:, :, None, :])
        return S, jnp.einsum('bhij,bhj->bhi', S, r_t)

    seq = tuple(jnp.moveaxis(t, 1, 0) for t in (r_h, w_h, k_h, v_h, kk, a_h))
    S_last, y = lax.scan(step, wkv_prev.astype(jnp.float32), seq)
    y = jnp.moveaxis(y, 0, 1)
    mean = jnp.mean(y, axis=-1, keepdims=True)
    var = jnp.mean(jnp.square(y - mean), axis=-1, keepdims=True)
    y = (y - mean) * lax.rsqrt(var + LNX_EPS) * heads(lnx_g) + heads(lnx_b)
    bonus = jnp.sum(r_h * k_h * heads(r_k), axis=-1, keepdims=True) * v_h
    out = (y + bonus).reshape(B, T, D_BR).astype(p.dtype) * g
    return out, p[:, -1], S_last

def pool_mixer(p, pool_prev, pos0, w_pool, pool_scale):
    B, T, _ = p.shape
    z_ext = jnp.concatenate([pool_prev.astype(p.dtype), p], axis=1).astype(jnp.float32)
    cs = jnp.concatenate([jnp.zeros((B, 1, D_BR), jnp.float32), jnp.cumsum(z_ext, axis=1)], axis=1)
    pos = pos0 + jnp.arange(T)
    outs = []
    for gi, w in enumerate(POOL_WINDOWS):
        sl = slice(gi * POOL_GROUP, (gi + 1) * POOL_GROUP)
        s = cs[:, POOL_CTX + 1:POOL_CTX + 1 + T, sl] - cs[:, POOL_CTX + 1 - w:POOL_CTX + 1 - w + T, sl]
        cnt = jnp.minimum(w, pos + 1).astype(jnp.float32)[None, :, None]
        outs.append(s / cnt - z_ext[:, POOL_CTX:, sl])
    d = jnp.stack(outs, axis=2).astype(p.dtype)
    y = jnp.einsum('btgc,gcd->btgd', d, w_pool).reshape(B, T, D_BR) * pool_scale
    return y, z_ext[:, -POOL_CTX:].astype(p.dtype)

def stick_breaking(q, k, v, qpos, kpos, sb_bias):
    z = jnp.einsum('bqhd,bkhd->bhqk', q.astype(jnp.float32), k.astype(jnp.float32)) * (HEAD_DIM ** -0.5)
    z = z + sb_bias.astype(jnp.float32)[None, :, None, None]
    causal = kpos[None, :] < qpos[:, None]
    log_keep = jnp.where(causal, jax.nn.log_sigmoid(-z), 0.0)
    after = lax.cumsum(log_keep, axis=3, reverse=True) - log_keep
    A = jnp.where(causal, jnp.exp(jax.nn.log_sigmoid(z) + after), 0.0)
    return jnp.einsum('bhqk,bkhd->bqhd', A, v.astype(jnp.float32)).astype(v.dtype)

def sb_attention(q, k_all, v_all, pos0, sb_bias):
    B, T, H, d = q.shape
    kpos = jnp.arange(k_all.shape[1])
    qpos = pos0 + jnp.arange(T)
    blk = SB_BLOCK if T % SB_BLOCK == 0 else T
    nb = T // blk
    qb = jnp.moveaxis(q.reshape(B, nb, blk, H, d), 1, 0)
    pb = qpos.reshape(nb, blk)
    o = lax.map(lambda args: stick_breaking(args[0], k_all, v_all, args[1], kpos, sb_bias), (qb, pb))
    return jnp.moveaxis(o, 0, 1).reshape(B, T, H * d)

def trunk_layer(l, x, c, pos0, k_past, v_past, conv_prev, shift_prev, wkv_prev, pool_prev, P):
    B, T, D = x.shape
    mod = (jax.nn.silu(c) @ P['ada_w'][l] + P['ada_b'][l]).reshape(B, N_MOD, D)
    sh1, sc1, g1, sh2, sc2, g2, sh3, sc3, g3 = [mod[:, i][:, None, :] for i in range(N_MOD)]
    ng = P['norm_g'][l]
    u = rmsnorm(x, ng[0]) * (1.0 + sc1) + sh1
    x = x + 0.5 * g1 * swiglu(u, P['w_ffn_up'][l, 0], P['w_ffn_down'][l, 0])
    u = rmsnorm(x, ng[1]) * (1.0 + sc2) + sh2
    proj = u @ P['w_in'][l]
    p_conv, p_rwkv, p_pool, p_sb = jnp.split(proj, IN_SPLITS, axis=-1)
    y_a, conv_new = short_conv_mixer(p_conv, conv_prev, P['conv_w'][l])
    y_b, shift_new, wkv_new = rwkv7_mixer(
        p_rwkv, shift_prev, wkv_prev, P['rwkv_mu'][l], P['rwkv_w0'][l], P['rwkv_w2'][l],
        P['rwkv_a0'][l], P['rwkv_a2'][l], P['rwkv_g2'][l], P['rwkv_k_k'][l], P['rwkv_k_a'][l],
        P['rwkv_r_k'][l], P['rwkv_lnx_g'][l], P['rwkv_lnx_b'][l])
    y_c, pool_new = pool_mixer(p_pool, pool_prev, pos0, P['pool_w'][l], P['pool_scale'][l])
    q, k, v = jnp.split(p_sb, 3, axis=-1)
    q = rmsnorm(q.reshape(B, T, N_HEADS, HEAD_DIM), P['q_norm_g'][l])
    k = rmsnorm(k.reshape(B, T, N_HEADS, HEAD_DIM), P['k_norm_g'][l])
    v = v.reshape(B, T, N_HEADS, HEAD_DIM)
    k_all = jnp.concatenate([k_past.astype(k.dtype), k], axis=1)
    v_all = jnp.concatenate([v_past.astype(v.dtype), v], axis=1)
    y_d = sb_attention(q, k_all, v_all, pos0, P['sb_bias'][l])
    merged = jnp.zeros_like(x)
    for i, y_i in enumerate((y_a, y_b, y_c, y_d)):
        merged = merged + jax.nn.sigmoid(u @ P['w_gate'][l, i]) * (y_i @ P['w_branch'][l, i])
    x = x + g2 * (merged @ P['w_out'][l])
    u = rmsnorm(x, ng[2]) * (1.0 + sc3) + sh3
    x = x + 0.5 * g3 * swiglu(u, P['w_ffn_up'][l, 1], P['w_ffn_down'][l, 1])
    return x, (k, v, conv_new, shift_new, wkv_new, pool_new)

def setup_inputs(seed: int = 0) -> dict:
    key = jax.random.key(seed)
    keys = list(jax.random.split(key, 48))
    f32 = jnp.float32
    L = DEPTH

    def nrm(shape, scale):
        return jax.random.normal(keys.pop(), shape, f32) * scale

    def near(shape, base):
        return base + nrm(shape, 0.02)

    n_pages = PAST_LEN // PAGE_SIZE
    n_used = DEC_BATCH * n_pages
    n_phys = (n_used * 5 + 3) // 4
    page_table = jax.random.permutation(keys.pop(), n_phys)[:n_used].reshape(DEC_BATCH, n_pages).astype(jnp.int32)
    return {
        'x_prompt': nrm((BATCH, SEQ, D_MODEL), 1.0),
        'x_sample': nrm((DEC_BATCH, DEC_SEQ, D_MODEL), 1.0),
        'c_prompt': nrm((BATCH, D_MODEL), 1.0),
        'c_sample': nrm((DEC_BATCH, D_MODEL), 1.0),
        'cache_k': nrm((L, n_phys, PAGE_SIZE, N_HEADS, HEAD_DIM), 1.0),
        'cache_v': nrm((L, n_phys, PAGE_SIZE, N_HEADS, HEAD_DIM), 1.0),
        'page_table': page_table,
        'state_conv': nrm((L, DEC_BATCH, CONV_W - 1, D_BR), 0.5),
        'state_shift': nrm((L, DEC_BATCH, D_RWKV_IN), 0.5),
        'state_wkv': nrm((L, DEC_BATCH, N_HEADS, HEAD_DIM, HEAD_DIM), 0.5),
        'state_pool': nrm((L, DEC_BATCH, POOL_CTX, D_BR), 0.5),
        'ada_w': nrm((L, D_MODEL, N_MOD * D_MODEL), 0.5 * D_MODEL ** -0.5),
        'ada_b': nrm((L, N_MOD * D_MODEL), 0.02),
        'norm_g': near((L, 3, D_MODEL), 1.0),
        'w_ffn_up': nrm((L, 2, D_MODEL, 2 * D_FF), D_MODEL ** -0.5),
        'w_ffn_down': nrm((L, 2, D_FF, D_MODEL), D_FF ** -0.5),
        'w_in': nrm((L, D_MODEL, D_IN), D_MODEL ** -0.5),
        'conv_w': nrm((L, CONV_W, D_BR), CONV_W ** -0.5),
        'rwkv_mu': jax.random.uniform(keys.pop(), (L, D_RWKV_IN), f32),
        'rwkv_w0': nrm((L, D_BR), 1.0),
        'rwkv_w2': nrm((L, RANK_W, D_BR), 0.1 * RANK_W ** -0.5),
        'rwkv_a0': nrm((L, D_BR), 0.1),
        'rwkv_a2': nrm((L, RANK_A, D_BR), RANK_A ** -0.5),
        'rwkv_g2': nrm((L, RANK_G, D_BR), RANK_G ** -0.5),
        'rwkv_k_k': near((L, D_BR), 0.85),
        'rwkv_k_a': near((L, D_BR), 1.0),
        'rwkv_r_k': nrm((L, D_BR), 0.1),
        'rwkv_lnx_g': near((L, D_BR), 1.0),
        'rwkv_lnx_b': nrm((L, D_BR), 0.02),
        'pool_w': nrm((L, len(POOL_WINDOWS), POOL_GROUP, POOL_GROUP), POOL_GROUP ** -0.5),
        'pool_scale': near((L, D_BR), 1.0),
        'q_norm_g': near((L, HEAD_DIM), 1.0),
        'k_norm_g': near((L, HEAD_DIM), 1.0),
        'sb_bias': SB_BIAS_INIT + nrm((L, N_HEADS), 0.5),
        'w_gate': nrm((L, N_BRANCH, D_MODEL, D_MODEL), D_MODEL ** -0.5),
        'w_branch': nrm((L, N_BRANCH, D_BR, D_MODEL), D_BR ** -0.5),
        'w_out': nrm((L, D_MODEL, D_MODEL), D_MODEL ** -0.5),
    }

def reference(x_prompt, x_sample, c_prompt, c_sample, cache_k, cache_v, page_table,
              state_conv, state_shift, state_wkv, state_pool,
              ada_w, ada_b, norm_g, w_ffn_up, w_ffn_down, w_in, conv_w,
              rwkv_mu, rwkv_w0, rwkv_w2, rwkv_a0, rwkv_a2, rwkv_g2, rwkv_k_k, rwkv_k_a, rwkv_r_k,
              rwkv_lnx_g, rwkv_lnx_b, pool_w, pool_scale, q_norm_g, k_norm_g, sb_bias,
              w_gate, w_branch, w_out):
    P = {'ada_w': ada_w, 'ada_b': ada_b, 'norm_g': norm_g, 'w_ffn_up': w_ffn_up,
         'w_ffn_down': w_ffn_down, 'w_in': w_in, 'conv_w': conv_w, 'rwkv_mu': rwkv_mu,
         'rwkv_w0': rwkv_w0, 'rwkv_w2': rwkv_w2, 'rwkv_a0': rwkv_a0, 'rwkv_a2': rwkv_a2,
         'rwkv_g2': rwkv_g2, 'rwkv_k_k': rwkv_k_k, 'rwkv_k_a': rwkv_k_a, 'rwkv_r_k': rwkv_r_k,
         'rwkv_lnx_g': rwkv_lnx_g, 'rwkv_lnx_b': rwkv_lnx_b, 'pool_w': pool_w,
         'pool_scale': pool_scale, 'q_norm_g': q_norm_g, 'k_norm_g': k_norm_g, 'sb_bias': sb_bias,
         'w_gate': w_gate, 'w_branch': w_branch, 'w_out': w_out}
    bp = x_prompt.shape[0]
    bs = x_sample.shape[0]
    n_pages = page_table.shape[1]
    past_len = n_pages * PAGE_SIZE
    dt = x_prompt.dtype
    hp, hs = x_prompt, x_sample
    new_p = [[] for _ in range(6)]
    new_s = [[] for _ in range(6)]
    for l in range(DEPTH):
        hp, st_p = trunk_layer(
            l, hp, c_prompt, 0,
            jnp.zeros((bp, 0, N_HEADS, HEAD_DIM), dt), jnp.zeros((bp, 0, N_HEADS, HEAD_DIM), dt),
            jnp.zeros((bp, CONV_W - 1, D_BR), dt), jnp.zeros((bp, D_RWKV_IN), dt),
            jnp.zeros((bp, N_HEADS, HEAD_DIM, HEAD_DIM), jnp.float32),
            jnp.zeros((bp, POOL_CTX, D_BR), dt), P)
        k_past = cache_k[l][page_table].reshape(bs, past_len, N_HEADS, HEAD_DIM)
        v_past = cache_v[l][page_table].reshape(bs, past_len, N_HEADS, HEAD_DIM)
        hs, st_s = trunk_layer(l, hs, c_sample, past_len, k_past, v_past, state_conv[l],
                               state_shift[l], state_wkv[l], state_pool[l], P)
        for lst, a in zip(new_p, st_p):
            lst.append(a)
        for lst, a in zip(new_s, st_s):
            lst.append(a)
    k_prompt, v_prompt, conv_prompt, shift_prompt, wkv_prompt, pool_prompt = [jnp.stack(a, axis=0) for a in new_p]
    k_sample, v_sample, conv_sample, shift_sample, wkv_sample, pool_sample = [jnp.stack(a, axis=0) for a in new_s]
    return (hp, hs, k_prompt, v_prompt, conv_prompt, shift_prompt, wkv_prompt, pool_prompt,
            k_sample, v_sample, conv_sample, shift_sample, wkv_sample, pool_sample)


_drawn_inputs = setup_inputs


def setup_inputs(seed=0):
    import zlib

    import numpy as np

    out = dict(_drawn_inputs(seed))
    spreads = {}
    factors = {'cache_k': 8.0,
     'cache_v': 8.0,
     'rwkv_w2': 4.05,
     'rwkv_k_k': 8.0,
     'rwkv_lnx_g': 8.0,
     'rwkv_lnx_b': 8.0,
     'pool_scale': 8.0,
     'q_norm_g': 8.0,
     'k_norm_g': 2.812,
     'sb_bias': 6.499}
    for name, (base, spread) in spreads.items():
        noise = np.random.default_rng([zlib.crc32(name.encode()), seed]).standard_normal(out[name].shape)
        drawn = base * np.exp(spread * noise) if base else spread * noise
        out[name] = __import__('jax').numpy.asarray(drawn.astype(out[name].dtype))
    for name, factor in factors.items():
        out[name] = (out[name] * factor).astype(out[name].dtype)
    return out
```

```python
from contextlib import ExitStack

import numpy as np

import concourse.bass as bass
from concourse import mybir

F32 = mybir.dt.float32
I32 = mybir.dt.int32
ALU = mybir.AluOpType
ACT = mybir.ActivationFunctionType

P = 128
D_MODEL, DEPTH = 1024, 2
KT = D_MODEL // P
TP, NSEQ, TD = 512, 8, 4
TS = NSEQ * TD
T = TP + TS
HALF = T // 2
NTT = TP // P
D_BR, HD, NH = 256, 64, 4
FF = 2816
FT = FF // P
DOWN_K = FT // 2
D_IN = 2816
NIN = D_IN // P
PAGE, NPAGE, NPHYS = 128, 8, 80
CH = 64
EPS, LNX_EPS = 1e-6, 64e-5
WINDOWS = (2, 4, 8, 16)
CTX = 15
R = 4
PANEL = 2048
NEG = -1e30

P_CONV, P_RWKV, P_POOL, P_Q, P_K, P_V = 0, 6, 14, 16, 18, 20
IN_ORDER = (8, 9, 10, 7, 0, 1, 2, 3, 4, 5, 6)
NBOTH = 7

(IDENT, ONES, BLK, TRI, CAUS, CNEG, M16U, M16L, E32L, E64L, SU64, LE64) = [P * i for i in range(12)]
S4U = 12 * P
S4L, LE4, NEG4 = S4U + TS, S4U + 2 * TS, S4U + 3 * TS
SCANM = S4U + 4 * TS
INVC = SCANM + T
SEQM = INVC + 32
BIAS = SEQM + NSEQ
NCST = BIAS + 3


def constants():
    c = np.zeros((P, NCST), np.float32)
    i, j = np.meshgrid(np.arange(P), np.arange(P), indexing="ij")

    def same(n):
        return i // n == j // n

    for at, m in ((IDENT, i == j), (ONES, i >= 0), (BLK, same(HD)), (TRI, i >= j), (CAUS, i < j),
                  (M16U, same(16) & (i < j)), (M16L, same(16) & (i > j)),
                  (E32L, same(32) & ~same(16) & (i > j)), (E64L, same(64) & ~same(32) & (i > j)),
                  (SU64, same(CH) & (i < j)), (LE64, same(CH) & (i <= j))):
        c[:, at:at + P] = m
    c[:, CNEG:CNEG + P] = np.where(i < j, 0.0, NEG)
    s = slice(0, TS)
    c[s, S4U:S4U + TS] = (same(TD) & (i < j))[s, s]
    c[s, S4L:S4L + TS] = (same(TD) & (i > j))[s, s]
    c[s, LE4:LE4 + TS] = (same(TD) & (i <= j))[s, s]
    c[s, NEG4:NEG4 + TS] = np.where(same(TD) & (i < j), 0.0, NEG)[s, s]
    t = np.arange(T)
    c[:, SCANM:SCANM + T] = np.where(t < TP, t % CH != 0, (t - TP) % TD != 0)
    for g, w in enumerate(WINDOWS):
        c[(g % 2) * 64:(g % 2) * 64 + 64, INVC + 16 * (g // 2):INVC + 16 * (g // 2) + 16] = (
            np.float32(1) / np.minimum(w, np.arange(16) + 1).astype(np.float32))
    c[s, SEQM:SEQM + NSEQ] = i[s, 0:NSEQ] // TD == j[s, 0:NSEQ]
    c[:, BIAS:BIAS + 3] = (EPS, HD * EPS, LNX_EPS)
    return c


ADAB, NG, MU, CW, W0, A0, KK_, KA, RK, LG, LB, PSC, QN, KN, SBB = (
    0, 72, 96, 104, 110, 112, 114, 116, 118, 120, 122, 124, 126, 127, 128)
W2A2, G2, PBD = 132, 132 + 256, 132 + 512
SCONV = PBD + 256
SSHIFT = SCONV + 2 * NSEQ * 2
SPOOL = SSHIFT + 8 * NSEQ
SWKV = SPOOL + 2 * NSEQ * CTX
NLP = SWKV + 2 * NSEQ * HD

SEG = {0: (0, 0, 512), 1: (1, 0, 384), 2: (2, 0, 256), 3: (1, 384, 128)}
OFF = {kt: 512 * b + c for kt, (b, c, _) in SEG.items()}

ADA_FIRST, ADA_IN = 8, 6
STAGES = [("ada", ADA_FIRST, ADA_FIRST), ("up0", 2 * FT, 3 * FT), ("down0", 16, 16),
          ("in", 11 + ADA_IN, 22 + ADA_IN), ("gate", 16, 64), ("out", 4, 8), ("up1", FT, 2 * FT),
          ("down1", 16, 16)]
assert ADA_FIRST + FT + ADA_IN == 36
PART0, _at = {}, 0
for _n, _, _k in STAGES:
    PART0[_n] = _at
    _at += _k
PARTS = _at
LOAD0 = {}
_cnt = [0] * R
for _n, _k, _ in STAGES:
    LOAD0[_n] = list(_cnt)
    _cnt = [c + (_k - s + R - 1) // R for s, c in enumerate(_cnt)]
LOADS = _cnt


def in_place(j):
    return (2 * j, 3 * j) if j < ADA_IN else (j + ADA_IN, 2 * j + ADA_IN)


def last_part(stage, n):
    if stage == "ada":
        k = n + 1
    elif stage == "up0":
        k = n // 2 * 3 + 2 + n % 2
    elif stage == "in":
        k = n // 2 * 3 + 2 + n % 2 if n < 2 * ADA_IN else 2 * (n - ADA_IN) + 2 + ADA_IN
    elif stage.startswith("down"):
        k = n + 1
    elif stage == "gate":
        k = (n // 4) * 16 + (n % 4) * 4 + 3
    else:
        k = 2 * n + 2
    return PART0[stage] + k


PART_STEP = {"ada": 4, "up0": 6, "up1": 8, "down0": 4, "down1": 4, "gate": 16, "out": 8}

VEC_LINKS, ACT_LINKS, RW_LINKS = 100, 17, 1


class Signal:

    def __init__(self, sem, per_layer, credit=0, unit=1):
        self.sem, self.per_layer, self.credit, self.unit = sem, per_layer, credit, unit

    def upto(self, layer, n):
        return layer * (self.per_layer * self.unit) + (n * self.unit + self.credit)


def build(nc, xT, cT, cst_d, lp_d, pages_d, w_ada, w_up, w_down, w_in, w_gate, w_branch, w_out,
          cache_d, o_y, o_k, o_v, o_conv, o_shift, o_wkv, o_pool):
    ctx = ExitStack()
    with ctx:
        def sb(name, shape, dt=F32):
            return ctx.enter_context(nc.sbuf_tensor(name, shape, dt))

        def signal(name, per_layer, credit=0, unit=1):
            return Signal(ctx.enter_context(nc.semaphore(name)), per_layer, credit, unit)

        x = sb("x", [P, KT, T])
        u = sb("u", [P, KT, T])
        proj = sb("proj", [P, NIN, T])
        y = sb("y", [P, KT, T])
        ring = sb("ring", [P, R, PANEL])
        wbr = sb("wbr", [P, PANEL])
        cst = sb("cst", [P, NCST])
        lp = sb("lp", [P, NLP])
        mod = sb("mod", [P, 72, 9])
        mod_a = sb("mod_a", [P, 24, 9])
        csil = sb("csil", [P, KT, 9])
        stage_out = sb("stage_out", [P, 2 * 18 + 8 * 9 + 2 * 9 * CTX])
        pages = sb("pages", [1, NSEQ * NPAGE], I32)
        ws = sb("ws", [P, 10760])
        hid, merged = proj, proj
        so_conv = stage_out[:, 0:36].rearrange("p (f n) -> p f n", f=2)
        so_shift = stage_out[:, 36:108].rearrange("p (f n) -> p f n", f=8)
        so_pool = stage_out[:, 108:378].rearrange("p (f n) -> p f n", f=2)

        def carve(at, *shape):
            n = int(np.prod(shape))
            v = ws[:, at:at + n]
            if len(shape) == 2:
                v = v.rearrange("p (a b) -> p a b", a=shape[0])
            if len(shape) == 3:
                v = v.rearrange("p (a b c) -> p a b c", a=shape[0], b=shape[1])
            if len(shape) == 4:
                v = v.rearrange("p (a b c d) -> p a b c d", a=shape[0], b=shape[1], c=shape[2])
            return v, at + n

        CR = 4 * 1024
        cache, at = carve(0, 4, 4, 256)
        sq, at1 = carve(at, 2, T)
        rs, at1 = carve(at1, T)
        gt, at1 = carve(at1, 2, T)
        ptmp, at1 = carve(at1, T)
        zc, at1 = carve(at, 2, TP + 2)
        zs, at1 = carve(at1, 2, NSEQ, TD + 2)
        pe, at1 = carve(at1, 2, TP + CTX)
        pes, at1 = carve(at1, 2, NSEQ, TD + CTX)
        s2s, at1 = carve(at1, 2, NSEQ, 18)
        s4s, at1 = carve(at1, 2, NSEQ, 16)
        s8s, at1 = carve(at1, 2, NSEQ, 12)
        s16s, at1 = carve(at1, 2, NSEQ, 4)
        pd, at1 = carve(at1, 2, T)
        fix, at1 = carve(at1, 2, 16)
        conv_end = at1
        NZ = 1280
        vtok, at1 = carve(at, 5, 256)
        spn, at1 = carve(at1, P)
        zbn, at1 = carve(at1, P)
        tn, at1 = carve(at1, P)
        qp, at1 = carve(at1, 2, NSEQ, 8)
        atq = at1
        sqk, at1 = carve(10760 - 4 * T, 4, T)
        assert conv_end <= 10760 - 4 * T
        zb, at1 = carve(atq, NZ)
        sp, at1 = carve(at1, NZ)
        sa, at1 = carve(at1, NZ)
        rd, at1 = carve(at1, 7, P)
        assert at1 <= 10760, at1
        at = CR
        Bt, at = carve(at, 2, P)
        At, at = carve(at, 2, P)
        Rt, at = carve(at, 2, P)
        Kt_, at = carve(at, 2, P)
        Bp, at = carve(at, 2, P)
        Kp, at = carve(at, 2, P)
        AtP, at = carve(at, 4, P)
        RtP, at = carve(at, 4, P)
        BtP, at = carve(at, 4, P)
        mat0 = at
        MA, at = carve(at, 4, P)
        MB, at = carve(at, 4, P)
        MC, at = carve(at, 4, P)
        MD, at = carve(at, 4, P)
        ME, at = carve(at, 4, P)
        MF, at = carve(at, 4, P)
        ET32, at = carve(at, 4, P)
        sam, _ = carve(mat0, NSEQ, 256)
        assert at <= 10760, at
        xs = proj[:, 14:22, :]
        e1, e3 = proj[:, 0:2, :], proj[:, 2:4, :]
        e2, bon = proj[:, 4:6, :], proj[:, 6:8, :]
        kkv, bv = proj[:, 8:10, :], proj[:, 10:12, :]
        gg = proj[:, 12:14, :]
        r_, k_, v_ = xs[:, 0:2, :], xs[:, 2:4, :], xs[:, 4:6, :]
        xt2 = xs[:, 6:8, :]
        yb = y[:, 2:4, :]
        wb = wbr[:, :]
        E64 = wb[:, 0:512].rearrange("p (h n) -> p h n", h=4)
        LakT = wb[:, 512:1024].rearrange("p (h n) -> p h n", h=4)
        MrbT = wb[:, 1024:1536].rearrange("p (h n) -> p h n", h=4)
        MrkT = wb[:, 1536:2048].rearrange("p (h n) -> p h n", h=4)
        xtf = xt2.rearrange("p f n -> p (f n)")
        turned, vt, r0 = xtf[:, 0:512], xtf[:, 512:768], xtf[:, 768:1024]
        bptok, kptok = xtf[:, 0:256], xtf[:, 256:512]
        rtail = sb("rtail", [P, 3 * 256 + 4 + 16])
        sat = rtail[:, 0:256]
        sbd = rtail[:, 256:512].rearrange("p (f n) -> p f n", f=2)
        stmp = rtail[:, 512:768].rearrange("p (f n) -> p f n", f=2)
        pend = rtail[:, 768:772].rearrange("p (f n) -> p f n", f=2)
        pends = rtail[:, 772:788].rearrange("p (f n) -> p f n", f=2)
        ps = ctx.enter_context(nc.psum_tensor("ps", [P, 8, 512], F32))

        MODC = 480

        def pair(b):
            return ps[:, 2 * b:2 * b + 2, 0:HALF]

        def halves(v):
            return v.rearrange("p (a n) -> p a n", a=2)

        pause = sb("pause", [P, 32])
        paused = [0]

        def pause_col():
            paused[0] += 1
            return pause[:, paused[0] - 1:paused[0]]

        def settled(bank=None):
            if bank is None:
                nc.vector.memset(pause_col(), 0.0)
            else:
                nc.tensor.matmul(ps[:, bank, 0:1], cst[:, ONES:ONES + P], cst[:, 0:1], start=True, stop=True)

        def next_bank(q):
            return 4 * ((q + 1) % 2) + 3

        def kept(j, c):
            if j < NBOTH:
                return (in_dve if c else in_act), j + 1
            return in_act, NBOTH + 2 * (j - NBOTH) + c + 1

        def col(at, n=1):
            return lp[:, at:at + n]

        def seqs(v):
            return v.rearrange("p (s t) -> p s t", s=NSEQ)

        def over(v, n):
            return v.unsqueeze(2).to_broadcast([v.shape[0], v.shape[1], n])

        def across(v, n):
            return v.unsqueeze(1).to_broadcast([v.shape[0], n, v.shape[1]])

        loaded = [signal(f"panel_loaded{s}", LOADS[s], unit=16) for s in range(R)]
        branch_loaded = signal("branch_loaded", 4, unit=16)
        lp_loaded = signal("params_loaded", 1, unit=16)
        start_loaded = signal("start_loaded", 0, unit=16)
        pages_loaded = signal("pages_loaded", 0, unit=16)
        cache_loaded = [signal(f"cache_loaded{s}", 8 * 4, unit=16) for s in range(4)]
        stored = signal("states_stored", 3, credit=16, unit=16)
        kv_stored = signal("kv_stored", 2, unit=16)
        wkv_stored = signal("wkv_stored", 3, credit=16, unit=16)
        y_stored = signal("y_stored", 0, unit=16)
        part = signal("part_done", PARTS, credit=1)
        mod_done = signal("mod_tiles", 36, credit=4)
        csil_done = signal("csil_done", 0)
        sq_done = signal("squares", 24)
        sum_done = signal("square_sums", 24)
        rt_done = signal("roots", 3)
        un_done = signal("normed", 24)
        up_done = signal("u_prompt", 24)
        us_done = signal("u_sample", 3)
        silu_done = signal("silu", 2 * FT)
        h_done = signal("hidden", 2 * FT, credit=2)
        x_done = signal("x_tiles", 24, credit=2)
        in_act = signal("proj_act", 22 - NBOTH, credit=2)
        in_dve = signal("proj_dve", NBOTH, credit=2)
        gate_done = signal("gate_sigmoid", 32)
        merge_done = signal("merged", 32, credit=2)
        so_ready = signal("states_staged", 3)
        kn_ready = signal("k_normed", 1)
        wkv_ready = signal("wkv_ready", 1)
        mix_done = signal("mix_done", 1, credit=1)
        pool_in = signal("pool_in", 1)
        pool_pe = signal("pool_products", 1)
        pool_out = signal("pool_out", 1)
        qk_sq = signal("qk_squares", 1)
        qk_sum = signal("qk_sums", 1)
        qk_ms = signal("qk_logs", 1)
        qk_rt = signal("qk_roots", 1)
        vt_pe = signal("v_turned", 1)
        vt_act = signal("v_tokens", 1)
        qp_done = signal("q_padded", 1)
        cache_used = signal("cache_used", 32, credit=4)
        at_pe = signal("att_products", 4 * 3)
        at_dve = signal("att_vector", 4 * 3)
        at_act = signal("att_scalar", 4 * 3)
        de_pe = signal("dec_products", 2)
        de_dve = signal("dec_vector", 4)
        de_act = signal("dec_scalar", 2)
        RW_PE, RW_DVE, RW_ACT = 10 + 2 * 3 + 1, 8 + 2 * 2 + 1, 6 + 2
        rp_pe = signal("rwkv_pre_products", 3)
        rp_dve = signal("rwkv_pre_vector", 6)
        rp_act = signal("rwkv_pre_scalar", 7)
        rw_pe = signal("rwkv_tile_products", NTT * RW_PE)
        rw_dve = signal("rwkv_tile_vector", NTT * RW_DVE)
        rw_act = signal("rwkv_tile_scalar", NTT * RW_ACT)
        rs_pe = signal("rwkv_sample_products", 7)
        rs_dve = signal("rwkv_sample_vector", 6)
        rs_act = signal("rwkv_sample_scalar", 3)
        gn_pe = signal("group_norm_sums", 2)
        gn_dve = signal("group_norm_vector", 2)
        gn_act = signal("group_norm_root", 1)
        vec = signal("vector_chain", VEC_LINKS)
        act_own = signal("scalar_chain", ACT_LINKS)

        block = ctx.enter_context(nc.Block())

        @block.sync
        def _(sp_):
            sp_.dma_start(cst[:, :], cst_d).then_inc(start_loaded.sem, 16)
            sp_.dma_start(csil[:, :, :], cT).then_inc(start_loaded.sem, 16)
            sp_.dma_start(x[:, :, :], xT).then_inc(start_loaded.sem, 16)

            srcs = {"up1": w_up, "down0": w_down, "down1": w_down, "gate": w_gate, "out": w_out}

            def source(stage, l, i, s):
                if stage == "ada":
                    return w_ada[l * 36 + i]
                if stage == "up0":
                    turn = i // R if isinstance(i, int) else i
                    if s % 2:
                        return w_ada[l * 36 + (turn * 2 + (ADA_FIRST + s // 2))]
                    return w_up[l * (2 * FT) + (turn * 2 + s // 2)]
                if stage == "in":
                    if i < 2 * ADA_IN and i % 2:
                        return w_ada[l * 36 + (ADA_FIRST + FT + i // 2)]
                    return w_in[l * 11 + (i // 2 if i < 2 * ADA_IN else i - ADA_IN)]
                f, n = int(stage[-1] == "1"), {"u": FT, "d": 16, "g": 16, "o": 4}[stage[0]]
                per = (2 if stage[:-1] in ("up", "down") else 1) * n
                return srcs[stage][l * per + (i + f * n)]

            with sp_.Fori(0, DEPTH) as l:
                sp_.wait_ge(mix_done.sem, mix_done.upto(l, 0))
                sp_.wait_ge(wkv_stored.sem, wkv_stored.upto(l, 0))
                sp_.dma_start(lp[:, :], lp_d[l]).then_inc(lp_loaded.sem, 16)

                prev = [None] * R
                for stage, n, _ in STAGES:
                    width = DOWN_K * P if stage.startswith("down") else PANEL

                    def load(i, s, wait):
                        sp_.wait_ge(part.sem, wait)
                        sp_.dma_start(ring[:, s, 0:width], source(stage, l, i, s))\
                            .then_inc(loaded[s].sem, 16)

                    for s in range(min(R, n)):
                        load(s, s, part.upto(l, 0 if prev[s] is None else prev[s]))
                        if stage == "gate" and s == R - 1:
                            sp_.wait_ge(mix_done.sem, mix_done.upto(l, 1))
                            sp_.dma_start(wbr[:, :], w_branch[l * 4]).then_inc(branch_loaded.sem, 16)
                    trips = n // R if stage != "in" else 1
                    if trips > 1:
                        with sp_.Fori(1, trips) as it:
                            for s in range(R):
                                load(it if stage == "up0" else it * R + s, s, part.upto(l, last_part(stage, s) - PART_STEP[stage]
                                                              + it * PART_STEP[stage]))
                                if stage == "gate" and s == R - 1:
                                    sp_.wait_ge(part.sem, part.upto(l, PART0["gate"] + it * 16))
                                    sp_.dma_start(wbr[:, :], w_branch[l * 4 + it])\
                                        .then_inc(branch_loaded.sem, 16)
                    for i in range(max(trips, 1) * R, n):
                        load(i, i % R, part.upto(l, last_part(stage, i - R)))
                    for s in range(R):
                        m = (n - 1 - s) // R * R + s
                        prev[s] = last_part(stage, m)
            sp_.wait_ge(x_done.sem, x_done.upto(DEPTH, 0))
            sp_.dma_start(o_y, x[:, :, :]).then_inc(y_stored.sem, 16)
            sp_.wait_ge(y_stored.sem, 16)
            sp_.wait_ge(stored.sem, stored.upto(DEPTH, 0))
            sp_.wait_ge(kv_stored.sem, kv_stored.upto(DEPTH, 0))
            sp_.wait_ge(wkv_stored.sem, wkv_stored.upto(DEPTH, 0))

        @block.gpsimd
        def _(pool):
            pool.dma_start(pages[:, :], pages_d).then_inc(pages_loaded.sem, 16)
            pool.wait_ge(pages_loaded.sem, 16)
            with pool.Fori(0, DEPTH) as l:
                with pool.Fori(0, 2) as kv:
                    with pool.Fori(0, 4) as turn:
                        for s in range(4):
                            n = kv * 16 + turn * 4 + s
                            pool.wait_ge(cache_used.sem, cache_used.upto(l, n - 3))
                            for pg in range(4):
                                page = pool.value_load(
                                    pages[0:1, bass.ds(turn * 16 + (4 * s + pg), 1)],
                                    min_val=0, max_val=NPHYS - 1)
                                dst = cache[:, s, pg, :]
                                pool.dma_start(dst, cache_d[kv * (DEPTH * NPHYS) + l * NPHYS + page])\
                                    .then_inc(cache_loaded[s].sem, 16)

        @block.tensor
        def _(pe_):
            def mm(out, lhsT, rhs, start=True, stop=True, skip=False):
                return nc.tensor.matmul(out, lhsT, rhs, start=start, stop=stop, skip_group_check=skip)

            def cmat(at, n=P, rows=P):
                return cst[0:rows, at:at + n]

            def tile(b, w, c0, rhs, k0=0, nk=KT, ks=256, first=True, last=True):
                for k in range(nk):
                    for hf in range(2):
                        m = mm(ps[:, 2 * b + hf, 0:HALF], w[:, k * ks + c0:k * ks + c0 + P],
                               rhs[:, k0 + k, hf * HALF:hf * HALF + HALF],
                               start=first and k == 0, stop=last and k == nk - 1)
                return m

            def panel(l, stage, it, s, turn=0):
                pe_.wait_ge(loaded[s].sem, loaded[s].upto(l, LOAD0[stage][s] + turn + 1 + it))

            def sum_squares(l, n):
                for k in range(KT):
                    pe_.wait_ge(sq_done.sem, sq_done.upto(l, 8 * n + k + 1))
                    for hf in range(2):
                        m = mm(ps[:, 6 + hf, 0:HALF], cmat(ONES), sq[:, k % 2, hf * HALF:hf * HALF + HALF],
                               start=k == 0, stop=k == KT - 1)
                    m.then_inc(sum_done.sem, 1)

            def wait_u(l, n):
                pe_.wait_ge(up_done.sem, up_done.upto(l, 8 * n + 8))
                pe_.wait_ge(us_done.sem, us_done.upto(l, n + 1))

            def modulation(s, bank):
                for c in range(2):
                    for k in range(KT):
                        m = mm(ps[:, bank, MODC + c * 9:MODC + c * 9 + 9],
                               ring[:, s, k * 256 + c * P:k * 256 + c * P + P], csil[:, k, :],
                               start=k == 0, stop=k == KT - 1)
                m.then_inc(part.sem, 1)

            def ffn(l, f):
                sum_squares(l, 2 * f)
                wait_u(l, 2 * f)

                def up_turn(it, first, units):
                    for q in range(first, first + units):
                        place, per_turn = (2 * q, 2) if f == 0 else (q, 1)
                        s = place % R
                        panel(l, f"up{f}", it * per_turn, s, place // R)
                        pe_.wait_ge(h_done.sem, h_done.upto(l, f * FT + q - 1 + it * 4))
                        b = 2 * (q % 2)
                        tile(b, ring[:, s, :], 0, u).then_inc(part.sem, 1)
                        if f == 0:
                            pe_.wait_ge(mod_done.sem, mod_done.upto(l, ADA_FIRST + q + it * 4))
                        tile(b + 1, ring[:, s, :], P, u).then_inc(part.sem, 1)
                        if f == 0:
                            panel(l, "up0", it * 2, s + 1, place // R)
                            pe_.wait_ge(h_done.sem, h_done.upto(l, q + it * 4))
                            modulation(s + 1, next_bank(q))

                settled(6)
                with pe_.Fori(0, FT // 4) as it:
                    up_turn(it, 0, 4)
                up_turn(0, FT // 4 * 4, FT % 4)
                pe_.wait_ge(h_done.sem, h_done.upto(l, (f + 1) * FT))
                if f == 0:
                    pe_.wait_ge(mod_done.sem, mod_done.upto(l, ADA_FIRST + FT))
                settled(7)
                with pe_.Fori(0, KT // 2) as it:
                    for b in range(2):
                        pe_.wait_ge(x_done.sem, x_done.upto(l, 16 * f + b - 1 + it * 2))
                        for hf in range(2):
                            panel(l, f"down{f}", it, 2 * b + hf)
                            tile(b, ring[:, 2 * b + hf, :], 0, hid, DOWN_K * hf, DOWN_K, P,
                                 first=hf == 0, last=hf == 1).then_inc(part.sem, 1)

            pe_.wait_ge(start_loaded.sem, 48)
            pe_.wait_ge(csil_done.sem, 1)
            with pe_.Fori(0, DEPTH) as l:
                pe_.wait_ge(x_done.sem, x_done.upto(l, 0))
                settled(7)
                with pe_.Fori(0, ADA_FIRST // R) as it:
                    for s in range(R):
                        panel(l, "ada", it, s)
                        pe_.wait_ge(mod_done.sem, mod_done.upto(l, s - 3 + it * R))
                        modulation(s, s)
                ffn(l, 0)

                sum_squares(l, 1)
                wait_u(l, 1)

                for j in range(11):
                    place = in_place(j)[0]
                    panel(l, "in", 0, place % R, place // R)
                    for c in range(2):
                        g, n = kept(j - 2, c) if j >= 2 else (in_dve if c else in_act, j - 1)
                        pe_.wait_ge(g.sem, g.upto(l, n))
                        if c and 0 < j <= ADA_IN:
                            pe_.wait_ge(mod_done.sem, mod_done.upto(l, ADA_FIRST + FT + j))
                        tile((2 * j + c) % 4, ring[:, place % R, :], c * P, u).then_inc(part.sem, 1)
                    if j < ADA_IN:
                        panel(l, "in", 0, place % R + 1, place // R)
                        pe_.wait_ge(in_dve.sem, in_dve.upto(l, j))
                        modulation(place % R + 1, next_bank(j))

                pe_.wait_ge(qk_sq.sem, qk_sq.upto(l, 1))
                pe_.wait_ge(in_act.sem, in_act.upto(l, in_act.per_layer))
                for i in range(4):
                    m = tile(i, cmat(BLK), 0, sqk, i, 1)
                m.then_inc(qk_sum.sem, 1)
                pe_.wait_ge(pool_in.sem, pool_in.upto(l, 1))
                pe_.wait_ge(qk_ms.sem, qk_ms.upto(l, 1))
                for ft in range(2):
                    m = tile(2 + ft, lp[:, PBD:PBD + 256], ft * P, pd, ft, 1)
                m.then_inc(pool_pe.sem, 1)
                for tt in range(4):
                    for ft in range(2):
                        nc.tensor.transpose(ps[:, tt // 2, (tt % 2) * 256 + ft * P:(tt % 2) * 256 + ft * P + P],
                                            proj[:, P_V + ft, tt * P:tt * P + P], cmat(IDENT))
                for ft in range(2):
                    m = nc.tensor.transpose(ps[0:TS, 2, ft * P:ft * P + P], proj[:, P_V + ft, TP:T],
                                            cmat(IDENT))
                m.then_inc(vt_pe.sem, 1)
                pe_.wait_ge(vt_act.sem, vt_act.upto(l, 1))
                pe_.wait_ge(pool_out.sem, pool_out.upto(l, 1))
                pe_.wait_ge(kn_ready.sem, kn_ready.upto(l, 1))
                pe_.wait_ge(qp_done.sem, qp_done.upto(l, 1))
                for h in range(NH):
                    ft, po = h // 2, HD * (h % 2)
                    if h:
                        pe_.wait_ge(at_act.sem, at_act.upto(l, 3 * h))
                    for kt in range(NTT):
                        b, c0, w = SEG[kt]
                        m = mm(ps[:, b, c0:c0 + w], proj[po:po + HD, P_K + ft, kt * P:kt * P + P],
                               proj[po:po + HD, P_Q + ft, kt * P:TP])
                    m.then_inc(at_pe.sem, 1)
                    for n in range(4 * h, 4 * h + 4):
                        s, hf = n // 2, n % 2
                        pe_.wait_ge(cache_loaded[n % 4].sem, cache_loaded[n % 4].upto(l, 4 * (n // 4 + 1)))
                        for pg in range(4):
                            for f2 in range(2):
                                o = ps[:, 6 + hf, pg * P + f2 * 64:pg * P + f2 * 64 + 64]\
                                    .rearrange("p (h q) -> p h q", h=2)[:, :, s * TD:s * TD + TD]
                                m = mm(o, cache[:, n % 4, pg, f2 * P:f2 * P + P],
                                       qp[:, f2, s, :].rearrange("p (h t) -> p h t", h=2))
                        m.then_inc(cache_used.sem, 1)
                    pe_.wait_ge(at_dve.sem, at_dve.upto(l, 3 * h + 2))
                    for kt in (3, 2, 1, 0):
                        b, c0, w = SEG[kt]
                        o0 = OFF[kt]
                        for k2 in range(NTT - 1, kt, -1):
                            w2 = SEG[k2][2]
                            mm(ps[:, 3 + b, c0 + w - w2:c0 + w], cmat(ONES), sp[:, OFF[k2]:OFF[k2] + w2],
                               start=k2 == NTT - 1, stop=False, skip=True)
                        m = mm(ps[:, 3 + b, c0:c0 + w], cmat(TRI), sp[:, o0:o0 + w], start=kt == NTT - 1,
                               skip=True)
                    m.then_inc(at_pe.sem, 1)
                    pe_.wait_ge(at_act.sem, at_act.upto(l, 3 * h + 2))
                    for kt in (3, 2, 1, 0):
                        w = SEG[kt][2]
                        m = mm(ps[po:po + HD, 0, TP - w:TP], vtok[:, kt, h * HD:h * HD + HD],
                               sa[:, OFF[kt]:OFF[kt] + w], start=kt == 3, stop=kt == 0, skip=True)
                    m.then_inc(at_pe.sem, 1)
                pe_.wait_ge(at_act.sem, at_act.upto(l, 12))
                for h in range(NH):
                    m = mm(ps[0:TS, 1, h * TS:h * TS + TS], proj[:, P_K + h // 2, TP:T],
                           qp[:, h // 2, :, (h % 2) * TD:(h % 2) * TD + TD])
                m.then_inc(de_pe.sem, 1)
                pe_.wait_ge(de_dve.sem, de_dve.upto(l, 2))
                for b in range(2):
                    n = 4 if b == 0 else 3
                    mm(ps[:, 2 + b, :], cmat(TRI), sp[:, b * 512:b * 512 + 512], stop=False, skip=True)
                    mm(ps[:, 2 + b, 0:n * P], cmat(ONES), rd[:, 4 * b:4 * b + n, :], start=False, stop=False,
                       skip=True)
                    mm(ps[:, 2 + b, :], cmat(ONES), across(spn[:, :], 4), start=False, skip=True)
                m = mm(ps[0:TS, 4, 0:P], cst[:, TRI:TRI + TS], spn[:, :])
                m.then_inc(de_pe.sem, 1)
                pe_.wait_ge(de_act.sem, de_act.upto(l, 2))
                for f2 in range(2):
                    mm(ps[:, 5, f2 * 64:f2 * 64 + 64], vtok[0:TS, 4, f2 * P:f2 * P + P],
                       tn[0:TS, f2 * 64:f2 * 64 + 64], start=f2 == 0, stop=False, skip=True)
                for n in range(16):
                    s, hf = n // 2, n % 2
                    pe_.wait_ge(cache_loaded[n % 4].sem, cache_loaded[n % 4].upto(l, 16 + 4 * (n // 4 + 1)))
                    for pg in range(4):
                        for f2 in range(2):
                            def at8(v):
                                return v.rearrange("p (h q) -> p h q", h=2)[:, :, s * TD:s * TD + TD]
                            m = mm(at8(ps[:, 5, f2 * 64:f2 * 64 + 64]), cache[:, n % 4, pg, f2 * P:f2 * P + P],
                                   at8(sa[:, (4 * hf + pg) * P + f2 * 64:(4 * hf + pg) * P + f2 * 64 + 64]),
                                   start=False, stop=hf == 1 and pg == 3, skip=True)
                    m.then_inc(cache_used.sem, 1)

                pe_.wait_ge(rp_act.sem, rp_act.upto(l, 2))
                pe_.wait_ge(de_dve.sem, de_dve.upto(l, 4))
                for ft in range(2):
                    for hf in range(2):
                        c = slice(hf * HALF, hf * HALF + HALF)
                        mm(ps[:, 2 * ft + hf, 0:HALF], lp[0:64, W2A2 + ft * P:W2A2 + ft * P + P], xt2[0:64, 0, c])
                        m = mm(ps[:, 4 + 2 * ft + hf, 0:HALF], lp[64:128, W2A2 + ft * P:W2A2 + ft * P + P],
                           xt2[64:128, 0, c])
                m.then_inc(rp_pe.sem, 1)
                pe_.wait_ge(rp_act.sem, rp_act.upto(l, 4))
                pe_.wait_ge(rp_dve.sem, rp_dve.upto(l, 2))
                for ft in range(2):
                    tile(ft, lp[:, G2:G2 + 256], ft * P, xt2, 1, 1)
                for ft in range(2):
                    m = tile(2 + ft, cmat(BLK), 0, bon, ft, 1)
                m.then_inc(rp_pe.sem, 1)
                pe_.wait_ge(rp_dve.sem, rp_dve.upto(l, 4))
                for ft in range(2):
                    m = tile(2 + ft, cmat(BLK), 0, bon, ft, 1)
                m.then_inc(rp_pe.sem, 1)

                def heads(b, lhsT, rhs, n=P, rows=P):
                    for h in range(NH):
                        m = mm(ps[0:rows, b, h * n:h * n + n], lhsT(h), rhs(h))
                    return m

                def ft_of(v, n=P):
                    return lambda h: v[:, h // 2, 0:n]

                def hd_of(v, n=P, rows=P):
                    return lambda h: v[0:rows, h, 0:n]

                settled(0)
                with pe_.Fori(0, NTT) as tt:
                    def tile_dve(n):
                        return rw_dve.upto(l, n + tt * RW_DVE)

                    def tile_act(n):
                        return rw_act.upto(l, n + tt * RW_ACT)

                    pe_.wait_ge(rw_dve.sem, tile_dve(1))
                    heads(0, ft_of(Bt), hd_of(AtP))
                    heads(1, ft_of(At), hd_of(BtP)).then_inc(rw_pe.sem, 1)
                    heads(2, ft_of(Kt_), hd_of(AtP))
                    heads(3, ft_of(Bt), hd_of(RtP))
                    heads(4, ft_of(Kt_), hd_of(RtP))
                    for ft in range(2):
                        nc.tensor.transpose(ps[:, 5, ft * P:ft * P + P], Bp[:, ft, :], cmat(IDENT))
                        nc.tensor.transpose(ps[:, 5, 256 + ft * P:256 + ft * P + P], Kp[:, ft, :], cmat(IDENT))
                    for ft in range(2):
                        m = nc.tensor.transpose(ps[:, 6, ft * P:ft * P + P], stmp[:, ft, :], cmat(IDENT))
                    m.then_inc(rw_pe.sem, 1)
                    pe_.wait_ge(rw_dve.sem, tile_dve(2))
                    heads(0, hd_of(MB), hd_of(MA))
                    heads(1, hd_of(MA), hd_of(MB)).then_inc(rw_pe.sem, 1)
                    pe_.wait_ge(rw_act.sem, tile_act(2))
                    pe_.wait_ge(rw_dve.sem, tile_dve(3))
                    heads(0, hd_of(MD), hd_of(ME))
                    heads(1, hd_of(MD), hd_of(MC))
                    heads(5, hd_of(MC), hd_of(MD)).then_inc(rw_pe.sem, 1)
                    pe_.wait_ge(rw_act.sem, tile_act(3))
                    pe_.wait_ge(rw_dve.sem, tile_dve(4))
                    heads(0, hd_of(MB), hd_of(MF))
                    heads(1, hd_of(MA), hd_of(MB)).then_inc(rw_pe.sem, 1)
                    pe_.wait_ge(rw_act.sem, tile_act(4))
                    pe_.wait_ge(rw_dve.sem, tile_dve(5))
                    heads(0, hd_of(MC), hd_of(ME)).then_inc(rw_pe.sem, 1)
                    pe_.wait_ge(rw_dve.sem, tile_dve(6))
                    for q, (ET, xa) in enumerate(((ET32, MF), (E64, ME))):
                        if q:
                            pe_.wait_ge(rw_dve.sem, tile_dve(7))
                        heads(0, hd_of(ET), hd_of(xa))
                        for h in range(NH):
                            m = nc.tensor.transpose(ps[:, 1, h * P:h * P + P], xa[:, h, :], cmat(IDENT))
                        m.then_inc(rw_pe.sem, 1)
                        pe_.wait_ge(rw_act.sem, tile_act(5 + q))
                        heads(2 if q else 5, hd_of(MB), hd_of(MA)).then_inc(rw_pe.sem, 1)
                    for c in range(2):
                        q0, rows = CH * c, slice(CH * c, CH * c + CH)
                        pe_.wait_ge(rw_dve.sem, tile_dve(8 + 2 * c))
                        for ft in range(2):
                            for h in (2 * ft, 2 * ft + 1):
                                mm(ps[rows, 0, h * HD:h * HD + HD], LakT[:, h, rows],
                                   vt[:, h * HD:h * HD + HD], start=h % 2 == 0, stop=False, skip=True)
                            m = mm(ps[rows, 0, ft * P:ft * P + P], At[:, ft, rows], sbd[:, ft, :],
                                   start=False, skip=True)
                        m.then_inc(rw_pe.sem, 1)
                        for ft in range(2):
                            mm(ps[:, 7, ft * P + q0:ft * P + q0 + CH], sbd[:, ft, :], Rt[:, ft, rows],
                               start=c == 0 and ft == 0, stop=False, skip=True)
                        pe_.wait_ge(rw_act.sem, tile_act(7 + c))
                        for h in range(NH):
                            m = mm(ps[rows, 1, h * HD:h * HD + HD], MF[:, h, rows],
                                   r0[:, h * HD:h * HD + HD])
                        m.then_inc(rw_pe.sem, 1)
                        pe_.wait_ge(rw_dve.sem, tile_dve(9 + 2 * c))
                        for ft in range(2):
                            c2 = slice(ft * P, ft * P + P)
                            mm(ps[:, 3, c2], bptok[rows, c2], sat[rows, c2], stop=False)
                            m = mm(ps[:, 3, c2], kptok[rows, c2], vt[rows, c2], start=False)
                        m.then_inc(rw_pe.sem, 1)
                    for h in range(NH):
                        ft, po = h // 2, HD * (h % 2)
                        o = ps[po:po + HD, 7, ft * P:ft * P + P]
                        c2 = slice(h * HD, h * HD + HD)
                        mm(o, sat[:, c2], MrbT[:, h, :], start=False, stop=False, skip=True)
                        m = mm(o, vt[:, c2], MrkT[:, h, :], start=False, skip=True)
                    m.then_inc(rw_pe.sem, 1)

                pe_.wait_ge(rs_dve.sem, rs_dve.upto(l, 1))
                pe_.wait_ge(rw_dve.sem, rw_dve.upto(l, rw_dve.per_layer))
                heads(0, ft_of(Bt, TS), hd_of(AtP, TS), TS, TS)
                heads(1, ft_of(At, TS), hd_of(BtP, TS), TS, TS)
                heads(2, ft_of(Kt_, TS), hd_of(AtP, TS), TS, TS)
                heads(3, ft_of(Bt, TS), hd_of(RtP, TS), TS, TS)
                heads(4, ft_of(Kt_, TS), hd_of(RtP, TS), TS, TS)
                for ft in range(2):
                    nc.tensor.transpose(ps[0:TS, 5, ft * P:ft * P + P], Bp[:, ft, 0:TS], cmat(IDENT))
                    nc.tensor.transpose(ps[0:TS, 5, 256 + ft * P:256 + ft * P + P], Kp[:, ft, 0:TS],
                                        cmat(IDENT))
                for ft in range(2):
                    m = nc.tensor.transpose(ps[0:TS, 6, ft * P:ft * P + P], v_[:, ft, TP:T], cmat(IDENT))
                m.then_inc(rs_pe.sem, 1)
                pe_.wait_ge(rs_dve.sem, rs_dve.upto(l, 2))
                pe_.wait_ge(rs_act.sem, rs_act.upto(l, 1))
                settled(6)
                m = heads(0, hd_of(MA, TS, TS), hd_of(MB, TS, TS), TS, TS)

                def by_seq(b, rhs, first):
                    for h in range(NH):
                        ft, po = h // 2, HD * (h % 2)
                        for s in range(NSEQ):
                            m = mm(ps[po:po + HD, b, ft * TS + s * TD:ft * TS + s * TD + TD],
                                   lp[:, SWKV + (ft * NSEQ + s) * HD:SWKV + (ft * NSEQ + s) * HD + HD],
                                   rhs[:, h, s * TD:s * TD + TD], start=first and h < 2 and s == 0,
                                   stop=False, skip=True)
                    return m

                by_seq(1, AtP, True)
                for h in range(NH):
                    ft, po = h // 2, HD * (h % 2)
                    m = mm(ps[po:po + HD, 1, ft * TS:ft * TS + TS], vt[0:TS, h * HD:h * HD + HD],
                           LakT[0:TS, h, 0:TS], start=False, skip=True)
                m.then_inc(rs_pe.sem, 1)
                pe_.wait_ge(rs_dve.sem, rs_dve.upto(l, 3))
                settled(6)
                heads(0, hd_of(MD, TS, TS), hd_of(ME, TS, TS), TS, TS)
                for ft in range(2):
                    m = nc.tensor.transpose(ps[0:TS, 2, ft * P:ft * P + P], stmp[:, ft, 0:TS], cmat(IDENT))
                m.then_inc(rs_pe.sem, 1)
                pe_.wait_ge(rs_dve.sem, rs_dve.upto(l, 4))
                pe_.wait_ge(rs_act.sem, rs_act.upto(l, 2))
                settled(6)
                for h in range(NH):
                    m = mm(ps[0:TS, 1, h * HD:h * HD + HD], MF[0:TS, h, 0:TS], r0[0:TS, h * HD:h * HD + HD])
                m.then_inc(rs_pe.sem, 1)
                pe_.wait_ge(rs_act.sem, rs_act.upto(l, 3))
                by_seq(7, RtP, True)
                for h in range(NH):
                    ft, po = h // 2, HD * (h % 2)
                    o, c2 = ps[po:po + HD, 7, ft * TS:ft * TS + TS], slice(h * HD, h * HD + HD)
                    mm(o, sat[0:TS, c2], MrbT[0:TS, h, 0:TS], start=False, stop=False, skip=True)
                    m = mm(o, vt[0:TS, c2], MrkT[0:TS, h, 0:TS], start=False, skip=True)
                m.then_inc(rs_pe.sem, 1)
                for q in range(2):
                    pe_.wait_ge(rs_dve.sem, rs_dve.upto(l, 5 + q))
                    for h in range(NH):
                        ft, po = h // 2, HD * (h % 2)
                        lhs = (bptok, kptok)[q][0:TS, h * HD:h * HD + HD]
                        m = mm(ps[po:po + HD, 3 + ft, :], lhs, sam[0:TS, :, h * HD:h * HD + HD],
                               start=q == 0, stop=q == 1, skip=True)
                    m.then_inc(rs_pe.sem, 1)
                for n in range(2):
                    pe_.wait_ge(gn_dve.sem, gn_dve.upto(l, n + 1))
                    for ft in range(2):
                        m = tile(ft, cmat(BLK), 0, yb if n == 0 else e2, ft, 1)
                    m.then_inc(gn_pe.sem, 1)
                pe_.wait_ge(mix_done.sem, mix_done.upto(l, 1))
                settled(7)
                with pe_.Fori(0, 4) as g:
                    for i in range(4):
                        panel(l, "gate", g, i)
                        for c in range(2):
                            q = 2 * i + c
                            b = 2 * (q % 2)
                            pe_.wait_ge(merge_done.sem, merge_done.upto(l, q - 1 + g * 8))
                            tile(b, ring[:, i, :], c * P, u).then_inc(part.sem, 1)
                            if q == 0:
                                pe_.wait_ge(branch_loaded.sem, branch_loaded.upto(l, 1 + g))
                            tile(b + 1, wbr[:, i * 512:i * 512 + 512], c * P, y, 2 * i, 2)\
                                .then_inc(part.sem, 1)
                pe_.wait_ge(merge_done.sem, merge_done.upto(l, 32))
                for s in range(4):
                    panel(l, "out", 0, s)
                    for c in range(2):
                        pe_.wait_ge(x_done.sem, x_done.upto(l, 8 + 2 * s + c - 1))
                        tile(c, ring[:, s, :], c * P, merged).then_inc(part.sem, 1)
                ffn(l, 1)

        @block.scalar
        def _(act):
            own = [0]

            def link(layer, ins):
                own[0] += 1
                ins.then_inc(act_own.sem, 1)
                act.wait_ge(act_own.sem, act_own.upto(layer, own[0]))

            def f(out, in_, func, **kw):
                return nc.scalar.activation(out, in_, func, **kw)

            def norm(l, n):
                for k in range(KT):
                    act.wait_ge(x_done.sem, x_done.upto(l, 8 * n - 7 + k if n else 0))
                    if k >= 2:
                        act.wait_ge(sum_done.sem, sum_done.upto(l, 8 * n + k - 1))
                    f(sq[:, k % 2, :], x[:, k, :], ACT.Square).then_inc(sq_done.sem, 1)
                act.wait_ge(sum_done.sem, sum_done.upto(l, 8 * n + 8))
                link(l, f(halves(rs[:, :]), pair(3), ACT.Ln, scale=1.0 / D_MODEL, bias=cst[:, BIAS:BIAS + 1]))
                f(rs[:, :], rs[:, :], ACT.Exp, scale=-0.5).then_inc(rt_done.sem, 1)
                for k in range(KT):
                    act.wait_ge(un_done.sem, un_done.upto(l, 8 * n + k + 1))
                    f(u[:, k, 0:TP], u[:, k, 0:TP], ACT.Identity, scale=mod_a[:, 8 * n + k, 0:1],
                      bias=mod[:, 24 * n + k, 0:1]).then_inc(up_done.sem, 1)

            def ffn(l, n):
                norm(l, 2 * n)

                def units(it, first, k):
                    per = 3 if n == 0 else 2
                    for j in range(k):
                        act.wait_ge(part.sem, part.upto(l, PART0[f"up{n}"] + per * (first + j) + 1
                                                        + it * (4 * per)))
                        f(halves(gt[:, j % 2, :]), pair(2 * (j % 2)), ACT.Silu).then_inc(silu_done.sem, 1)

                with act.Fori(0, FT // 4) as it:
                    units(it, 0, 4)
                units(0, FT // 4 * 4, FT % 4)

            act.wait_ge(start_loaded.sem, 48)
            f(csil[:, :, :], csil[:, :, :], ACT.Silu).then_inc(csil_done.sem, 1)
            with act.Fori(0, DEPTH) as l:
                own[0] = 0
                ffn(l, 0)
                norm(l, 1)
                for j in range(11):
                    for c in range(1 if j < NBOTH else 2):
                        act.wait_ge(part.sem, part.upto(l, PART0["in"] + in_place(j)[1] + c + 1))
                        f(halves(proj[:, 2 * IN_ORDER[j] + c, :]), pair((2 * j + c) % 4), ACT.Copy)\
                            .then_inc(in_act.sem, 1)
                    if j == 3:
                        act.wait_ge(in_act.sem, in_act.upto(l, 2))
                        act.wait_ge(in_dve.sem, in_dve.upto(l, 2))
                        f(sqk[:, :, :], proj[:, P_Q:P_Q + 4, :], ACT.Square).then_inc(qk_sq.sem, 1)
                act.wait_ge(qk_sum.sem, qk_sum.upto(l, 1))
                for i in range(4):
                    a, b = (1.0, BIAS + 1) if i < 2 else (1.0 / HD, BIAS)
                    m = f(halves(sqk[:, i, :]), pair(i), ACT.Ln, scale=a, bias=cst[:, b:b + 1])
                m.then_inc(qk_ms.sem, 1)
                act.wait_ge(qk_ms.sem, qk_ms.upto(l, 1))
                f(sqk[:, :, :], sqk[:, :, :], ACT.Exp, scale=-0.5).then_inc(qk_rt.sem, 1)
                act.wait_ge(pool_pe.sem, pool_pe.upto(l, 1))
                for ft in range(2):
                    m = f(halves(y[:, 4 + ft, :]), pair(2 + ft), ACT.Identity, scale=col(PSC + ft))
                m.then_inc(pool_out.sem, 1)
                act.wait_ge(so_ready.sem, so_ready.upto(l, 3))
                act.dma_start(o_conv[l], so_conv).then_inc(stored.sem, 16)
                act.dma_start(o_pool[l], so_pool).then_inc(stored.sem, 16)
                act.dma_start(o_shift[l], so_shift).then_inc(stored.sem, 16)
                act.wait_ge(vt_pe.sem, vt_pe.upto(l, 1))
                f(vtok[:, 0:4, :], ps[:, 0:2, :], ACT.Copy)
                f(vtok[0:TS, 4, :], ps[0:TS, 2, 0:256], ACT.Copy).then_inc(vt_act.sem, 1)
                act.wait_ge(kn_ready.sem, kn_ready.upto(l, 1))
                act.dma_start(o_k[l], proj[:, P_K:P_K + 2, :]).then_inc(kv_stored.sem, 16)
                act.dma_start(o_v[l], proj[:, P_V:P_V + 2, :]).then_inc(kv_stored.sem, 16)

                def log1p_exp(a, b, ready):
                    link(l, f(b, a, ACT.Abs))
                    link(l, f(b, b, ACT.Exp, scale=-1.0))
                    return f(b, b, ACT.Ln, bias=1.0)

                for h in range(NH):
                    act.wait_ge(at_dve.sem, at_dve.upto(l, 3 * h + 1))
                    log1p_exp(zb[:, :], sa[:, :], None).then_inc(at_act.sem, 1)
                    act.wait_ge(at_dve.sem, at_dve.upto(l, 3 * h + 3))
                    f(sa[:, :], sa[:, :], ACT.Exp).then_inc(at_act.sem, 1)
                    act.wait_ge(at_pe.sem, at_pe.upto(l, 3 * h + 3))
                    po = HD * (h % 2)
                    f(y[po:po + HD, 6 + h // 2, 0:TP], ps[po:po + HD, 0, :], ACT.Copy).then_inc(at_act.sem, 1)
                act.wait_ge(de_dve.sem, de_dve.upto(l, 1))
                log1p_exp(zb[:, 0:1024], sa[:, 0:1024], None)
                log1p_exp(zbn[0:TS, :], tn[0:TS, :], None).then_inc(de_act.sem, 1)
                act.wait_ge(de_dve.sem, de_dve.upto(l, 3))
                f(sa[:, 0:1024], sa[:, 0:1024], ACT.Exp)
                f(tn[0:TS, :], tn[0:TS, :], ACT.Exp).then_inc(de_act.sem, 1)

                act.wait_ge(rp_dve.sem, rp_dve.upto(l, 1))
                f(xt2[0:64, 0, :], xt2[0:64, 0, :], ACT.Tanh).then_inc(rp_act.sem, 1)
                f(xt2[:, 1, :], xt2[:, 1, :], ACT.Sigmoid).then_inc(rp_act.sem, 1)
                act.wait_ge(rp_pe.sem, rp_pe.upto(l, 1))
                for ft in range(2):
                    m = f(halves(e1[:, ft, :]), pair(ft), ACT.Sigmoid, bias=col(W0 + ft))
                m.then_inc(rp_act.sem, 1)
                for ft in range(2):
                    m = f(halves(bv[:, ft, :]), pair(2 + ft), ACT.Sigmoid, bias=col(A0 + ft))
                m.then_inc(rp_act.sem, 1)
                act.wait_ge(rp_pe.sem, rp_pe.upto(l, 2))
                for ft in range(2):
                    m = f(halves(gg[:, ft, :]), pair(ft), ACT.Copy)
                m.then_inc(rp_act.sem, 1)
                act.wait_ge(rp_dve.sem, rp_dve.upto(l, 3))
                link(l, f(xt2[:, :, :], xt2[:, :, :], ACT.Ln))
                f(xt2[:, :, :], xt2[:, :, :], ACT.Exp, scale=-0.5).then_inc(rp_act.sem, 1)
                act.wait_ge(rp_dve.sem, rp_dve.upto(l, 5))
                f(e2, e2, ACT.Exp)
                f(e1, e3, ACT.Exp)
                f(e3, e3, ACT.Exp, scale=-1.0).then_inc(rp_act.sem, 1)
                with act.Fori(0, NTT) as tt:
                    def tile_pe(n):
                        return rw_pe.upto(l, n + tt * RW_PE)

                    def flat(v):
                        return v.rearrange("p h n -> p (h n)")

                    act.wait_ge(rw_pe.sem, tile_pe(2))
                    f(turned, ps[:, 5, :], ACT.Copy)
                    f(vt, ps[:, 6, 0:256], ACT.Copy).then_inc(rw_act.sem, 1)
                    act.wait_ge(rw_pe.sem, tile_pe(3))
                    f(flat(MD), ps[:, 1, :], ACT.Copy).then_inc(rw_act.sem, 1)
                    act.wait_ge(rw_pe.sem, tile_pe(4))
                    f(flat(MA), ps[:, 1, :], ACT.Copy)
                    f(flat(MB), ps[:, 5, :], ACT.Copy).then_inc(rw_act.sem, 1)
                    act.wait_ge(rw_pe.sem, tile_pe(5))
                    f(flat(MC), ps[:, 1, :], ACT.Copy).then_inc(rw_act.sem, 1)
                    for q in range(2):
                        act.wait_ge(rw_pe.sem, tile_pe(7 + 2 * q))
                        f(flat(MA), ps[:, 0, :], ACT.Copy)
                        f(flat(MB), ps[:, 1, :], ACT.Copy).then_inc(rw_act.sem, 1)
                    for c in range(2):
                        rows = slice(CH * c, CH * c + CH)
                        act.wait_ge(rw_pe.sem, tile_pe(11 + 3 * c))
                        f(r0[rows, :], ps[rows, 0, 0:256], ACT.Copy).then_inc(rw_act.sem, 1)
                act.wait_ge(rs_pe.sem, rs_pe.upto(l, 1))
                f(turned[0:TS, :], ps[0:TS, 5, :], ACT.Copy)
                f(vt[0:TS, :], ps[0:TS, 6, 0:256], ACT.Copy).then_inc(rs_act.sem, 1)
                act.wait_ge(rs_pe.sem, rs_pe.upto(l, 3))
                f(r0[0:TS, :], ps[0:TS, 2, 0:256], ACT.Copy).then_inc(rs_act.sem, 1)
                act.wait_ge(rs_pe.sem, rs_pe.upto(l, 4))
                f(sat[0:TS, :], ps[0:TS, 1, 0:256], ACT.Copy).then_inc(rs_act.sem, 1)
                act.wait_ge(gn_pe.sem, gn_pe.upto(l, 2))
                for ft in range(2):
                    m = f(halves(e2[:, ft, :]), pair(ft), ACT.Ln, scale=1.0 / HD, bias=cst[:, BIAS + 2:BIAS + 3])
                link(l, m)
                f(e2, e2, ACT.Exp, scale=-0.5).then_inc(gn_act.sem, 1)
                act.wait_ge(wkv_ready.sem, wkv_ready.upto(l, 1))
                act.dma_start(o_wkv[l, :, :, 1:9, :], lp[:, SWKV:SWKV + 2 * NSEQ * HD].rearrange(
                    "p (f s i) -> p f s i", f=2, s=NSEQ)).then_inc(wkv_stored.sem, 16)
                for q in range(2):
                    rows = slice(HD * q, HD * q + HD)
                    act.dma_start(o_wkv[l, rows, :, 0, :], sbd[rows, :, rows])\
                        .then_inc(wkv_stored.sem, 16)
                with act.Fori(0, 4) as g:
                    for q in range(8):
                        act.wait_ge(part.sem, part.upto(l, PART0["gate"] + 2 * q + 1 + g * 16))
                        f(halves(gt[:, q % 2, :]), pair(2 * (q % 2)), ACT.Sigmoid).then_inc(gate_done.sem, 1)
                ffn(l, 1)
                assert own[0] == ACT_LINKS, ("ACT_LINKS", own[0])

        @block.vector
        def _(dve):
            V = nc.vector
            own = [0]

            def link(layer, ins):
                own[0] = own[0] + 1
                ins.then_inc(vec.sem, 1)
                dve.wait_ge(vec.sem, vec.upto(layer, own[0]))

            def tt_(out, a, b, op):
                return V.tensor_tensor(out, a, b, op)

            def stt(out, a, s, b, op0, op1):
                return V.scalar_tensor_tensor(out=out, in0=a, scalar=s, in1=b, op0=op0, op1=op1)

            def ts(out, a, s1, op0, s2=None, op1=ALU.bypass):
                return V.tensor_scalar(out, a, s1, s2, op0, op1)

            MUL, ADD, SUB, MAX = ALU.mult, ALU.add, ALU.subtract, ALU.max

            def norm(l, n):
                dve.wait_ge(rt_done.sem, rt_done.upto(l, n + 1))
                for k in range(KT):
                    tt_(u[:, k, :], x[:, k, :], rs[:, :], MUL).then_inc(un_done.sem, 1)
                dve.wait_ge(un_done.sem, un_done.upto(l, 8 * n + 8))
                us = u[:, :, TP:T].rearrange("p k (s t) -> p k s t", s=NSEQ)

                def by_seq(v):
                    return v.unsqueeze(3).to_broadcast([P, KT, NSEQ, TD])

                link(l, tt_(us, us, by_seq(mod_a[:, 8 * n:8 * n + 8, 1:9]), MUL))
                tt_(us, us, by_seq(mod[:, 24 * n:24 * n + 8, 1:9]), ADD).then_inc(us_done.sem, 1)

            def residual(l, m, b, gate):
                g = gate + m
                stt(x[:, m, 0:HALF], ps[:, 2 * b, 0:HALF], mod[:, g, 0:1], x[:, m, 0:HALF], MUL, ADD)
                stt(x[:, m, HALF:TP], ps[:, 2 * b + 1, 0:TP - HALF], mod[:, g, 0:1], x[:, m, HALF:TP], MUL, ADD)
                room = ptmp[:, m * TS:m * TS + TS]
                link(l, tt_(seqs(room), seqs(ps[:, 2 * b + 1, TP - HALF:HALF]),
                            over(mod[:, g, 1:9], TD), MUL))
                tt_(x[:, m, TP:T], x[:, m, TP:T], room, ADD).then_inc(x_done.sem, 1)

            def keep_modulation(l, p, n, bank, it=0, step=0):
                dve.wait_ge(part.sem, part.upto(l, p + it * (3 * step if p > PART0["up0"] else step)))
                t0 = bass.ds(it * (2 * step) + 2 * n, 2)
                tt_(mod[:, t0, :], ps[:, bank, MODC:MODC + 18].rearrange("p (a n) -> p a n", a=2),
                    over(lp[:, bass.ds(it * (2 * step) + (ADAB + 2 * n), 2)], 9), ADD).then_inc(mod_done.sem, 1)

            def modulation_factors(l, panels, norms, gates):
                dve.wait_ge(mod_done.sem, mod_done.upto(l, panels))
                for n in norms:
                    m = stt(mod_a[:, 8 * n:8 * n + 8, :], mod[:, 24 * n + 8:24 * n + 16, :], 1.0,
                            over(lp[:, NG + 8 * n:NG + 8 * n + 8], 9), ADD, MUL)
                for g in gates:
                    m = ts(mod[:, g:g + 8, :], mod[:, g:g + 8, :], 0.5, MUL)
                link(l, m)

            def ffn(l, n):
                norm(l, 2 * n)

                per = 3 if n == 0 else 2

                def units(it, first, k):
                    for j in range(k):
                        q = first + j
                        dve.wait_ge(part.sem, part.upto(l, PART0[f"up{n}"] + per * q + 2 + it * (4 * per)))
                        dve.wait_ge(silu_done.sem, silu_done.upto(l, n * FT + q + 1 + it * 4))
                        tt_(halves(hid[:, q + it * 4, :]), halves(gt[:, j % 2, :]), pair(2 * (j % 2) + 1), MUL)\
                            .then_inc(h_done.sem, 1)
                        if n == 0:
                            keep_modulation(l, PART0["up0"] + 3 * q + 3, ADA_FIRST + q, next_bank(q), it, 4)

                settled()
                with dve.Fori(0, FT // 4) as it:
                    units(it, 0, 4)
                units(0, FT // 4 * 4, FT % 4)
                if n == 0:
                    modulation_factors(l, ADA_FIRST + FT, (1,), (16,))
                for m in range(KT):
                    dve.wait_ge(part.sem, part.upto(l, PART0[f"down{n}"] + 2 * m + 2))
                    residual(l, m, m % 2, 16 if n == 0 else 64)

            def conv(l):
                b_, c_, xv = proj[:, 0:2, :], proj[:, 2:4, :], proj[:, 4:6, :]

                def smp(v):
                    return v[:, :, TP:T].rearrange("p f (s t) -> p f s t", s=NSEQ)

                V.memset(zc[:, :, 0:2], 0.0)
                V.tensor_copy(zs[:, :, :, 0:2], lp[:, SCONV:SCONV + 32].rearrange("p (f s t) -> p f s t",
                                                                                   f=2, s=NSEQ))
                tt_(zc[:, :, 2:TP + 2], c_[:, :, 0:TP], xv[:, :, 0:TP], MUL)
                link(l, tt_(zs[:, :, :, 2:6], smp(c_), smp(xv), MUL))
                V.tensor_copy(so_conv[:, :, 0:2], zc[:, :, TP:TP + 2])
                V.tensor_copy(so_conv[:, :, 2:18].rearrange("p f (s t) -> p f s t", s=NSEQ),
                              zs[:, :, :, 4:6]).then_inc(so_ready.sem, 1)
                for tap in range(3):
                    for ft in range(2):
                        w = col(CW + 2 * tap + ft)
                        yp, ys = y[:, ft, 0:TP], seqs(y[:, ft, TP:T])
                        zp_, zs_ = zc[:, ft, tap:tap + TP], zs[:, ft, :, tap:tap + TD]
                        if tap == 0:
                            ts(yp, zp_, w, MUL)
                            m = ts(ys, zs_, w, MUL)
                        else:
                            stt(yp, zp_, w, yp, MUL, ADD)
                            m = stt(ys, zs_, w, ys, MUL, ADD)
                    link(l, m)
                tt_(y[:, 0:2, :], y[:, 0:2, :], b_, MUL)

            def pooling(l):
                z = proj[:, P_POOL:P_POOL + 2, :]
                V.memset(pe[:, :, 0:CTX], 0.0)
                V.tensor_copy(pe[:, :, CTX:], z[:, :, 0:TP])
                V.tensor_copy(pes[:, :, :, 0:CTX], lp[:, SPOOL:SPOOL + 2 * NSEQ * CTX].rearrange(
                    "p (f s t) -> p f s t", f=2, s=NSEQ))
                link(l, V.tensor_copy(pes[:, :, :, CTX:], z[:, :, TP:T].rearrange("p f (s t) -> p f s t",
                                                                                  s=NSEQ)))
                V.tensor_copy(so_pool[:, :, 0:CTX], pe[:, :, TP:TP + CTX])
                V.tensor_copy(so_pool[:, :, CTX:].rearrange("p f (s t) -> p f s t", s=NSEQ),
                              pes[:, :, :, TD:TD + CTX]).then_inc(so_ready.sem, 1)
                s2, s4 = y[:, 2:4, :], y[:, 6:8, :]
                s8, s16 = proj[:, 2, :], proj[:, 3, :]
                tt_(s2[:, :, 0:526], pe[:, :, 0:526], pe[:, :, 1:527], ADD)
                link(l, tt_(s2s[:, :, :, :], pes[:, :, :, 0:18], pes[:, :, :, 1:19], ADD))
                tt_(s4[:, :, 0:524], s2[:, :, 0:524], s2[:, :, 2:526], ADD)
                link(l, tt_(s4s[:, :, :, :], s2s[:, :, :, 0:16], s2s[:, :, :, 2:18], ADD))
                tt_(s8[:, 0:520], s4[:, 1, 0:520], s4[:, 1, 4:524], ADD)
                link(l, tt_(s8s[:, :, :, :], s4s[:, :, :, 0:12], s4s[:, :, :, 4:16], ADD))
                tt_(s16[:, 0:512], s8[:, 0:512], s8[:, 8:520], ADD)
                link(l, tt_(s16s[:, :, :, :], s8s[:, :, :, 0:4], s8s[:, :, :, 8:12], ADD))
                groups = ((0, 0, s2[:, 0, 14:526], s2s[:, 0, :, 14:18], 2), (0, 64, s4[:, 0, 12:524],
                          s4s[:, 0, :, 12:16], 4), (1, 0, s8[:, 8:520], s8s[:, 1, :, 8:12], 8),
                          (1, 64, s16[:, 0:512], s16s[:, 1, :, 0:4], 16))
                for ft, po, sp_, ss_, w in groups:
                    r = slice(po, po + 64)
                    tt_(fix[r, ft, :], sp_[r, 0:16], cst[r, INVC + 16 * ft:INVC + 16 * ft + 16], MUL)
                    stt(pd[r, ft, 16:TP], sp_[r, 16:TP], 1.0 / w, pe[r, ft, CTX + 16:CTX + TP], MUL, SUB)
                    m = stt(seqs(pd[:, ft, TP:T])[r], ss_[r], 1.0 / w, pes[r, ft, :, CTX:CTX + TD], MUL, SUB)
                link(l, m)
                tt_(pd[:, :, 0:16], fix[:, :, :], pe[:, :, CTX:CTX + 16], SUB).then_inc(pool_in.sem, 1)

            def qk_norm(l):
                dve.wait_ge(qk_rt.sem, qk_rt.upto(l, 1))
                k, q = proj[:, P_K:P_K + 2, :], proj[:, P_Q:P_Q + 2, :]
                stt(k, k, col(KN), sqk[:, 2:4, :], MUL, MUL).then_inc(kn_ready.sem, 1)
                link(l, stt(q, q, col(QN), sqk[:, 0:2, :], MUL, MUL))
                V.memset(spn[:, :], 0.0)
                link(l, V.memset(qp[:, :, :, :], 0.0))
                for r, c in ((slice(0, 64), 0), (slice(64, 128), TD)):
                    m = V.tensor_copy(qp[r, :, :, c:c + TD],
                                      q[r, :, TP:T].rearrange("p f (s t) -> p f s t", s=NSEQ))
                m.then_inc(qp_done.sem, 1)

            def bank_run(b):
                return ps[:, b:b + 3, :].rearrange("p b n -> p (b n)")[:, 0:NZ]

            def attention(l):
                for h in range(NH):
                    dve.wait_ge(at_pe.sem, at_pe.upto(l, 3 * h + 1))
                    ts(zb[:, :], bank_run(0), col(SBB + h), ADD).then_inc(at_dve.sem, 1)
                    dve.wait_ge(at_act.sem, at_act.upto(l, 3 * h + 1))
                    link(l, stt(sp[:, :], zb[:, :], 0.0, sa[:, :], MAX, ADD))
                    for kt in range(NTT):
                        d = sp[:, OFF[kt]:OFF[kt] + P]
                        m = tt_(d, d, cst[:, CAUS:CAUS + P], MUL)
                    m.then_inc(at_dve.sem, 1)
                    dve.wait_ge(at_pe.sem, at_pe.upto(l, 3 * h + 2))
                    link(l, tt_(sa[:, :], zb[:, :], bank_run(3), SUB))
                    for kt in range(NTT):
                        d = sa[:, OFF[kt]:OFF[kt] + P]
                        m = tt_(d, d, cst[:, CNEG:CNEG + P], ADD)
                    m.then_inc(at_dve.sem, 1)

            def sample_attention(l):
                dve.wait_ge(de_pe.sem, de_pe.upto(l, 1))
                dve.wait_ge(cache_used.sem, cache_used.upto(l, 16))
                bias = lp[:, SBB:SBB + NH]
                for b in range(2):
                    for pg in range(4):
                        c = slice((4 * b + pg) * P, (4 * b + pg) * P + P)
                        tt_(zb[:, c].rearrange("p (h q) -> p h q", h=NH),
                            ps[:, 6 + b, pg * P:pg * P + P].rearrange("p (h q) -> p h q", h=NH),
                            over(bias, TS), ADD)
                tt_(zbn[0:TS, :].rearrange("p (h q) -> p h q", h=NH),
                    ps[0:TS, 1, 0:P].rearrange("p (h q) -> p h q", h=NH),
                    over(bias[0:TS], TS), ADD).then_inc(de_dve.sem, 1)
                dve.wait_ge(de_act.sem, de_act.upto(l, 1))
                stt(sp[:, 0:1024], zb[:, 0:1024], 0.0, sa[:, 0:1024], MAX, ADD)
                link(l, stt(spn[0:TS, :], zbn[0:TS, :], 0.0, tn[0:TS, :], MAX, ADD))

                def new(v):
                    return v[0:TS, :].rearrange("p (h q) -> p h q", h=NH)

                tt_(new(spn), new(spn), across(cst[0:TS, S4U:S4U + TS], NH), MUL)
                link(l, V.tensor_copy(rd[:, 6, :], sp[:, 7 * P:8 * P]))
                for pg in range(5, -1, -1):
                    m = tt_(rd[:, pg, :], rd[:, pg + 1, :], sp[:, (pg + 1) * P:(pg + 2) * P], ADD)
                    if pg:
                        link(l, m)
                m.then_inc(de_dve.sem, 1)
                dve.wait_ge(de_pe.sem, de_pe.upto(l, 2))
                tt_(sa[:, 0:1024], zb[:, 0:1024], ps[:, 2:4, :].rearrange("p b n -> p (b n)"), SUB)
                link(l, tt_(tn[0:TS, :], zbn[0:TS, :], ps[0:TS, 4, 0:P], SUB))
                tt_(new(tn), new(tn), across(cst[0:TS, NEG4:NEG4 + TS], NH), ADD).then_inc(de_dve.sem, 1)
                dve.wait_ge(cache_used.sem, cache_used.upto(l, 32))
                for q in range(2):
                    r = slice(64 * q, 64 * q + 64)
                    m = V.tensor_copy(y[r, 6:8, TP:T],
                                      ps[r, 5, 0:P].rearrange("p (f h q) -> p f h q", f=2, h=2)[:, :, q, :])
                m.then_inc(de_dve.sem, 1)

            def rwkv_pre(l):
                pr = proj[:, P_RWKV:P_RWKV + 8, :]
                dve.wait_ge(kv_stored.sem, kv_stored.upto(l, 2))
                prs, xss = (v[:, :, TP:T].rearrange("p f (s t) -> p f s t", s=NSEQ) for v in (pr, xs))
                tt_(xs[:, :, 1:TP], pr[:, :, 0:TP - 1], pr[:, :, 1:TP], SUB)
                ts(xs[:, :, 0:1], pr[:, :, 0:1], -1.0, MUL)
                tt_(xss[:, :, :, 1:TD], prs[:, :, :, 0:TD - 1], prs[:, :, :, 1:TD], SUB)
                link(l, tt_(xss[:, :, :, 0], lp[:, SSHIFT:SSHIFT + 64].rearrange("p (f s) -> p f s", f=8),
                            prs[:, :, :, 0], SUB))
                for j in range(8):
                    m = stt(xs[:, j, :], xs[:, j, :], col(MU + j), pr[:, j, :], MUL, ADD)
                m.then_inc(rp_dve.sem, 1)
                dve.wait_ge(rp_dve.sem, rp_dve.upto(l, 1))
                for ft in range(2):
                    m = ts(kkv[:, ft, :], k_[:, ft, :], col(KK_ + ft), MUL)
                link(l, m)
                tt_(bon, kkv, kkv, MUL).then_inc(rp_dve.sem, 1)
                dve.wait_ge(rp_pe.sem, rp_pe.upto(l, 2))
                for ft in range(2):
                    m = ts(halves(xt2[:, ft, :]), pair(2 + ft), 1e-24, MAX)
                m.then_inc(rp_dve.sem, 1)
                dve.wait_ge(rp_act.sem, rp_act.upto(l, 6))
                tt_(kkv, kkv, xt2, MUL)
                for ft in range(2):
                    m = ts(e2[:, ft, :], bv[:, ft, :], -1.0, ADD, col(KA + ft), MUL)
                link(l, m)
                tt_(bv, kkv, bv, MUL)
                link(l, stt(k_, e2, 1.0, k_, ADD, MUL))
                for ft in range(2):
                    m = stt(bon[:, ft, :], r_[:, ft, :], col(RK + ft), k_[:, ft, :], MUL, MUL)
                m.then_inc(rp_dve.sem, 1)
                link(l, ts(e1, e1, -float(np.exp(-0.5)), MUL))
                for ft in range(2):
                    m = V.tensor_tensor_scan(e3[:, ft, :], cst[:, SCANM:SCANM + T], e1[:, ft, :], 0.0, MUL, ADD)
                link(l, m)
                tt_(e2, e3, e1, SUB).then_inc(rp_dve.sem, 1)
                dve.wait_ge(rp_pe.sem, rp_pe.upto(l, 3))
                for ft in range(2):
                    m = tt_(halves(bon[:, ft, :]), pair(2 + ft), halves(v_[:, ft, :]), MUL)
                m.then_inc(rp_dve.sem, 1)
                dve.wait_ge(rp_act.sem, rp_act.upto(l, 7))
                dve.wait_ge(wkv_stored.sem, wkv_stored.upto(l, 0))
                for v in (AtP, RtP, BtP):
                    V.memset(v[:, :, :], 0.0)
                link(l, V.memset(sbd[:, :, :], 0.0))

            def scaled(l, c, n, ends, split):
                V.tensor_copy(*ends)
                stt(At[:, :, 0:n], kkv[:, :, c], -1.0, e2[:, :, c], MUL, MUL)
                tt_(Rt[:, :, 0:n], r_[:, :, c], e1[:, :, c], MUL)
                tt_(Bt[:, :, 0:n], bv[:, :, c], e3[:, :, c], MUL)
                link(l, tt_(Kt_[:, :, 0:n], k_[:, :, c], e3[:, :, c], MUL))
                e, k = ends[0], split
                for o, i in ((Bp, Bt), (Kp, Kt_)):
                    tt_(o[:, :, 0:n].rearrange("p f (c n) -> p f c n", c=k),
                        i[:, :, 0:n].rearrange("p f (c n) -> p f c n", c=k),
                        e.unsqueeze(3).to_broadcast([P, 2, k, n // k]), MUL)
                for o, i in ((AtP, At), (RtP, Rt), (BtP, Bt)):
                    o = o.rearrange("p (f q) n -> p f q n", f=2)
                    for q in range(2):
                        r = slice(64 * q, 64 * q + 64)
                        m = V.tensor_copy(o[r, :, q, 0:n], i[r, :, 0:n])
                return m

            def flat(v):
                return v.rearrange("p h n -> p (h n)")

            def bank(b):
                return ps[:, b, :].rearrange("p (h n) -> p h n", h=NH)

            def rwkv_tiles(l):
                first = own[0]
                settled()
                with dve.Fori(0, NTT) as tt:
                    own[0] = first + tt * RW_LINKS
                    count = 0

                    def tlink(ins):
                        nonlocal count
                        count += 1
                        link(l, ins)

                    def tile_pe(n):
                        dve.wait_ge(rw_pe.sem, rw_pe.upto(l, n + tt * RW_PE))

                    def tile_act(n):
                        dve.wait_ge(rw_act.sem, rw_act.upto(l, n + tt * RW_ACT))

                    def masked(o, b, at):
                        return tt_(o, bank(b), across(cst[:, at:at + P], NH), MUL)

                    c = bass.ds(tt * P, P)
                    V.tensor_copy(stmp[:, :, :], v_[:, :, c])
                    ends = e1[:, :, c].rearrange("p f (c n) -> p f c n", c=2)[:, :, :, CH - 1]
                    scaled(l, c, P, (pend, ends), 2).then_inc(rw_dve.sem, 1)
                    count += 1
                    tile_pe(1)
                    masked(MA, 0, M16U)
                    masked(MB, 1, M16L)
                    masked(ET32, 1, E32L)
                    masked(E64, 1, E64L).then_inc(rw_dve.sem, 1)
                    dve.wait_ge(rw_dve.sem, rw_dve.upto(l, 2 + tt * RW_DVE))
                    tt_(ME, MA, across(cst[:, IDENT:IDENT + P], NH), ADD)
                    tile_pe(3)
                    V.tensor_copy(flat(MC), ps[:, 0, :]).then_inc(rw_dve.sem, 1)
                    masked(LakT, 2, SU64)
                    masked(MrbT, 3, LE64)
                    masked(MrkT, 4, LE64)
                    tile_pe(4)
                    tt_(flat(MF), flat(ME), ps[:, 0, :], ADD).then_inc(rw_dve.sem, 1)
                    tile_pe(5)
                    dve.wait_ge(rw_dve.sem, rw_dve.upto(l, 4 + tt * RW_DVE))
                    tt_(flat(ME), flat(MF), ps[:, 0, :], ADD).then_inc(rw_dve.sem, 1)
                    tile_pe(6)
                    dve.wait_ge(rw_dve.sem, rw_dve.upto(l, 5 + tt * RW_DVE))
                    tt_(flat(MF), flat(ME), ps[:, 0, :], ADD).then_inc(rw_dve.sem, 1)
                    tile_pe(8)
                    dve.wait_ge(rw_dve.sem, rw_dve.upto(l, 6 + tt * RW_DVE))
                    tt_(flat(ME), flat(MF), ps[:, 5, :], ADD).then_inc(rw_dve.sem, 1)
                    tile_pe(10)
                    dve.wait_ge(rw_dve.sem, rw_dve.upto(l, 7 + tt * RW_DVE))
                    tt_(flat(MF), flat(ME), ps[:, 2, :], ADD).then_inc(rw_dve.sem, 1)
                    for ch in range(2):
                        rows = slice(CH * ch, CH * ch + CH)
                        tt_(stmp[:, :, :], sbd[:, :, :], over(pend[:, :, ch], P), MUL)
                        tile_pe(12 + 3 * ch)
                        V.tensor_copy(sat[rows, :], ps[rows, 1, 0:256]).then_inc(rw_dve.sem, 1)
                        tile_pe(13 + 3 * ch)
                        for q in range(2):
                            r = slice(64 * q, 64 * q + 64)
                            m = tt_(sbd[r, :, r], stmp[r, :, r],
                                    ps[r, 3, 0:256].rearrange("p (f n) -> p f n", f=2)[:, :, r], ADD)
                        m.then_inc(rw_dve.sem, 1)
                        dve.wait_ge(rw_dve.sem, rw_dve.upto(l, 10 + 2 * ch + tt * RW_DVE))
                    tile_pe(17)
                    V.tensor_copy(yb[:, :, c], ps[:, 7, 0:256].rearrange("p (f n) -> p f n", f=2))\
                        .then_inc(rw_dve.sem, 1)
                    assert count == RW_LINKS, count
                own[0] = first + NTT * RW_LINKS

            def rwkv_sample(l):
                def small(v):
                    return v[0:TS, :, 0:TS]

                def sbank(b):
                    return ps[0:TS, b, 0:P].rearrange("p (h n) -> p h n", h=NH)

                def masked(o, b, at):
                    return tt_(small(o), sbank(b), across(cst[0:TS, at:at + TS], NH), MUL)

                ends = e1[:, :, TP:T].rearrange("p f (s t) -> p f s t", s=NSEQ)[:, :, :, TD - 1]
                scaled(l, slice(TP, T), TS, (pends, ends), NSEQ).then_inc(rs_dve.sem, 1)
                dve.wait_ge(rs_pe.sem, rs_pe.upto(l, 1))
                link(l, masked(MA, 0, S4U))
                masked(MB, 1, S4L)
                tt_(small(ME), small(MA), across(cst[0:TS, IDENT:IDENT + TS], NH), ADD)
                masked(LakT, 2, S4U)
                masked(MrbT, 3, LE4)
                masked(MrkT, 4, LE4).then_inc(rs_dve.sem, 1)
                dve.wait_ge(rs_pe.sem, rs_pe.upto(l, 2))
                V.tensor_copy(small(MD), sbank(0))
                V.tensor_copy(stmp[:, :, 0:TS], ps[:, 1, 0:2 * TS].rearrange("p (f n) -> p f n", f=2))\
                    .then_inc(rs_dve.sem, 1)
                dve.wait_ge(rs_pe.sem, rs_pe.upto(l, 3))
                tt_(small(MF), small(ME), sbank(0), ADD).then_inc(rs_dve.sem, 1)
                dve.wait_ge(rs_act.sem, rs_act.upto(l, 3))
                seqm = over(cst[0:TS, SEQM:SEQM + NSEQ], 256)
                tt_(sam[0:TS], across(sat[0:TS, :], NSEQ), seqm, MUL).then_inc(rs_dve.sem, 1)
                dve.wait_ge(rs_pe.sem, rs_pe.upto(l, 5))
                V.tensor_copy(yb[:, :, TP:T], ps[:, 7, 0:2 * TS].rearrange("p (f n) -> p f n", f=2))
                dve.wait_ge(rs_pe.sem, rs_pe.upto(l, 6))
                tt_(sam[0:TS], across(vt[0:TS, :], NSEQ), seqm, MUL).then_inc(rs_dve.sem, 1)
                st = lp[:, SWKV:SWKV + 2 * NSEQ * HD].rearrange("p (f s i) -> p f s i", f=2, s=NSEQ)
                link(l, tt_(st, st, pends.unsqueeze(3).to_broadcast([P, 2, NSEQ, HD]), MUL))
                dve.wait_ge(rs_pe.sem, rs_pe.upto(l, 7))
                tt_(st, st, ps[:, 3:5, :].rearrange("p f (s i) -> p f s i", s=NSEQ), ADD)\
                    .then_inc(wkv_ready.sem, 1)

            def group_norm(l):
                dve.wait_ge(wkv_ready.sem, wkv_ready.upto(l, 1))
                V.memset(pause_col(), 0.0).then_inc(gn_dve.sem, 1)
                dve.wait_ge(gn_pe.sem, gn_pe.upto(l, 1))
                for ft in range(2):
                    m = stt(halves(yb[:, ft, :]), pair(ft), -1.0 / HD, halves(yb[:, ft, :]), MUL, ADD)
                link(l, m)
                tt_(e2, yb, yb, MUL).then_inc(gn_dve.sem, 1)
                dve.wait_ge(gn_act.sem, gn_act.upto(l, 1))
                link(l, tt_(yb, yb, e2, MUL))
                for ft in range(2):
                    m = ts(yb[:, ft, :], yb[:, ft, :], col(LG + ft), MUL, col(LB + ft), ADD)
                link(l, m)
                link(l, tt_(yb, yb, bon, ADD))
                tt_(yb, yb, gg, MUL).then_inc(mix_done.sem, 1)

            V.memset(pause_col(), 0.0).then_inc(mod_done.sem, mod_done.credit)
            for sg in (h_done, x_done, in_act, in_dve, merge_done, cache_used, part, mix_done, stored, wkv_stored):
                V.memset(pause_col(), 0.0).then_inc(sg.sem, sg.credit)
            dve.wait_ge(start_loaded.sem, 48)
            with dve.Fori(0, DEPTH) as l:
                own[0] = 0
                dve.wait_ge(lp_loaded.sem, lp_loaded.upto(l, 1))
                settled()
                with dve.Fori(0, ADA_FIRST // R) as it:
                    for s in range(R):
                        keep_modulation(l, PART0["ada"] + s + 1, s, s, it, R)
                modulation_factors(l, ADA_FIRST, (0,), ())
                ffn(l, 0)
                norm(l, 1)
                for j in range(11):
                    if j < NBOTH:
                        dve.wait_ge(part.sem, part.upto(l, PART0["in"] + in_place(j)[1] + 2))
                        V.tensor_copy(halves(proj[:, 2 * IN_ORDER[j] + 1, :]), pair((2 * j + 1) % 4))\
                            .then_inc(in_dve.sem, 1)
                    if j < ADA_IN:
                        keep_modulation(l, PART0["in"] + in_place(j)[1] + 3, ADA_FIRST + FT + j, next_bank(j))
                dve.wait_ge(in_act.sem, in_act.upto(l, NBOTH))
                dve.wait_ge(in_dve.sem, in_dve.upto(l, NBOTH))
                modulation_factors(l, 36, (2,), (64,))
                dve.wait_ge(stored.sem, stored.upto(l, 0))
                conv(l)
                pooling(l)
                dve.wait_ge(in_act.sem, in_act.upto(l, in_act.per_layer))
                sh = proj[:, P_RWKV:P_RWKV + 8, :]
                V.tensor_copy(so_shift[:, :, 0:1], sh[:, :, TP - 1:TP])
                V.tensor_copy(so_shift[:, :, 1:9], sh[:, :, TP:T].rearrange(
                    "p f (s t) -> p f s t", s=NSEQ)[:, :, :, TD - 1]).then_inc(so_ready.sem, 1)
                qk_norm(l)
                attention(l)
                sample_attention(l)
                rwkv_pre(l)
                rwkv_tiles(l)
                rwkv_sample(l)
                group_norm(l)
                first = own[0]
                settled()
                with dve.Fori(0, 4) as g:
                    own[0] = first + g * 6
                    for q in range(8):
                        i, c = q // 2, q % 2
                        dve.wait_ge(part.sem, part.upto(l, PART0["gate"] + 2 * q + 2 + g * 16))
                        dve.wait_ge(gate_done.sem, gate_done.upto(l, q + 1 + g * 8))
                        mt = merged[:, c + g * 2, :]
                        dve.wait_ge(merge_done.sem, merge_done.upto(l, q + g * 8))
                        dst = mt if i == 0 else ptmp[:, :]
                        m = tt_(halves(dst), halves(gt[:, q % 2, :]), pair(2 * (q % 2) + 1), MUL)
                        if i:
                            link(l, m)
                            m = tt_(mt, mt, ptmp[:, :], ADD)
                        m.then_inc(merge_done.sem, 1)
                own[0] = first + 4 * 6
                for m in range(KT):
                    dve.wait_ge(part.sem, part.upto(l, PART0["out"] + m + 1))
                    residual(l, m, m % 2, 40)
                ffn(l, 1)
                assert own[0] == VEC_LINKS, ("VEC_LINKS", own[0])


def kernel(**a):
    import concourse.bacc as bacc
    from concourse.bass_utils import run_bass_kernel_spmd

    a = {k: np.asarray(v) for k, v in a.items()}
    L = DEPTH

    def c(v):
        return np.ascontiguousarray(v)

    def feat(v):
        v = v.reshape(v.shape[:-1] + (-1, P))
        return np.moveaxis(v, (-1, -2), (0, 1))

    tokens = np.concatenate([a["x_prompt"][0], a["x_sample"].reshape(TS, D_MODEL)], 0)
    cond = np.concatenate([a["c_prompt"], a["c_sample"]], 0)
    packs = []
    for l in range(L):
        vecs = [a["ada_b"][l], a["norm_g"][l].reshape(-1), a["rwkv_mu"][l], a["conv_w"][l].reshape(-1),
                a["rwkv_w0"][l], a["rwkv_a0"][l], a["rwkv_k_k"][l], a["rwkv_k_a"][l], a["rwkv_r_k"][l],
                a["rwkv_lnx_g"][l], a["rwkv_lnx_b"][l], a["pool_scale"][l],
                np.tile(a["q_norm_g"][l], 2), np.tile(a["k_norm_g"][l], 2)]
        cols = [np.concatenate(vecs).reshape(128, P).T, np.broadcast_to(a["sb_bias"][l], (P, NH)),
                np.concatenate([a["rwkv_w2"][l], a["rwkv_a2"][l]], 0), a["rwkv_g2"][l]]
        bd = np.zeros((P, 2, P), np.float32)
        for g in range(4):
            r = slice(64 * (g % 2), 64 * (g % 2) + 64)
            bd[r, g // 2, r] = a["pool_w"][l, g]
        cols += [bd.reshape(P, -1), feat(a["state_conv"][l]).reshape(P, -1),
                 feat(a["state_shift"][l]).reshape(P, -1), feat(a["state_pool"][l]).reshape(P, -1)]
        w = a["state_wkv"][l].reshape(NSEQ, 2, 2, HD, HD).transpose(2, 4, 1, 0, 3)
        cols.append(w.reshape(P, -1))
        packs.append(np.concatenate(cols, 1))

    def panels(w, n):
        return c(w.reshape(L, KT, P, n, 256).transpose(0, 3, 2, 1, 4).reshape(L * n, P, PANEL))

    up = a["w_ffn_up"].reshape(L, 2, KT, P, 2, FT, P).transpose(0, 1, 5, 3, 2, 4, 6)
    down = a["w_ffn_down"].reshape(L, 2, 2, DOWN_K, P, KT, P).transpose(0, 1, 5, 2, 4, 3, 6)
    gate = a["w_gate"].reshape(L, 4, KT, P, 4, 256).transpose(0, 4, 1, 3, 2, 5)
    branch = a["w_branch"].reshape(L, 4, 2, P, 4, 256).transpose(0, 4, 3, 1, 2, 5)
    keys = a["cache_k"].reshape(L * NPHYS, PAGE, 2, 2, HD).transpose(0, 3, 4, 2, 1)
    cache = np.concatenate([keys.reshape(L * NPHYS, P, 256), a["cache_v"].reshape(L * NPHYS, PAGE, 256)], 0)
    arrays = {
        "xT": c(feat(tokens)), "cT": c(feat(cond)), "constants": constants(), "params": c(np.stack(packs)),
        "page_table": c(a["page_table"].reshape(1, -1).astype(np.int32)),
        "w_ada": panels(a["ada_w"], 36), "w_up": c(up.reshape(L * 44, P, PANEL)),
        "w_down": c(down.reshape(L * 32, P, DOWN_K * P)), "w_in": panels(a["w_in"], 11)[(np.arange(L)[:, None] * 11 + IN_ORDER).reshape(-1)],
        "w_gate": c(gate.reshape(L * 16, P, PANEL)), "w_branch": c(branch.reshape(L * 4, P, PANEL)),
        "w_out": panels(a["w_out"], 4), "cache": c(cache),
    }
    outs = {"o_y": (P, KT, T), "o_k": (L, P, 2, T), "o_v": (L, P, 2, T), "o_conv": (L, P, 2, 18),
            "o_shift": (L, P, 8, 9), "o_wkv": (L, P, 2, 9, HD), "o_pool": (L, P, 2, 9 * CTX)}

    nc = bacc.Bacc("TRN2", target_bir_lowering=False, num_devices=1)
    ins = [nc.dram_tensor(k, v.shape, mybir.dt.from_np(v.dtype), kind="ExternalInput").ap()
           for k, v in arrays.items()]
    outp = [nc.dram_tensor(k, s, F32, kind="ExternalOutput").ap() for k, s in outs.items()]
    build(nc, *ins, *outp)
    r = run_bass_kernel_spmd(nc, [arrays], core_ids=[0]).results[0]

    def rows(v):
        return c(v.transpose(2, 1, 0).reshape(v.shape[2], -1))

    def both(v, prompt, sample):
        t = np.stack([rows(v[l]) for l in range(L)])
        n = int(np.prod(prompt[:-1]))
        return c(t[:, :n].reshape((L,) + prompt)), c(t[:, n:].reshape((L,) + sample))

    yy = rows(r["o_y"])
    kp, ks = both(r["o_k"], (1, TP, D_BR), (NSEQ, TD, D_BR))
    vp, vs = both(r["o_v"], (1, TP, D_BR), (NSEQ, TD, D_BR))
    cp, cs = both(r["o_conv"], (1, 2, D_BR), (NSEQ, 2, D_BR))
    shp, shs = both(r["o_shift"], (1, D_MODEL), (NSEQ, D_MODEL))
    pp, pl = both(r["o_pool"], (1, CTX, D_BR), (NSEQ, CTX, D_BR))
    wkv = r["o_wkv"].reshape(L, 2, HD, 2, 9, HD).transpose(0, 4, 3, 1, 5, 2).reshape(L, 9, NH, HD, HD)
    return (c(yy[:TP].reshape(1, TP, D_MODEL)), c(yy[TP:].reshape(NSEQ, TD, D_MODEL)),
            kp.reshape(L, 1, TP, NH, HD), vp.reshape(L, 1, TP, NH, HD), cp, shp, c(wkv[:, 0:1]), pp,
            ks.reshape(L, NSEQ, TD, NH, HD), vs.reshape(L, NSEQ, TD, NH, HD), cs, shs, c(wkv[:, 1:]), pl)
```

```python
from contextlib import ExitStack

import numpy as np

import concourse.bass as bass
from concourse import mybir

F32 = mybir.dt.float32
I32 = mybir.dt.int32
ALU = mybir.AluOpType
ACT = mybir.ActivationFunctionType

P = 128
D_MODEL, DEPTH = 1024, 2
KT = D_MODEL // P
TP, NSEQ, TD = 512, 8, 4
TS = NSEQ * TD
T = TP + TS
HALF = T // 2
NTT = TP // P
D_BR, HD, NH = 256, 64, 4
FF = 2816
FT = FF // P
DOWN_K = FT // 2
D_IN = 2816
NIN = D_IN // P
PAGE, NPAGE, NPHYS = 128, 8, 80
CH = 64
EPS, LNX_EPS = 1e-6, 64e-5
WINDOWS = (2, 4, 8, 16)
CTX = 15
R = 4
PANEL = 2048
NEG = -1e30

P_CONV, P_POOL, P_RWKV, P_Q, P_K, P_V = 0, 6, 8, 16, 18, 20
IN_FROM = (8, 9, 10, 7, 0, 1, 2, 3, 4, 5, 6)
IN_ORDER = (8, 9, 10, 3, 0, 1, 2, 4, 5, 6, 7)
NBOTH = 7

(IDENT, ONES, BLK, TRI, CAUS, CNEG, M16U, M16L, E32L, E64L, SU64, LE64) = [P * i for i in range(12)]
S4U = 12 * P
S4L, LE4, NEG4 = S4U + TS, S4U + 2 * TS, S4U + 3 * TS
SCANM = S4U + 4 * TS
INVC = SCANM + T
SEQM = INVC + 32
BIAS = SEQM + NSEQ
NCST = BIAS + 3


def constants():
    c = np.zeros((P, NCST), np.float32)
    i, j = np.meshgrid(np.arange(P), np.arange(P), indexing="ij")

    def same(n):
        return i // n == j // n

    for at, m in ((IDENT, i == j), (ONES, i >= 0), (BLK, same(HD)), (TRI, i >= j), (CAUS, i < j),
                  (M16U, same(16) & (i < j)), (M16L, same(16) & (i > j)),
                  (E32L, same(32) & ~same(16) & (i > j)), (E64L, same(64) & ~same(32) & (i > j)),
                  (SU64, same(CH) & (i < j)), (LE64, same(CH) & (i <= j))):
        c[:, at:at + P] = m
    c[:, CNEG:CNEG + P] = np.where(i < j, 0.0, NEG)
    s = slice(0, TS)
    c[s, S4U:S4U + TS] = (same(TD) & (i < j))[s, s]
    c[s, S4L:S4L + TS] = (same(TD) & (i > j))[s, s]
    c[s, LE4:LE4 + TS] = (same(TD) & (i <= j))[s, s]
    c[s, NEG4:NEG4 + TS] = np.where(same(TD) & (i < j), 0.0, NEG)[s, s]
    t = np.arange(T)
    c[:, SCANM:SCANM + T] = np.where(t < TP, t % CH != 0, (t - TP) % TD != 0)
    for g, w in enumerate(WINDOWS):
        c[(g % 2) * 64:(g % 2) * 64 + 64, INVC + 16 * (g // 2):INVC + 16 * (g // 2) + 16] = (
            np.float32(1) / np.minimum(w, np.arange(16) + 1).astype(np.float32))
    c[s, SEQM:SEQM + NSEQ] = i[s, 0:NSEQ] // TD == j[s, 0:NSEQ]
    c[:, BIAS:BIAS + 3] = (EPS, HD * EPS, LNX_EPS)
    return c


ADAB, NG, MU, CW, W0, A0, KK_, KA, RK, LG, LB, PSC, QN, KN, SBB = (
    0, 72, 96, 104, 110, 112, 114, 116, 118, 120, 122, 124, 126, 127, 128)
W2A2, G2, PBD = 132, 132 + 256, 132 + 512
SCONV = PBD + 256
SSHIFT = SCONV + 2 * NSEQ * 2
SPOOL = SSHIFT + 8 * NSEQ
SWKV = SPOOL + 2 * NSEQ * CTX
NLP = SWKV + 2 * NSEQ * HD

SEG = {0: (0, 0, 512), 1: (1, 0, 384), 2: (2, 0, 256), 3: (1, 384, 128)}
OFF = {kt: 512 * b + c for kt, (b, c, _) in SEG.items()}

BRANCH_ORDER = (0, 2, 3, 1)
ADA_FIRST, ADA_IN = 8, 6
STAGES = [("ada", ADA_FIRST, ADA_FIRST), ("up0", 2 * FT, 3 * FT), ("down0", 16, 16),
          ("in", 11 + ADA_IN, 22 + ADA_IN), ("gate_ac", 16, 64), ("gate_d", 8, 32), ("gate_b", 8, 16),
          ("out", 4, 8), ("up1", FT, 2 * FT),
          ("down1", 16, 16)]
assert ADA_FIRST + FT + ADA_IN == 36
PART0, _at = {}, 0
for _n, _, _k in STAGES:
    PART0[_n] = _at
    _at += _k
PARTS = _at
LOAD0 = {}
_cnt = [0] * R
for _n, _k, _ in STAGES:
    LOAD0[_n] = list(_cnt)
    if _n == "gate_d":
        _cnt = [c + (4 if s < 2 else 0) for s, c in enumerate(_cnt)]
    else:
        _cnt = [c + (_k - s + R - 1) // R for s, c in enumerate(_cnt)]
LOADS = _cnt


def in_place(j):
    return (2 * j, 3 * j) if j < ADA_IN else (j + ADA_IN, 2 * j + ADA_IN)


def last_part(stage, n):
    if stage == "ada":
        k = n + 1
    elif stage == "up0":
        k = n // 2 * 3 + 2 + n % 2
    elif stage == "in":
        k = n // 2 * 3 + 2 + n % 2 if n < 2 * ADA_IN else 2 * (n - ADA_IN) + 2 + ADA_IN
    elif stage.startswith("down"):
        k = n + 1
    elif stage in ("gate_ac", "gate_d"):
        k = n // 2 * 8 + 7 + n % 2
    elif stage == "gate_b":
        k = n // 2 * 4 + 3 + n % 2
    else:
        k = 2 * n + 2
    return PART0[stage] + k


PART_STEP = {"ada": 4, "up0": 6, "up1": 8, "down0": 4, "down1": 4, "gate_ac": 16, "gate_d": 8,
             "gate_b": 8, "out": 8}

VEC_LINKS, ACT_LINKS, RW_LINKS = 117, 17, 5


class Signal:

    def __init__(self, sem, per_layer, credit=0, unit=1):
        self.sem, self.per_layer, self.credit, self.unit = sem, per_layer, credit, unit

    def upto(self, layer, n):
        return layer * (self.per_layer * self.unit) + (n * self.unit + self.credit)


def build(nc, xT, cT, cst_d, lp_d, pages_d, w_ada, w_up, w_down, w_in, w_gate, w_branch, w_out,
          cache_d, o_y, o_k, o_v, o_conv, o_shift, o_wkv, o_pool):
    ctx = ExitStack()
    with ctx:
        def sb(name, shape, dt=F32):
            return ctx.enter_context(nc.sbuf_tensor(name, shape, dt))

        def signal(name, per_layer, credit=0, unit=1):
            return Signal(ctx.enter_context(nc.semaphore(name)), per_layer, credit, unit)

        x = sb("x", [P, KT, T])
        u = sb("u", [P, KT, T])
        proj = sb("proj", [P, NIN, T])
        y = sb("y", [P, KT, T])
        ring = sb("ring", [P, R, PANEL])
        masked_room = sb("masked_room", [P, 16 * P])
        cst = sb("cst", [P, NCST])
        lp = sb("lp", [P, NLP])
        mod = sb("mod", [P, 72, 9])
        mod_a = sb("mod_a", [P, 24, 9])
        csil = sb("csil", [P, KT, 9])
        stage_out = sb("stage_out", [P, 2 * 18 + 8 * 9 + 2 * 9 * CTX])
        pages = sb("pages", [1, NSEQ * NPAGE], I32)
        ws = sb("ws", [P, 10760])
        hid, merged = proj, proj
        so_conv = stage_out[:, 0:36].rearrange("p (f n) -> p f n", f=2)
        so_shift = stage_out[:, 36:108].rearrange("p (f n) -> p f n", f=8)
        so_pool = stage_out[:, 108:378].rearrange("p (f n) -> p f n", f=2)

        def halves_of(v):
            return v.rearrange("p (a n) -> p a n", a=2)

        def carve(at, *shape):
            n = int(np.prod(shape))
            v = ws[:, at:at + n]
            if len(shape) == 2:
                v = v.rearrange("p (a b) -> p a b", a=shape[0])
            if len(shape) == 3:
                v = v.rearrange("p (a b c) -> p a b c", a=shape[0], b=shape[1])
            if len(shape) == 4:
                v = v.rearrange("p (a b c d) -> p a b c d", a=shape[0], b=shape[1], c=shape[2])
            return v, at + n

        CR = 4 * 1024
        cache, at = carve(0, 4, 4, 256)
        sq, at1 = carve(at, 2, T)
        rs, at1 = carve(at1, T)
        gt, at1 = carve(at1, 2, T)
        ptmp, at1 = carve(at1, T)
        zc, at1 = carve(at, 2, TP + 2)
        zs, at1 = carve(at1, 2, NSEQ, TD + 2)
        pe, at1 = carve(at1, 2, TP + CTX)
        pes, at1 = carve(at1, 2, NSEQ, TD + CTX)
        s2s, at1 = carve(at1, 2, NSEQ, 18)
        s4s, at1 = carve(at1, 2, NSEQ, 16)
        s8s, at1 = carve(at1, 2, NSEQ, 12)
        s16s, at1 = carve(at1, 2, NSEQ, 4)
        pd, at1 = carve(at1, 2, T)
        fix, at1 = carve(at1, 2, 16)
        conv_end = at1
        NZ = 1280
        vtok, at1 = carve(at, 5, 256)
        spn, at1 = carve(at1, P)
        zbn, at1 = carve(at1, P)
        tn, at1 = carve(at1, P)
        qp, at1 = carve(at1, 2, NSEQ, 8)
        atq = at1
        sqk, at1 = carve(10760 - 4 * T, 4, T)
        assert conv_end <= 10760 - 4 * T
        zb, at1 = carve(atq, NZ)
        sp, at1 = carve(at1, NZ)
        sa, at1 = carve(at1, NZ)
        rd, at1 = carve(at1, 7, P)
        assert at1 <= 10760, at1
        at = CR
        Bt, at = carve(at, 2, P)
        At, at = carve(at, 2, P)
        Rt, at = carve(at, 2, P)
        Kt_, at = carve(at, 2, P)
        Bp, at = carve(at, 2, P)
        Kp, at = carve(at, 2, P)
        AtP, at = carve(at, 4, P)
        RtP, at = carve(at, 4, P)
        BtP, at = carve(at, 4, P)
        mat0 = at
        MA, at = carve(at, 4, P)
        MB, at = carve(at, 4, P)
        MC, at = carve(at, 4, P)
        MD, at = carve(at, 4, P)
        ME, at = carve(at, 4, P)
        MF, at = carve(at, 4, P)
        ET32, at = carve(at, 4, P)
        sam, _ = carve(mat0, NSEQ, 256)
        assert at <= 10760, at
        r_, k_, v_ = y[:, 4:6, :], proj[:, 16:18, :], proj[:, 18:20, :]
        xt2 = proj[:, 20:22, :]
        kkv, bv = proj[:, 8:10, :], proj[:, 10:12, :]
        gg, bon = proj[:, 12:14, :], proj[:, 14:16, :]
        e1, at = carve(0, 2, T)
        e3, at = carve(at, 2, T)
        e2, at = carve(at, 2, T)
        sig_d, at = carve(at, 2, HALF)
        prod_d, at = carve(at, HALF)
        assert at <= CR
        sig_ac, prod_ac = halves_of(y[:, 2, :]), y[:, 3, 0:HALF]
        yb = y[:, 2:4, :]
        wb = masked_room[:, :]
        E64 = wb[:, 0:512].rearrange("p (h n) -> p h n", h=4)
        LakT = wb[:, 512:1024].rearrange("p (h n) -> p h n", h=4)
        MrbT = wb[:, 1024:1536].rearrange("p (h n) -> p h n", h=4)
        MrkT = wb[:, 1536:2048].rearrange("p (h n) -> p h n", h=4)
        xtf = xt2.rearrange("p f n -> p (f n)")
        turned, vt, r0 = xtf[:, 0:512], xtf[:, 512:768], xtf[:, 768:1024]
        bptok, kptok = xtf[:, 0:256], xtf[:, 256:512]
        rtail = sb("rtail", [P, 3 * 256 + 4 + 16])
        sat = rtail[:, 0:256]
        sbd = rtail[:, 256:512].rearrange("p (f n) -> p f n", f=2)
        stmp = rtail[:, 512:768].rearrange("p (f n) -> p f n", f=2)
        pend = rtail[:, 768:772].rearrange("p (f n) -> p f n", f=2)
        pends = rtail[:, 772:788].rearrange("p (f n) -> p f n", f=2)
        ps = ctx.enter_context(nc.psum_tensor("ps", [P, 8, 512], F32))

        MODC = 480

        def pair(b):
            return ps[:, 2 * b:2 * b + 2, 0:HALF]

        def halves(v):
            return v.rearrange("p (a n) -> p a n", a=2)

        pause = sb("pause", [P, 32])
        paused = [0]

        def pause_col():
            paused[0] += 1
            return pause[:, paused[0] - 1:paused[0]]

        def settled(bank=None):
            if bank is None:
                nc.vector.memset(pause_col(), 0.0)
            else:
                nc.tensor.matmul(ps[:, bank, 0:1], cst[:, ONES:ONES + P], cst[:, 0:1], start=True, stop=True)

        def next_bank(q):
            return 4 * ((q + 1) % 2) + 3

        def kept(j, c):
            if j < NBOTH:
                return (in_dve if c else in_act), j + 1
            return in_act, NBOTH + 2 * (j - NBOTH) + c + 1

        def col(at, n=1):
            return lp[:, at:at + n]

        def seqs(v):
            return v.rearrange("p (s t) -> p s t", s=NSEQ)

        def over(v, n):
            return v.unsqueeze(2).to_broadcast([v.shape[0], v.shape[1], n])

        def across(v, n):
            return v.unsqueeze(1).to_broadcast([v.shape[0], n, v.shape[1]])

        loaded = [signal(f"panel_loaded{s}", LOADS[s], unit=16) for s in range(R)]
        lp_loaded = signal("params_loaded", 1, unit=16)
        start_loaded = signal("start_loaded", 0, unit=16)
        pages_loaded = signal("pages_loaded", 0, unit=16)
        cache_loaded = [signal(f"cache_loaded{s}", 8 * 4, unit=16) for s in range(4)]
        stored = signal("states_stored", 3, credit=16, unit=16)
        kv_stored = signal("kv_stored", 2, unit=16)
        wkv_stored = signal("wkv_stored", 3, credit=16, unit=16)
        y_stored = signal("y_stored", 0, unit=16)
        part = signal("part_done", PARTS, credit=1)
        mod_done = signal("mod_tiles", 36, credit=4)
        csil_done = signal("csil_done", 0)
        sq_done = signal("squares", 24)
        sum_done = signal("square_sums", 24)
        rt_done = signal("roots", 3)
        un_done = signal("normed", 24)
        up_done = signal("u_prompt", 24)
        us_done = signal("u_sample", 3)
        silu_done = signal("silu", 2 * FT)
        h_done = signal("hidden", 2 * FT, credit=2)
        x_done = signal("x_tiles", 24, credit=2)
        in_act = signal("proj_act", 22 - NBOTH, credit=2)
        in_dve = signal("proj_dve", NBOTH, credit=2)
        gate_done = signal("gate_sigmoid", 8)
        merge_done = signal("merged", 8, credit=2)
        fill_gate = signal("half_gates", 48, credit=1)
        fill_sum = signal("half_merged", 48, credit=1)
        so_ready = signal("states_staged", 3)
        kn_ready = signal("k_normed", 1)
        wkv_ready = signal("wkv_ready", 1)
        mix_done = signal("mix_done", 1, credit=1)
        pool_in = signal("pool_in", 1)
        pool_pe = signal("pool_products", 1)
        pool_out = signal("pool_out", 1)
        qk_sq = signal("qk_squares", 1)
        qk_sum = signal("qk_sums", 1)
        qk_ms = signal("qk_logs", 1)
        qk_rt = signal("qk_roots", 1)
        vt_pe = signal("v_turned", 1)
        vt_act = signal("v_tokens", 1)
        qp_done = signal("q_padded", 1)
        cache_used = signal("cache_used", 32 + 4, credit=4)
        at_pe = signal("att_products", 4 * 3)
        at_dve = signal("att_vector", 4 * 3)
        at_act = signal("att_scalar", 4 * 3)
        de_pe = signal("dec_products", 2)
        de_dve = signal("dec_vector", 4)
        de_act = signal("dec_scalar", 2)
        RW_PE, RW_DVE, RW_ACT = 10 + 2 * 3 + 1, 8 + 2 * 2 + 1, 6 + 2
        rp_pe = signal("rwkv_pre_products", 3)
        rp_dve = signal("rwkv_pre_vector", 6)
        rp_act = signal("rwkv_pre_scalar", 7)
        rw_pe = signal("rwkv_tile_products", NTT * RW_PE)
        rw_dve = signal("rwkv_tile_vector", NTT * RW_DVE)
        rw_act = signal("rwkv_tile_scalar", NTT * RW_ACT)
        rs_pe = signal("rwkv_sample_products", 7)
        rs_dve = signal("rwkv_sample_vector", 6)
        rs_act = signal("rwkv_sample_scalar", 3)
        gn_pe = signal("group_norm_sums", 2)
        gn_dve = signal("group_norm_vector", 2)
        gn_act = signal("group_norm_root", 1)
        vec = signal("vector_chain", VEC_LINKS)
        act_own = signal("scalar_chain", ACT_LINKS)

        block = ctx.enter_context(nc.Block())

        @block.sync
        def _(sp_):
            sp_.dma_start(cst[:, :], cst_d).then_inc(start_loaded.sem, 16)
            sp_.dma_start(csil[:, :, :], cT).then_inc(start_loaded.sem, 16)
            sp_.dma_start(x[:, :, :], xT).then_inc(start_loaded.sem, 16)

            srcs = {"up1": w_up, "down0": w_down, "down1": w_down, "out": w_out}

            def source(stage, l, i, s):
                if stage == "ada":
                    return w_ada[l * 36 + i]
                if stage == "up0":
                    turn = i
                    if s % 2:
                        return w_ada[l * 36 + (turn * 2 + (ADA_FIRST + s // 2))]
                    return w_up[l * (2 * FT) + (turn * 2 + s // 2)]
                if stage == "in":
                    if i < 2 * ADA_IN and i % 2:
                        return w_ada[l * 36 + (ADA_FIRST + FT + i // 2)]
                    return w_in[l * 11 + (i // 2 if i < 2 * ADA_IN else i - ADA_IN)]
                if stage.startswith("gate"):
                    per_turn, first = {"gate_ac": (2, 0), "gate_d": (1, 8), "gate_b": (2, 12)}[stage]
                    turn = i
                    return (w_branch if s % 2 else w_gate)[l * 16 + (turn * per_turn + (first + s // 2))]
                f, n = int(stage[-1] == "1"), {"u": FT, "d": 16, "o": 4}[stage[0]]
                per = (2 if stage[:-1] in ("up", "down") else 1) * n
                return srcs[stage][l * per + (i + f * n)]

            with sp_.Fori(0, DEPTH) as l:
                sp_.wait_ge(mix_done.sem, mix_done.upto(l, 0))
                sp_.wait_ge(wkv_stored.sem, wkv_stored.upto(l, 0))
                sp_.dma_start(lp[:, :], lp_d[l]).then_inc(lp_loaded.sem, 16)

                prev = [None] * R
                for stage, n, _ in STAGES:
                    def load(i, s, wait):
                        width = (DOWN_K * P if stage.startswith("down") else
                                 512 if stage.startswith("gate") and s % 2 else PANEL)
                        sp_.wait_ge(part.sem, wait)
                        sp_.dma_start(ring[:, s, 0:width], source(stage, l, i, s))\
                            .then_inc(loaded[s].sem, 16)

                    slots = 2 if stage == "gate_d" else R
                    by_turn = stage == "up0" or stage.startswith("gate")
                    for s in range(min(slots, n)):
                        load(0 if by_turn else s, s,
                             part.upto(l, 0 if prev[s] is None else prev[s]))
                    trips = n // slots if stage != "in" else 1
                    if trips > 1:
                        with sp_.Fori(1, trips) as it:
                            for s in range(slots):
                                load(it if by_turn else it * R + s, s,
                                     part.upto(l, last_part(stage, s) - PART_STEP[stage]
                                               + it * PART_STEP[stage]))
                    for i in range(max(trips, 1) * slots, n):
                        load(i, i % R, part.upto(l, last_part(stage, i - R)))
                    for s in range(slots):
                        prev[s] = last_part(stage, (n - 1 - s) // slots * slots + s)
            sp_.wait_ge(x_done.sem, x_done.upto(DEPTH, 0))
            sp_.dma_start(o_y, x[:, :, :]).then_inc(y_stored.sem, 16)
            sp_.wait_ge(y_stored.sem, 16)
            sp_.wait_ge(stored.sem, stored.upto(DEPTH, 0))
            sp_.wait_ge(kv_stored.sem, kv_stored.upto(DEPTH, 0))
            sp_.wait_ge(wkv_stored.sem, wkv_stored.upto(DEPTH, 0))

        @block.gpsimd
        def _(pool):
            pool.dma_start(pages[:, :], pages_d).then_inc(pages_loaded.sem, 16)
            pool.wait_ge(pages_loaded.sem, 16)
            with pool.Fori(0, DEPTH) as l:
                with pool.Fori(0, 2) as kv:
                    with pool.Fori(0, 4) as turn:
                        for s in range(4):
                            n = kv * 16 + turn * 4 + s
                            pool.wait_ge(cache_used.sem, cache_used.upto(l, n - 3))
                            for pg in range(4):
                                page = pool.value_load(
                                    pages[0:1, bass.ds(turn * 16 + (4 * s + pg), 1)],
                                    min_val=0, max_val=NPHYS - 1)
                                dst = cache[:, s, pg, :]
                                pool.dma_start(dst, cache_d[kv * (DEPTH * NPHYS) + l * NPHYS + page])\
                                    .then_inc(cache_loaded[s].sem, 16)

        @block.tensor
        def _(pe_):
            def mm(out, lhsT, rhs, start=True, stop=True, skip=False):
                return nc.tensor.matmul(out, lhsT, rhs, start=start, stop=stop, skip_group_check=skip)

            def cmat(at, n=P, rows=P):
                return cst[0:rows, at:at + n]

            def tile(b, w, c0, rhs, k0=0, nk=KT, ks=256, first=True, last=True):
                for k in range(nk):
                    for hf in range(2):
                        m = mm(ps[:, 2 * b + hf, 0:HALF], w[:, k * ks + c0:k * ks + c0 + P],
                               rhs[:, k0 + k, hf * HALF:hf * HALF + HALF],
                               start=first and k == 0, stop=last and k == nk - 1)
                return m

            def panel(l, stage, it, s, turn=0):
                pe_.wait_ge(loaded[s].sem, loaded[s].upto(l, LOAD0[stage][s] + turn + 1 + it))

            def sum_squares(l, n):
                for k in range(KT):
                    pe_.wait_ge(sq_done.sem, sq_done.upto(l, 8 * n + k + 1))
                    for hf in range(2):
                        m = mm(ps[:, 6 + hf, 0:HALF], cmat(ONES), sq[:, k % 2, hf * HALF:hf * HALF + HALF],
                               start=k == 0, stop=k == KT - 1)
                    m.then_inc(sum_done.sem, 1)

            def wait_u(l, n):
                pe_.wait_ge(up_done.sem, up_done.upto(l, 8 * n + 8))
                pe_.wait_ge(us_done.sem, us_done.upto(l, n + 1))

            def modulation(s, bank):
                for c in range(2):
                    for k in range(KT):
                        m = mm(ps[:, bank, MODC + c * 9:MODC + c * 9 + 9],
                               ring[:, s, k * 256 + c * P:k * 256 + c * P + P], csil[:, k, :],
                               start=k == 0, stop=k == KT - 1)
                m.then_inc(part.sem, 1)

            def ffn(l, f):
                sum_squares(l, 2 * f)
                wait_u(l, 2 * f)

                def up_turn(it, first, units):
                    for q in range(first, first + units):
                        place, per_turn = (2 * q, 2) if f == 0 else (q, 1)
                        s = place % R
                        panel(l, f"up{f}", it * per_turn, s, place // R)
                        pe_.wait_ge(h_done.sem, h_done.upto(l, f * FT + q - 1 + it * 4))
                        b = 2 * (q % 2)
                        tile(b, ring[:, s, :], 0, u).then_inc(part.sem, 1)
                        if f == 0:
                            pe_.wait_ge(mod_done.sem, mod_done.upto(l, ADA_FIRST + q + it * 4))
                        tile(b + 1, ring[:, s, :], P, u).then_inc(part.sem, 1)
                        if f == 0:
                            panel(l, "up0", it * 2, s + 1, place // R)
                            pe_.wait_ge(h_done.sem, h_done.upto(l, q + it * 4))
                            modulation(s + 1, next_bank(q))

                settled(6)
                with pe_.Fori(0, FT // 4) as it:
                    up_turn(it, 0, 4)
                up_turn(0, FT // 4 * 4, FT % 4)
                pe_.wait_ge(h_done.sem, h_done.upto(l, (f + 1) * FT))
                if f == 0:
                    pe_.wait_ge(mod_done.sem, mod_done.upto(l, ADA_FIRST + FT))
                settled(7)
                with pe_.Fori(0, KT // 2) as it:
                    for b in range(2):
                        pe_.wait_ge(x_done.sem, x_done.upto(l, 16 * f + b - 1 + it * 2))
                        for hf in range(2):
                            panel(l, f"down{f}", it, 2 * b + hf)
                            tile(b, ring[:, 2 * b + hf, :], 0, hid, DOWN_K * hf, DOWN_K, P,
                                 first=hf == 0, last=hf == 1).then_inc(part.sem, 1)

            pe_.wait_ge(start_loaded.sem, 48)
            pe_.wait_ge(csil_done.sem, 1)
            with pe_.Fori(0, DEPTH) as l:
                pe_.wait_ge(x_done.sem, x_done.upto(l, 0))
                settled(7)
                with pe_.Fori(0, ADA_FIRST // R) as it:
                    for s in range(R):
                        panel(l, "ada", it, s)
                        pe_.wait_ge(mod_done.sem, mod_done.upto(l, s - 3 + it * R))
                        modulation(s, s)
                ffn(l, 0)

                sum_squares(l, 1)
                wait_u(l, 1)

                for j in range(11):
                    place = in_place(j)[0]
                    panel(l, "in", 0, place % R, place // R)
                    for c in range(2):
                        g, n = kept(j - 2, c) if j >= 2 else (in_dve if c else in_act, j - 1)
                        pe_.wait_ge(g.sem, g.upto(l, n))
                        if c and 0 < j <= ADA_IN:
                            pe_.wait_ge(mod_done.sem, mod_done.upto(l, ADA_FIRST + FT + j))
                        tile((2 * j + c) % 4, ring[:, place % R, :], c * P, u).then_inc(part.sem, 1)
                    if j < ADA_IN:
                        panel(l, "in", 0, place % R + 1, place // R)
                        pe_.wait_ge(in_dve.sem, in_dve.upto(l, j))
                        modulation(place % R + 1, next_bank(j))

                pe_.wait_ge(qk_sq.sem, qk_sq.upto(l, 1))
                pe_.wait_ge(in_act.sem, in_act.upto(l, in_act.per_layer))
                for i in range(4):
                    m = tile(i, cmat(BLK), 0, sqk, i, 1)
                m.then_inc(qk_sum.sem, 1)
                pe_.wait_ge(pool_in.sem, pool_in.upto(l, 1))
                pe_.wait_ge(qk_ms.sem, qk_ms.upto(l, 1))
                for ft in range(2):
                    m = tile(2 + ft, lp[:, PBD:PBD + 256], ft * P, pd, ft, 1)
                m.then_inc(pool_pe.sem, 1)
                for tt in range(4):
                    for ft in range(2):
                        nc.tensor.transpose(ps[:, tt // 2, (tt % 2) * 256 + ft * P:(tt % 2) * 256 + ft * P + P],
                                            proj[:, P_V + ft, tt * P:tt * P + P], cmat(IDENT))
                for ft in range(2):
                    m = nc.tensor.transpose(ps[0:TS, 2, ft * P:ft * P + P], proj[:, P_V + ft, TP:T],
                                            cmat(IDENT))
                m.then_inc(vt_pe.sem, 1)
                pe_.wait_ge(vt_act.sem, vt_act.upto(l, 1))
                pe_.wait_ge(pool_out.sem, pool_out.upto(l, 1))
                pe_.wait_ge(kn_ready.sem, kn_ready.upto(l, 1))
                pe_.wait_ge(qp_done.sem, qp_done.upto(l, 1))
                def fill(stage, f, a, b, it=0):
                    first, y0, step = (0, 4 * (f // 16), 0) if stage == "gate_ac" else (32, 6, 4)
                    pair_, c, hf = f // 4, f // 2 % 2, f % 2
                    sg = 2 * pair_ % R
                    cols = slice(hf * HALF, hf * HALF + HALF)
                    for j in range(a, b):
                        gate = j < KT
                        if j in (0, KT) and f % 4 == 0:
                            panel(l, stage, it, sg + j // KT, 2 * pair_ // R)
                        if j == 0:
                            pe_.wait_ge(fill_gate.sem, fill_gate.upto(l, first + f + it * step))
                        if j == KT:
                            pe_.wait_ge(fill_sum.sem, fill_sum.upto(l, first + f + it * step))
                        k = j if gate else j - KT
                        m = mm(ps[:, 4 if gate else 5, 0:HALF],
                               ring[:, sg + (not gate), k * 256 + c * P:k * 256 + c * P + P],
                               (u if gate else y)[:, k if gate else y0 + k, cols],
                               start=k == 0, stop=j in (KT - 1, KT + 1))
                        if j in (KT - 1, KT + 1):
                            m.then_inc(part.sem, 1)

                def scores(h):
                    ft, po = h // 2, HD * (h % 2)
                    for kt in range(NTT):
                        b, c0, w = SEG[kt]
                        m = mm(ps[:, b, c0:c0 + w], proj[po:po + HD, P_K + ft, kt * P:kt * P + P],
                               proj[po:po + HD, P_Q + ft, kt * P:TP])
                    m.then_inc(at_pe.sem, 1)
                    for n in range(4 * h, 4 * h + 4):
                        s, hf = n // 2, n % 2
                        pe_.wait_ge(cache_loaded[n % 4].sem, cache_loaded[n % 4].upto(l, 4 * (n // 4 + 1)))
                        for pg in range(4):
                            for f2 in range(2):
                                o = ps[:, 6 + hf, pg * P + f2 * 64:pg * P + f2 * 64 + 64]\
                                    .rearrange("p (h q) -> p h q", h=2)[:, :, s * TD:s * TD + TD]
                                m = mm(o, cache[:, n % 4, pg, f2 * P:f2 * P + P],
                                       qp[:, f2, s, :].rearrange("p (h t) -> p h t", h=2))
                        m.then_inc(cache_used.sem, 1)

                scores(0)
                for h in range(NH):
                    po = HD * (h % 2)
                    pe_.wait_ge(at_dve.sem, at_dve.upto(l, 3 * h + 2))
                    for kt in (3, 2, 1, 0):
                        b, c0, w = SEG[kt]
                        o0 = OFF[kt]
                        for k2 in range(NTT - 1, kt, -1):
                            w2 = SEG[k2][2]
                            mm(ps[:, b, c0 + w - w2:c0 + w], cmat(ONES), sp[:, OFF[k2]:OFF[k2] + w2],
                               start=k2 == NTT - 1, stop=False, skip=True)
                        m = mm(ps[:, b, c0:c0 + w], cmat(TRI), sp[:, o0:o0 + w], start=kt == NTT - 1,
                               skip=True)
                    m.then_inc(at_pe.sem, 1)
                    fill("gate_ac", 3 * h, 0, 10)
                    if h < NH - 1:
                        pe_.wait_ge(at_dve.sem, at_dve.upto(l, 3 * h + 3))
                        scores(h + 1)
                    pe_.wait_ge(at_act.sem, at_act.upto(l, 3 * h + 2))
                    for kt in (3, 2, 1, 0):
                        w = SEG[kt][2]
                        m = mm(ps[po:po + HD, 3, TP - w:TP], vtok[:, kt, h * HD:h * HD + HD],
                               sa[:, OFF[kt]:OFF[kt] + w], start=kt == 3, stop=kt == 0, skip=True)
                    m.then_inc(at_pe.sem, 1)
                    if h < NH - 1:
                        fill("gate_ac", 3 * h + 1, 0, 10)
                        fill("gate_ac", 3 * h + 2, 0, 10)
                for h in range(NH):
                    m = mm(ps[0:TS, 1, h * TS:h * TS + TS], proj[:, P_K + h // 2, TP:T],
                           qp[:, h // 2, :, (h % 2) * TD:(h % 2) * TD + TD])
                m.then_inc(de_pe.sem, 1)
                for f in range(10, 14):
                    fill("gate_ac", f, 0, 10)
                pe_.wait_ge(de_dve.sem, de_dve.upto(l, 2))
                pe_.wait_ge(at_act.sem, at_act.upto(l, 12))
                for b in range(2):
                    n = 4 if b == 0 else 3
                    mm(ps[:, 2 + b, :], cmat(TRI), sp[:, b * 512:b * 512 + 512], stop=False, skip=True)
                    mm(ps[:, 2 + b, 0:n * P], cmat(ONES), rd[:, 4 * b:4 * b + n, :], start=False, stop=False,
                       skip=True)
                    mm(ps[:, 2 + b, :], cmat(ONES), across(spn[:, :], 4), start=False, skip=True)
                m = mm(ps[0:TS, 0, 0:P], cst[:, TRI:TRI + TS], spn[:, :])
                m.then_inc(de_pe.sem, 1)
                for f in range(14, 16):
                    fill("gate_ac", f, 0, 10)
                pe_.wait_ge(de_act.sem, de_act.upto(l, 2))
                for f2 in range(2):
                    mm(ps[:, 1, f2 * 64:f2 * 64 + 64], vtok[0:TS, 4, f2 * P:f2 * P + P],
                       tn[0:TS, f2 * 64:f2 * 64 + 64], start=f2 == 0, stop=False, skip=True)
                for n in range(16):
                    s, hf = n // 2, n % 2
                    pe_.wait_ge(cache_loaded[n % 4].sem, cache_loaded[n % 4].upto(l, 16 + 4 * (n // 4 + 1)))
                    for pg in range(4):
                        for f2 in range(2):
                            def at8(v):
                                return v.rearrange("p (h q) -> p h q", h=2)[:, :, s * TD:s * TD + TD]
                            m = mm(at8(ps[:, 1, f2 * 64:f2 * 64 + 64]), cache[:, n % 4, pg, f2 * P:f2 * P + P],
                                   at8(sa[:, (4 * hf + pg) * P + f2 * 64:(4 * hf + pg) * P + f2 * 64 + 64]),
                                   start=False, stop=hf == 1 and pg == 3, skip=True)
                    m.then_inc(cache_used.sem, 1)
                    fill("gate_ac", 16 + n, 0, 10)

                pe_.wait_ge(rp_act.sem, rp_act.upto(l, 2))
                pe_.wait_ge(de_dve.sem, de_dve.upto(l, 4))
                pe_.wait_ge(fill_sum.sem, fill_sum.upto(l, 32))
                for ft in range(2):
                    for hf in range(2):
                        c = slice(hf * HALF, hf * HALF + HALF)
                        mm(ps[:, 2 * ft + hf, 0:HALF], lp[0:64, W2A2 + ft * P:W2A2 + ft * P + P], xt2[0:64, 0, c])
                        m = mm(ps[:, 4 + 2 * ft + hf, 0:HALF], lp[64:128, W2A2 + ft * P:W2A2 + ft * P + P],
                           xt2[64:128, 0, c])
                m.then_inc(rp_pe.sem, 1)
                pe_.wait_ge(rp_act.sem, rp_act.upto(l, 4))
                pe_.wait_ge(rp_dve.sem, rp_dve.upto(l, 2))
                for ft in range(2):
                    tile(ft, lp[:, G2:G2 + 256], ft * P, xt2, 1, 1)
                for ft in range(2):
                    m = tile(2 + ft, cmat(BLK), 0, bon, ft, 1)
                m.then_inc(rp_pe.sem, 1)
                pe_.wait_ge(rp_dve.sem, rp_dve.upto(l, 4))
                for ft in range(2):
                    m = tile(2 + ft, cmat(BLK), 0, bon, ft, 1)
                m.then_inc(rp_pe.sem, 1)

                def heads(b, lhsT, rhs, n=P, rows=P):
                    for h in range(NH):
                        m = mm(ps[0:rows, b, h * n:h * n + n], lhsT(h), rhs(h))
                    return m

                def ft_of(v, n=P):
                    return lambda h: v[:, h // 2, 0:n]

                def hd_of(v, n=P, rows=P):
                    return lambda h: v[0:rows, h, 0:n]

                settled(0)
                with pe_.Fori(0, NTT) as tt:
                    def tile_dve(n):
                        return rw_dve.upto(l, n + tt * RW_DVE)

                    def tile_act(n):
                        return rw_act.upto(l, n + tt * RW_ACT)

                    pe_.wait_ge(rw_dve.sem, tile_dve(1))
                    heads(0, ft_of(Bt), hd_of(AtP))
                    heads(1, ft_of(At), hd_of(BtP)).then_inc(rw_pe.sem, 1)
                    heads(2, ft_of(Kt_), hd_of(AtP))
                    heads(3, ft_of(Bt), hd_of(RtP))
                    for ft in range(2):
                        nc.tensor.transpose(ps[:, 7, ft * P:ft * P + P], Bp[:, ft, :], cmat(IDENT))
                        nc.tensor.transpose(ps[:, 7, 256 + ft * P:256 + ft * P + P], Kp[:, ft, :], cmat(IDENT))
                    for ft in range(2):
                        m = nc.tensor.transpose(ps[:, 6, ft * P:ft * P + P], stmp[:, ft, :], cmat(IDENT))
                    m.then_inc(rw_pe.sem, 1)
                    fill("gate_d", 0, 0, 3, tt)
                    pe_.wait_ge(rw_dve.sem, tile_dve(2))
                    heads(0, hd_of(MB), hd_of(MA))
                    heads(1, hd_of(MA), hd_of(MB)).then_inc(rw_pe.sem, 1)
                    fill("gate_d", 0, 3, 6, tt)
                    pe_.wait_ge(rw_act.sem, tile_act(2))
                    pe_.wait_ge(rw_dve.sem, tile_dve(3))
                    heads(0, hd_of(MD), hd_of(ME))
                    heads(1, hd_of(MD), hd_of(MC))
                    heads(7, hd_of(MC), hd_of(MD)).then_inc(rw_pe.sem, 1)
                    fill("gate_d", 0, 6, 8, tt)
                    pe_.wait_ge(rw_act.sem, tile_act(3))
                    pe_.wait_ge(rw_dve.sem, tile_dve(4))
                    heads(0, hd_of(MB), hd_of(MF))
                    heads(3, ft_of(Kt_), hd_of(RtP))
                    heads(1, hd_of(MA), hd_of(MB)).then_inc(rw_pe.sem, 1)
                    fill("gate_d", 0, 8, 10, tt)
                    pe_.wait_ge(rw_act.sem, tile_act(4))
                    pe_.wait_ge(rw_dve.sem, tile_dve(5))
                    heads(0, hd_of(MC), hd_of(ME)).then_inc(rw_pe.sem, 1)
                    fill("gate_d", 1, 0, 3, tt)
                    pe_.wait_ge(rw_dve.sem, tile_dve(6))
                    for q, (ET, xa) in enumerate(((ET32, MF), (E64, ME))):
                        if q:
                            pe_.wait_ge(rw_dve.sem, tile_dve(7))
                        heads(0, hd_of(ET), hd_of(xa))
                        for h in range(NH):
                            m = nc.tensor.transpose(ps[:, 1, h * P:h * P + P], xa[:, h, :], cmat(IDENT))
                        m.then_inc(rw_pe.sem, 1)
                        fill("gate_d", 1, 8 if q else 3, 10 if q else 5, tt)
                        pe_.wait_ge(rw_act.sem, tile_act(5 + q))
                        heads(2 if q else 7, hd_of(MB), hd_of(MA)).then_inc(rw_pe.sem, 1)
                        fill("gate_d", 2 if q else 1, 0 if q else 5, 4 if q else 8, tt)
                    for c in range(2):
                        q0, rows = CH * c, slice(CH * c, CH * c + CH)
                        pe_.wait_ge(rw_dve.sem, tile_dve(8 + 2 * c))
                        for ft in range(2):
                            for h in (2 * ft, 2 * ft + 1):
                                mm(ps[rows, 0, h * HD:h * HD + HD], LakT[:, h, rows],
                                   vt[:, h * HD:h * HD + HD], start=h % 2 == 0, stop=False, skip=True)
                            m = mm(ps[rows, 0, ft * P:ft * P + P], At[:, ft, rows], sbd[:, ft, :],
                                   start=False, skip=True)
                        m.then_inc(rw_pe.sem, 1)
                        for ft in range(2):
                            mm(ps[:, 6, 256 + ft * P + q0:256 + ft * P + q0 + CH], sbd[:, ft, :], Rt[:, ft, rows],
                               start=c == 0 and ft == 0, stop=False, skip=True)
                        fill("gate_d", 3 if c else 2, 4, 7, tt)
                        pe_.wait_ge(rw_act.sem, tile_act(7 + c))
                        for h in range(NH):
                            m = mm(ps[rows, 1, h * HD:h * HD + HD], MF[:, h, rows],
                                   r0[:, h * HD:h * HD + HD])
                        m.then_inc(rw_pe.sem, 1)
                        fill("gate_d", 3 if c else 2, 7, 10, tt)
                        pe_.wait_ge(rw_dve.sem, tile_dve(9 + 2 * c))
                        for ft in range(2):
                            c2 = slice(ft * P, ft * P + P)
                            mm(ps[:, 3, c2], bptok[rows, c2], sat[rows, c2], stop=False)
                            m = mm(ps[:, 3, c2], kptok[rows, c2], vt[rows, c2], start=False)
                        m.then_inc(rw_pe.sem, 1)
                        if c == 0:
                            fill("gate_d", 3, 0, 4, tt)
                    for h in range(NH):
                        ft, po = h // 2, HD * (h % 2)
                        o = ps[po:po + HD, 6, 256 + ft * P:256 + ft * P + P]
                        c2 = slice(h * HD, h * HD + HD)
                        mm(o, sat[:, c2], MrbT[:, h, :], start=False, stop=False, skip=True)
                        m = mm(o, vt[:, c2], MrkT[:, h, :], start=False, skip=True)
                    m.then_inc(rw_pe.sem, 1)

                pe_.wait_ge(rs_dve.sem, rs_dve.upto(l, 1))
                pe_.wait_ge(rw_dve.sem, rw_dve.upto(l, rw_dve.per_layer))
                pe_.wait_ge(fill_sum.sem, fill_sum.upto(l, 48))
                heads(0, ft_of(Bt, TS), hd_of(AtP, TS), TS, TS)
                heads(1, ft_of(At, TS), hd_of(BtP, TS), TS, TS)
                heads(2, ft_of(Kt_, TS), hd_of(AtP, TS), TS, TS)
                heads(3, ft_of(Bt, TS), hd_of(RtP, TS), TS, TS)
                heads(4, ft_of(Kt_, TS), hd_of(RtP, TS), TS, TS)
                for ft in range(2):
                    nc.tensor.transpose(ps[0:TS, 5, ft * P:ft * P + P], Bp[:, ft, 0:TS], cmat(IDENT))
                    nc.tensor.transpose(ps[0:TS, 5, 256 + ft * P:256 + ft * P + P], Kp[:, ft, 0:TS],
                                        cmat(IDENT))
                for ft in range(2):
                    m = nc.tensor.transpose(ps[0:TS, 6, ft * P:ft * P + P], v_[:, ft, TP:T], cmat(IDENT))
                m.then_inc(rs_pe.sem, 1)
                pe_.wait_ge(rs_dve.sem, rs_dve.upto(l, 2))
                pe_.wait_ge(rs_act.sem, rs_act.upto(l, 1))
                settled(6)
                m = heads(0, hd_of(MA, TS, TS), hd_of(MB, TS, TS), TS, TS)

                def by_seq(b, rhs, first):
                    for h in range(NH):
                        ft, po = h // 2, HD * (h % 2)
                        for s in range(NSEQ):
                            m = mm(ps[po:po + HD, b, ft * TS + s * TD:ft * TS + s * TD + TD],
                                   lp[:, SWKV + (ft * NSEQ + s) * HD:SWKV + (ft * NSEQ + s) * HD + HD],
                                   rhs[:, h, s * TD:s * TD + TD], start=first and h < 2 and s == 0,
                                   stop=False, skip=True)
                    return m

                by_seq(1, AtP, True)
                for h in range(NH):
                    ft, po = h // 2, HD * (h % 2)
                    m = mm(ps[po:po + HD, 1, ft * TS:ft * TS + TS], vt[0:TS, h * HD:h * HD + HD],
                           LakT[0:TS, h, 0:TS], start=False, skip=True)
                m.then_inc(rs_pe.sem, 1)
                pe_.wait_ge(rs_dve.sem, rs_dve.upto(l, 3))
                settled(6)
                heads(0, hd_of(MD, TS, TS), hd_of(ME, TS, TS), TS, TS)
                for ft in range(2):
                    m = nc.tensor.transpose(ps[0:TS, 2, ft * P:ft * P + P], stmp[:, ft, 0:TS], cmat(IDENT))
                m.then_inc(rs_pe.sem, 1)
                pe_.wait_ge(rs_dve.sem, rs_dve.upto(l, 4))
                pe_.wait_ge(rs_act.sem, rs_act.upto(l, 2))
                settled(6)
                for h in range(NH):
                    m = mm(ps[0:TS, 1, h * HD:h * HD + HD], MF[0:TS, h, 0:TS], r0[0:TS, h * HD:h * HD + HD])
                m.then_inc(rs_pe.sem, 1)
                pe_.wait_ge(rs_act.sem, rs_act.upto(l, 3))
                by_seq(7, RtP, True)
                for h in range(NH):
                    ft, po = h // 2, HD * (h % 2)
                    o, c2 = ps[po:po + HD, 7, ft * TS:ft * TS + TS], slice(h * HD, h * HD + HD)
                    mm(o, sat[0:TS, c2], MrbT[0:TS, h, 0:TS], start=False, stop=False, skip=True)
                    m = mm(o, vt[0:TS, c2], MrkT[0:TS, h, 0:TS], start=False, skip=True)
                m.then_inc(rs_pe.sem, 1)
                for q in range(2):
                    pe_.wait_ge(rs_dve.sem, rs_dve.upto(l, 5 + q))
                    for h in range(NH):
                        ft, po = h // 2, HD * (h % 2)
                        lhs = (bptok, kptok)[q][0:TS, h * HD:h * HD + HD]
                        m = mm(ps[po:po + HD, 3 + ft, :], lhs, sam[0:TS, :, h * HD:h * HD + HD],
                               start=q == 0, stop=q == 1, skip=True)
                    m.then_inc(rs_pe.sem, 1)
                for n in range(2):
                    pe_.wait_ge(gn_dve.sem, gn_dve.upto(l, n + 1))
                    for ft in range(2):
                        m = tile(ft, cmat(BLK), 0, yb if n == 0 else e2, ft, 1)
                    m.then_inc(gn_pe.sem, 1)
                pe_.wait_ge(mix_done.sem, mix_done.upto(l, 1))
                settled(7)
                with pe_.Fori(0, 2) as g:
                    for q in range(4):
                        s, c = q // 2 * 2, q % 2
                        b = 2 * (q % 2)
                        if c == 0:
                            panel(l, "gate_b", g, s)
                            panel(l, "gate_b", g, s + 1)
                        pe_.wait_ge(merge_done.sem, merge_done.upto(l, q - 1 + g * 4))
                        tile(b, ring[:, s, :], c * P, u).then_inc(part.sem, 1)
                        tile(b + 1, ring[:, s + 1, :], c * P, y, 2, 2).then_inc(part.sem, 1)
                pe_.wait_ge(merge_done.sem, merge_done.upto(l, 8))
                for s in range(4):
                    panel(l, "out", 0, s)
                    for c in range(2):
                        pe_.wait_ge(x_done.sem, x_done.upto(l, 8 + 2 * s + c - 1))
                        tile(c, ring[:, s, :], c * P, merged).then_inc(part.sem, 1)
                ffn(l, 1)

        @block.scalar
        def _(act):
            own = [0]

            def link(layer, ins):
                own[0] += 1
                ins.then_inc(act_own.sem, 1)
                act.wait_ge(act_own.sem, act_own.upto(layer, own[0]))

            def f(out, in_, func, **kw):
                return nc.scalar.activation(out, in_, func, **kw)

            def norm(l, n):
                for k in range(KT):
                    act.wait_ge(x_done.sem, x_done.upto(l, 8 * n - 7 + k if n else 0))
                    if k >= 2:
                        act.wait_ge(sum_done.sem, sum_done.upto(l, 8 * n + k - 1))
                    f(sq[:, k % 2, :], x[:, k, :], ACT.Square).then_inc(sq_done.sem, 1)
                act.wait_ge(sum_done.sem, sum_done.upto(l, 8 * n + 8))
                link(l, f(halves(rs[:, :]), pair(3), ACT.Ln, scale=1.0 / D_MODEL, bias=cst[:, BIAS:BIAS + 1]))
                f(rs[:, :], rs[:, :], ACT.Exp, scale=-0.5).then_inc(rt_done.sem, 1)
                for k in range(KT):
                    act.wait_ge(un_done.sem, un_done.upto(l, 8 * n + k + 1))
                    f(u[:, k, 0:TP], u[:, k, 0:TP], ACT.Identity, scale=mod_a[:, 8 * n + k, 0:1],
                      bias=mod[:, 24 * n + k, 0:1]).then_inc(up_done.sem, 1)

            def ffn(l, n):
                norm(l, 2 * n)

                def units(it, first, k):
                    per = 3 if n == 0 else 2
                    for j in range(k):
                        act.wait_ge(part.sem, part.upto(l, PART0[f"up{n}"] + per * (first + j) + 1
                                                        + it * (4 * per)))
                        f(halves(gt[:, j % 2, :]), pair(2 * (j % 2)), ACT.Silu).then_inc(silu_done.sem, 1)

                with act.Fori(0, FT // 4) as it:
                    units(it, 0, 4)
                units(0, FT // 4 * 4, FT % 4)

            act.wait_ge(start_loaded.sem, 48)
            f(csil[:, :, :], csil[:, :, :], ACT.Silu).then_inc(csil_done.sem, 1)
            with act.Fori(0, DEPTH) as l:
                own[0] = 0
                ffn(l, 0)
                norm(l, 1)
                for j in range(11):
                    for c in range(1 if j < NBOTH else 2):
                        act.wait_ge(part.sem, part.upto(l, PART0["in"] + in_place(j)[1] + c + 1))
                        f(halves(proj[:, 2 * IN_ORDER[j] + c, :]), pair((2 * j + c) % 4), ACT.Copy)\
                            .then_inc(in_act.sem, 1)
                    if j == 3:
                        act.wait_ge(in_act.sem, in_act.upto(l, 2))
                        act.wait_ge(in_dve.sem, in_dve.upto(l, 2))
                        f(sqk[:, :, :], proj[:, P_Q:P_Q + 4, :], ACT.Square).then_inc(qk_sq.sem, 1)
                act.wait_ge(qk_sum.sem, qk_sum.upto(l, 1))
                for i in range(4):
                    a, b = (1.0, BIAS + 1) if i < 2 else (1.0 / HD, BIAS)
                    m = f(halves(sqk[:, i, :]), pair(i), ACT.Ln, scale=a, bias=cst[:, b:b + 1])
                m.then_inc(qk_ms.sem, 1)
                act.wait_ge(qk_ms.sem, qk_ms.upto(l, 1))
                f(sqk[:, :, :], sqk[:, :, :], ACT.Exp, scale=-0.5).then_inc(qk_rt.sem, 1)
                act.wait_ge(pool_pe.sem, pool_pe.upto(l, 1))
                for ft in range(2):
                    m = f(halves(y[:, 4 + ft, :]), pair(2 + ft), ACT.Identity, scale=col(PSC + ft))
                m.then_inc(pool_out.sem, 1)
                act.wait_ge(so_ready.sem, so_ready.upto(l, 3))
                act.dma_start(o_conv[l], so_conv).then_inc(stored.sem, 16)
                act.dma_start(o_pool[l], so_pool).then_inc(stored.sem, 16)
                act.dma_start(o_shift[l], so_shift).then_inc(stored.sem, 16)
                act.wait_ge(vt_pe.sem, vt_pe.upto(l, 1))
                f(vtok[:, 0:4, :], ps[:, 0:2, :], ACT.Copy)
                f(vtok[0:TS, 4, :], ps[0:TS, 2, 0:256], ACT.Copy).then_inc(vt_act.sem, 1)
                act.wait_ge(kn_ready.sem, kn_ready.upto(l, 1))
                act.dma_start(o_k[l], proj[:, P_K:P_K + 2, :]).then_inc(kv_stored.sem, 16)
                act.dma_start(o_v[l], proj[:, P_V:P_V + 2, :]).then_inc(kv_stored.sem, 16)

                def log1p_exp(a, b, ready):
                    link(l, f(b, a, ACT.Abs))
                    link(l, f(b, b, ACT.Exp, scale=-1.0))
                    return f(b, b, ACT.Ln, bias=1.0)

                def fill_sigmoid(stage, f, it=0):
                    sig = sig_ac if stage == "gate_ac" else sig_d
                    act.wait_ge(part.sem, part.upto(l, PART0[stage] + 2 * f + 1 + it * 8))
                    f_ = nc.scalar.activation(sig[:, f % 2, :], ps[:, 4, 0:HALF], ACT.Sigmoid)
                    f_.then_inc(fill_gate.sem, 1)

                for h in range(NH):
                    act.wait_ge(at_dve.sem, at_dve.upto(l, 3 * h + 1))
                    log1p_exp(zb[:, :], sa[:, :], None).then_inc(at_act.sem, 1)
                    if h:
                        fill_sigmoid("gate_ac", 3 * h - 2)
                        fill_sigmoid("gate_ac", 3 * h - 1)
                    act.wait_ge(at_dve.sem, at_dve.upto(l, 3 * h + 3))
                    f(sa[:, :], sa[:, :], ACT.Exp).then_inc(at_act.sem, 1)
                    fill_sigmoid("gate_ac", 3 * h)
                    act.wait_ge(at_pe.sem, at_pe.upto(l, 3 * h + 4 if h < NH - 1 else 3 * NH))
                    po = HD * (h % 2)
                    f(y[po:po + HD, 6 + h // 2, 0:TP], ps[po:po + HD, 3, :], ACT.Copy).then_inc(at_act.sem, 1)
                act.wait_ge(de_dve.sem, de_dve.upto(l, 1))
                log1p_exp(zb[:, 0:1024], sa[:, 0:1024], None)
                log1p_exp(zbn[0:TS, :], tn[0:TS, :], None).then_inc(de_act.sem, 1)
                for n in range(10, 14):
                    fill_sigmoid("gate_ac", n)
                act.wait_ge(de_dve.sem, de_dve.upto(l, 3))
                f(sa[:, 0:1024], sa[:, 0:1024], ACT.Exp)
                f(tn[0:TS, :], tn[0:TS, :], ACT.Exp).then_inc(de_act.sem, 1)
                for n in range(14, 32):
                    fill_sigmoid("gate_ac", n)

                act.wait_ge(rp_dve.sem, rp_dve.upto(l, 1))
                f(xt2[0:64, 0, :], xt2[0:64, 0, :], ACT.Tanh).then_inc(rp_act.sem, 1)
                f(xt2[:, 1, :], xt2[:, 1, :], ACT.Sigmoid).then_inc(rp_act.sem, 1)
                act.wait_ge(rp_pe.sem, rp_pe.upto(l, 1))
                for ft in range(2):
                    m = f(halves(e1[:, ft, :]), pair(ft), ACT.Sigmoid, bias=col(W0 + ft))
                m.then_inc(rp_act.sem, 1)
                for ft in range(2):
                    m = f(halves(bv[:, ft, :]), pair(2 + ft), ACT.Sigmoid, bias=col(A0 + ft))
                m.then_inc(rp_act.sem, 1)
                act.wait_ge(rp_pe.sem, rp_pe.upto(l, 2))
                for ft in range(2):
                    m = f(halves(gg[:, ft, :]), pair(ft), ACT.Copy)
                m.then_inc(rp_act.sem, 1)
                act.wait_ge(rp_dve.sem, rp_dve.upto(l, 3))
                link(l, f(xt2[:, :, :], xt2[:, :, :], ACT.Ln))
                f(xt2[:, :, :], xt2[:, :, :], ACT.Exp, scale=-0.5).then_inc(rp_act.sem, 1)
                act.wait_ge(rp_dve.sem, rp_dve.upto(l, 5))
                f(e2, e2, ACT.Exp)
                f(e1, e3, ACT.Exp)
                f(e3, e3, ACT.Exp, scale=-1.0).then_inc(rp_act.sem, 1)
                with act.Fori(0, NTT) as tt:
                    def tile_pe(n):
                        return rw_pe.upto(l, n + tt * RW_PE)

                    def flat(v):
                        return v.rearrange("p h n -> p (h n)")

                    act.wait_ge(rw_pe.sem, tile_pe(2))
                    f(turned, ps[:, 7, :], ACT.Copy)
                    f(vt, ps[:, 6, 0:256], ACT.Copy).then_inc(rw_act.sem, 1)
                    act.wait_ge(rw_pe.sem, tile_pe(3))
                    f(flat(MD), ps[:, 1, :], ACT.Copy).then_inc(rw_act.sem, 1)
                    act.wait_ge(rw_pe.sem, tile_pe(4))
                    f(flat(MA), ps[:, 1, :], ACT.Copy)
                    f(flat(MB), ps[:, 7, :], ACT.Copy).then_inc(rw_act.sem, 1)
                    act.wait_ge(rw_pe.sem, tile_pe(5))
                    f(flat(MC), ps[:, 1, :], ACT.Copy).then_inc(rw_act.sem, 1)
                    fill_sigmoid("gate_d", 0, tt)
                    for q in range(2):
                        act.wait_ge(rw_pe.sem, tile_pe(7 + 2 * q))
                        f(flat(MA), ps[:, 0, :], ACT.Copy)
                        f(flat(MB), ps[:, 1, :], ACT.Copy).then_inc(rw_act.sem, 1)
                    fill_sigmoid("gate_d", 1, tt)
                    for c in range(2):
                        rows = slice(CH * c, CH * c + CH)
                        act.wait_ge(rw_pe.sem, tile_pe(11 + 3 * c))
                        f(r0[rows, :], ps[rows, 0, 0:256], ACT.Copy).then_inc(rw_act.sem, 1)
                        fill_sigmoid("gate_d", 2 + c, tt)
                act.wait_ge(rs_pe.sem, rs_pe.upto(l, 1))
                f(turned[0:TS, :], ps[0:TS, 5, :], ACT.Copy)
                f(vt[0:TS, :], ps[0:TS, 6, 0:256], ACT.Copy).then_inc(rs_act.sem, 1)
                act.wait_ge(rs_pe.sem, rs_pe.upto(l, 3))
                f(r0[0:TS, :], ps[0:TS, 2, 0:256], ACT.Copy).then_inc(rs_act.sem, 1)
                act.wait_ge(rs_pe.sem, rs_pe.upto(l, 4))
                f(sat[0:TS, :], ps[0:TS, 1, 0:256], ACT.Copy).then_inc(rs_act.sem, 1)
                act.wait_ge(gn_pe.sem, gn_pe.upto(l, 2))
                for ft in range(2):
                    m = f(halves(e2[:, ft, :]), pair(ft), ACT.Ln, scale=1.0 / HD, bias=cst[:, BIAS + 2:BIAS + 3])
                link(l, m)
                f(e2, e2, ACT.Exp, scale=-0.5).then_inc(gn_act.sem, 1)
                act.wait_ge(wkv_ready.sem, wkv_ready.upto(l, 1))
                act.dma_start(o_wkv[l, :, :, 1:9, :], lp[:, SWKV:SWKV + 2 * NSEQ * HD].rearrange(
                    "p (f s i) -> p f s i", f=2, s=NSEQ)).then_inc(wkv_stored.sem, 16)
                for q in range(2):
                    rows = slice(HD * q, HD * q + HD)
                    act.dma_start(o_wkv[l, rows, :, 0, :], sbd[rows, :, rows])\
                        .then_inc(wkv_stored.sem, 16)
                with act.Fori(0, 2) as g:
                    for q in range(4):
                        act.wait_ge(part.sem, part.upto(l, PART0["gate_b"] + 2 * q + 1 + g * 8))
                        f(halves(gt[:, q % 2, :]), pair(2 * (q % 2)), ACT.Sigmoid).then_inc(gate_done.sem, 1)
                ffn(l, 1)
                assert own[0] == ACT_LINKS, ("ACT_LINKS", own[0])

        @block.vector
        def _(dve):
            V = nc.vector
            own = [0]

            def link(layer, ins):
                own[0] = own[0] + 1
                ins.then_inc(vec.sem, 1)
                dve.wait_ge(vec.sem, vec.upto(layer, own[0]))

            def tt_(out, a, b, op):
                return V.tensor_tensor(out, a, b, op)

            def stt(out, a, s, b, op0, op1):
                return V.scalar_tensor_tensor(out=out, in0=a, scalar=s, in1=b, op0=op0, op1=op1)

            def ts(out, a, s1, op0, s2=None, op1=ALU.bypass):
                return V.tensor_scalar(out, a, s1, s2, op0, op1)

            MUL, ADD, SUB, MAX = ALU.mult, ALU.add, ALU.subtract, ALU.max

            def norm(l, n):
                dve.wait_ge(rt_done.sem, rt_done.upto(l, n + 1))
                for k in range(KT):
                    tt_(u[:, k, :], x[:, k, :], rs[:, :], MUL).then_inc(un_done.sem, 1)
                dve.wait_ge(un_done.sem, un_done.upto(l, 8 * n + 8))
                us = u[:, :, TP:T].rearrange("p k (s t) -> p k s t", s=NSEQ)

                def by_seq(v):
                    return v.unsqueeze(3).to_broadcast([P, KT, NSEQ, TD])

                link(l, tt_(us, us, by_seq(mod_a[:, 8 * n:8 * n + 8, 1:9]), MUL))
                tt_(us, us, by_seq(mod[:, 24 * n:24 * n + 8, 1:9]), ADD).then_inc(us_done.sem, 1)

            def residual(l, m, b, gate):
                g = gate + m
                stt(x[:, m, 0:HALF], ps[:, 2 * b, 0:HALF], mod[:, g, 0:1], x[:, m, 0:HALF], MUL, ADD)
                stt(x[:, m, HALF:TP], ps[:, 2 * b + 1, 0:TP - HALF], mod[:, g, 0:1], x[:, m, HALF:TP], MUL, ADD)
                room = ptmp[:, m * TS:m * TS + TS]
                link(l, tt_(seqs(room), seqs(ps[:, 2 * b + 1, TP - HALF:HALF]),
                            over(mod[:, g, 1:9], TD), MUL))
                tt_(x[:, m, TP:T], x[:, m, TP:T], room, ADD).then_inc(x_done.sem, 1)

            def keep_modulation(l, p, n, bank, it=0, step=0):
                dve.wait_ge(part.sem, part.upto(l, p + it * (3 * step if p > PART0["up0"] else step)))
                t0 = bass.ds(it * (2 * step) + 2 * n, 2)
                tt_(mod[:, t0, :], ps[:, bank, MODC:MODC + 18].rearrange("p (a n) -> p a n", a=2),
                    over(lp[:, bass.ds(it * (2 * step) + (ADAB + 2 * n), 2)], 9), ADD).then_inc(mod_done.sem, 1)

            def modulation_factors(l, panels, norms, gates):
                dve.wait_ge(mod_done.sem, mod_done.upto(l, panels))
                for n in norms:
                    m = stt(mod_a[:, 8 * n:8 * n + 8, :], mod[:, 24 * n + 8:24 * n + 16, :], 1.0,
                            over(lp[:, NG + 8 * n:NG + 8 * n + 8], 9), ADD, MUL)
                for g in gates:
                    m = ts(mod[:, g:g + 8, :], mod[:, g:g + 8, :], 0.5, MUL)
                link(l, m)

            def ffn(l, n):
                norm(l, 2 * n)

                per = 3 if n == 0 else 2

                def units(it, first, k):
                    for j in range(k):
                        q = first + j
                        dve.wait_ge(part.sem, part.upto(l, PART0[f"up{n}"] + per * q + 2 + it * (4 * per)))
                        dve.wait_ge(silu_done.sem, silu_done.upto(l, n * FT + q + 1 + it * 4))
                        tt_(halves(hid[:, q + it * 4, :]), halves(gt[:, j % 2, :]), pair(2 * (j % 2) + 1), MUL)\
                            .then_inc(h_done.sem, 1)
                        if n == 0:
                            keep_modulation(l, PART0["up0"] + 3 * q + 3, ADA_FIRST + q, next_bank(q), it, 4)

                settled()
                with dve.Fori(0, FT // 4) as it:
                    units(it, 0, 4)
                units(0, FT // 4 * 4, FT % 4)
                if n == 0:
                    modulation_factors(l, ADA_FIRST + FT, (1,), (16,))
                for m in range(KT):
                    dve.wait_ge(part.sem, part.upto(l, PART0[f"down{n}"] + 2 * m + 2))
                    residual(l, m, m % 2, 16 if n == 0 else 64)

            def conv(l):
                b_, c_, xv = proj[:, 0:2, :], proj[:, 2:4, :], proj[:, 4:6, :]

                def smp(v):
                    return v[:, :, TP:T].rearrange("p f (s t) -> p f s t", s=NSEQ)

                V.memset(zc[:, :, 0:2], 0.0)
                V.tensor_copy(zs[:, :, :, 0:2], lp[:, SCONV:SCONV + 32].rearrange("p (f s t) -> p f s t",
                                                                                   f=2, s=NSEQ))
                tt_(zc[:, :, 2:TP + 2], c_[:, :, 0:TP], xv[:, :, 0:TP], MUL)
                link(l, tt_(zs[:, :, :, 2:6], smp(c_), smp(xv), MUL))
                V.tensor_copy(so_conv[:, :, 0:2], zc[:, :, TP:TP + 2])
                V.tensor_copy(so_conv[:, :, 2:18].rearrange("p f (s t) -> p f s t", s=NSEQ),
                              zs[:, :, :, 4:6]).then_inc(so_ready.sem, 1)
                for tap in range(3):
                    for ft in range(2):
                        w = col(CW + 2 * tap + ft)
                        yp, ys = y[:, ft, 0:TP], seqs(y[:, ft, TP:T])
                        zp_, zs_ = zc[:, ft, tap:tap + TP], zs[:, ft, :, tap:tap + TD]
                        if tap == 0:
                            ts(yp, zp_, w, MUL)
                            m = ts(ys, zs_, w, MUL)
                        else:
                            stt(yp, zp_, w, yp, MUL, ADD)
                            m = stt(ys, zs_, w, ys, MUL, ADD)
                    link(l, m)
                tt_(y[:, 0:2, :], y[:, 0:2, :], b_, MUL)

            def pooling(l):
                z = proj[:, P_POOL:P_POOL + 2, :]
                V.memset(pe[:, :, 0:CTX], 0.0)
                V.tensor_copy(pe[:, :, CTX:], z[:, :, 0:TP])
                V.tensor_copy(pes[:, :, :, 0:CTX], lp[:, SPOOL:SPOOL + 2 * NSEQ * CTX].rearrange(
                    "p (f s t) -> p f s t", f=2, s=NSEQ))
                link(l, V.tensor_copy(pes[:, :, :, CTX:], z[:, :, TP:T].rearrange("p f (s t) -> p f s t",
                                                                                  s=NSEQ)))
                V.tensor_copy(so_pool[:, :, 0:CTX], pe[:, :, TP:TP + CTX])
                V.tensor_copy(so_pool[:, :, CTX:].rearrange("p f (s t) -> p f s t", s=NSEQ),
                              pes[:, :, :, TD:TD + CTX]).then_inc(so_ready.sem, 1)
                s2, s4 = y[:, 2:4, :], y[:, 6:8, :]
                s8, s16 = proj[:, 2, :], proj[:, 3, :]
                tt_(s2[:, :, 0:526], pe[:, :, 0:526], pe[:, :, 1:527], ADD)
                link(l, tt_(s2s[:, :, :, :], pes[:, :, :, 0:18], pes[:, :, :, 1:19], ADD))
                tt_(s4[:, :, 0:524], s2[:, :, 0:524], s2[:, :, 2:526], ADD)
                link(l, tt_(s4s[:, :, :, :], s2s[:, :, :, 0:16], s2s[:, :, :, 2:18], ADD))
                tt_(s8[:, 0:520], s4[:, 1, 0:520], s4[:, 1, 4:524], ADD)
                link(l, tt_(s8s[:, :, :, :], s4s[:, :, :, 0:12], s4s[:, :, :, 4:16], ADD))
                tt_(s16[:, 0:512], s8[:, 0:512], s8[:, 8:520], ADD)
                link(l, tt_(s16s[:, :, :, :], s8s[:, :, :, 0:4], s8s[:, :, :, 8:12], ADD))
                groups = ((0, 0, s2[:, 0, 14:526], s2s[:, 0, :, 14:18], 2), (0, 64, s4[:, 0, 12:524],
                          s4s[:, 0, :, 12:16], 4), (1, 0, s8[:, 8:520], s8s[:, 1, :, 8:12], 8),
                          (1, 64, s16[:, 0:512], s16s[:, 1, :, 0:4], 16))
                for ft, po, sp_, ss_, w in groups:
                    r = slice(po, po + 64)
                    tt_(fix[r, ft, :], sp_[r, 0:16], cst[r, INVC + 16 * ft:INVC + 16 * ft + 16], MUL)
                    stt(pd[r, ft, 16:TP], sp_[r, 16:TP], 1.0 / w, pe[r, ft, CTX + 16:CTX + TP], MUL, SUB)
                    m = stt(seqs(pd[:, ft, TP:T])[r], ss_[r], 1.0 / w, pes[r, ft, :, CTX:CTX + TD], MUL, SUB)
                link(l, m)
                tt_(pd[:, :, 0:16], fix[:, :, :], pe[:, :, CTX:CTX + 16], SUB).then_inc(pool_in.sem, 1)

            def qk_norm(l):
                dve.wait_ge(qk_rt.sem, qk_rt.upto(l, 1))
                k, q = proj[:, P_K:P_K + 2, :], proj[:, P_Q:P_Q + 2, :]
                stt(k, k, col(KN), sqk[:, 2:4, :], MUL, MUL).then_inc(kn_ready.sem, 1)
                link(l, stt(q, q, col(QN), sqk[:, 0:2, :], MUL, MUL))
                V.memset(spn[:, :], 0.0)
                link(l, V.memset(qp[:, :, :, :], 0.0))
                for r, c in ((slice(0, 64), 0), (slice(64, 128), TD)):
                    m = V.tensor_copy(qp[r, :, :, c:c + TD],
                                      q[r, :, TP:T].rearrange("p f (s t) -> p f s t", s=NSEQ))
                m.then_inc(qp_done.sem, 1)

            def bank_run(b):
                return ps[:, b:b + 3, :].rearrange("p b n -> p (b n)")[:, 0:NZ]

            def fill_merge(l, stage, f, it=0, link=link):
                first, step = (0, 0) if stage == "gate_ac" else (32, 4)
                sig, prod = (sig_ac, prod_ac) if stage == "gate_ac" else (sig_d, prod_d)
                m, hf = f // 2 % KT, f % 2
                dst = merged[:, m + it * 2, hf * HALF:hf * HALF + HALF]
                dve.wait_ge(part.sem, part.upto(l, PART0[stage] + 2 * f + 2 + it * 8))
                dve.wait_ge(fill_gate.sem, fill_gate.upto(l, first + f + 1 + it * step))
                o = dst if stage == "gate_ac" and f < 16 else prod
                ins = tt_(o, sig[:, f % 2, :], ps[:, 5, 0:HALF], MUL)
                if o is prod:
                    link(l, ins)
                    ins = tt_(dst, dst, prod, ADD)
                ins.then_inc(fill_sum.sem, 1)

            def attention(l):
                for h in range(NH):
                    dve.wait_ge(at_pe.sem, at_pe.upto(l, 3 * h if h else 1))
                    if h:
                        dve.wait_ge(at_dve.sem, at_dve.upto(l, 3 * h))
                    ts(zb[:, :], bank_run(0), col(SBB + h), ADD).then_inc(at_dve.sem, 1)
                    if h:
                        fill_merge(l, "gate_ac", 3 * h - 3)
                    dve.wait_ge(at_act.sem, at_act.upto(l, 3 * h + 1))
                    link(l, stt(sp[:, :], zb[:, :], 0.0, sa[:, :], MAX, ADD))
                    for kt in range(NTT):
                        d = sp[:, OFF[kt]:OFF[kt] + P]
                        m = tt_(d, d, cst[:, CAUS:CAUS + P], MUL)
                    m.then_inc(at_dve.sem, 1)
                    if h:
                        fill_merge(l, "gate_ac", 3 * h - 2)
                        fill_merge(l, "gate_ac", 3 * h - 1)
                    dve.wait_ge(at_pe.sem, at_pe.upto(l, 3 * h + 2))
                    link(l, tt_(sa[:, :], zb[:, :], bank_run(0), SUB))
                    for kt in range(NTT):
                        d = sa[:, OFF[kt]:OFF[kt] + P]
                        m = tt_(d, d, cst[:, CNEG:CNEG + P], ADD)
                    m.then_inc(at_dve.sem, 1)
                fill_merge(l, "gate_ac", 9)

            def sample_attention(l):
                dve.wait_ge(de_pe.sem, de_pe.upto(l, 1))
                dve.wait_ge(cache_used.sem, cache_used.upto(l, 16))
                bias = lp[:, SBB:SBB + NH]
                for b in range(2):
                    for pg in range(4):
                        c = slice((4 * b + pg) * P, (4 * b + pg) * P + P)
                        tt_(zb[:, c].rearrange("p (h q) -> p h q", h=NH),
                            ps[:, 6 + b, pg * P:pg * P + P].rearrange("p (h q) -> p h q", h=NH),
                            over(bias, TS), ADD)
                tt_(zbn[0:TS, :].rearrange("p (h q) -> p h q", h=NH),
                    ps[0:TS, 1, 0:P].rearrange("p (h q) -> p h q", h=NH),
                    over(bias[0:TS], TS), ADD).then_inc(de_dve.sem, 1)
                dve.wait_ge(de_act.sem, de_act.upto(l, 1))
                stt(sp[:, 0:1024], zb[:, 0:1024], 0.0, sa[:, 0:1024], MAX, ADD)
                link(l, stt(spn[0:TS, :], zbn[0:TS, :], 0.0, tn[0:TS, :], MAX, ADD))

                def new(v):
                    return v[0:TS, :].rearrange("p (h q) -> p h q", h=NH)

                tt_(new(spn), new(spn), across(cst[0:TS, S4U:S4U + TS], NH), MUL)
                link(l, V.tensor_copy(rd[:, 6, :], sp[:, 7 * P:8 * P]))
                for pg in range(5, -1, -1):
                    m = tt_(rd[:, pg, :], rd[:, pg + 1, :], sp[:, (pg + 1) * P:(pg + 2) * P], ADD)
                    if pg:
                        link(l, m)
                m.then_inc(de_dve.sem, 1)
                for n in range(10, 14):
                    fill_merge(l, "gate_ac", n)
                dve.wait_ge(de_pe.sem, de_pe.upto(l, 2))
                tt_(sa[:, 0:1024], zb[:, 0:1024], ps[:, 2:4, :].rearrange("p b n -> p (b n)"), SUB)
                link(l, tt_(tn[0:TS, :], zbn[0:TS, :], ps[0:TS, 0, 0:P], SUB))
                tt_(new(tn), new(tn), across(cst[0:TS, NEG4:NEG4 + TS], NH), ADD).then_inc(de_dve.sem, 1)
                for n in range(14, 32):
                    fill_merge(l, "gate_ac", n)
                dve.wait_ge(cache_used.sem, cache_used.upto(l, 32))
                for q in range(2):
                    r = slice(64 * q, 64 * q + 64)
                    m = V.tensor_copy(y[r, 6:8, TP:T],
                                      ps[r, 1, 0:P].rearrange("p (f h q) -> p f h q", f=2, h=2)[:, :, q, :])
                m.then_inc(de_dve.sem, 1)

            def rwkv_pre(l):
                pr = proj[:, P_RWKV:P_RWKV + 8, :]
                dve.wait_ge(kv_stored.sem, kv_stored.upto(l, 2))
                for a, b, xs in ((0, 2, r_), (2, 8, proj[:, P_Q:P_Q + 6, :])):
                    pv = pr[:, a:b, :]
                    prs, xss = (v[:, :, TP:T].rearrange("p f (s t) -> p f s t", s=NSEQ) for v in (pv, xs))
                    tt_(xs[:, :, 1:TP], pv[:, :, 0:TP - 1], pv[:, :, 1:TP], SUB)
                    ts(xs[:, :, 0:1], pv[:, :, 0:1], -1.0, MUL)
                    tt_(xss[:, :, :, 1:TD], prs[:, :, :, 0:TD - 1], prs[:, :, :, 1:TD], SUB)
                    link(l, tt_(xss[:, :, :, 0], lp[:, SSHIFT + NSEQ * a:SSHIFT + NSEQ * b].rearrange(
                        "p (f s) -> p f s", f=b - a), prs[:, :, :, 0], SUB))
                    for j in range(a, b):
                        m = stt(xs[:, j - a, :], xs[:, j - a, :], col(MU + j), pr[:, j, :], MUL, ADD)
                m.then_inc(rp_dve.sem, 1)
                dve.wait_ge(rp_dve.sem, rp_dve.upto(l, 1))
                for ft in range(2):
                    m = ts(kkv[:, ft, :], k_[:, ft, :], col(KK_ + ft), MUL)
                link(l, m)
                tt_(bon, kkv, kkv, MUL).then_inc(rp_dve.sem, 1)
                dve.wait_ge(rp_pe.sem, rp_pe.upto(l, 2))
                for ft in range(2):
                    m = ts(halves(xt2[:, ft, :]), pair(2 + ft), 1e-24, MAX)
                m.then_inc(rp_dve.sem, 1)
                dve.wait_ge(rp_act.sem, rp_act.upto(l, 6))
                tt_(kkv, kkv, xt2, MUL)
                for ft in range(2):
                    m = ts(e2[:, ft, :], bv[:, ft, :], -1.0, ADD, col(KA + ft), MUL)
                link(l, m)
                tt_(bv, kkv, bv, MUL)
                link(l, stt(k_, e2, 1.0, k_, ADD, MUL))
                for ft in range(2):
                    m = stt(bon[:, ft, :], r_[:, ft, :], col(RK + ft), k_[:, ft, :], MUL, MUL)
                m.then_inc(rp_dve.sem, 1)
                link(l, ts(e1, e1, -float(np.exp(-0.5)), MUL))
                for ft in range(2):
                    m = V.tensor_tensor_scan(e3[:, ft, :], cst[:, SCANM:SCANM + T], e1[:, ft, :], 0.0, MUL, ADD)
                link(l, m)
                tt_(e2, e3, e1, SUB).then_inc(rp_dve.sem, 1)
                dve.wait_ge(rp_pe.sem, rp_pe.upto(l, 3))
                for ft in range(2):
                    m = tt_(halves(bon[:, ft, :]), pair(2 + ft), halves(v_[:, ft, :]), MUL)
                m.then_inc(rp_dve.sem, 1)
                dve.wait_ge(rp_act.sem, rp_act.upto(l, 7))
                dve.wait_ge(wkv_stored.sem, wkv_stored.upto(l, 0))
                for v in (AtP, RtP, BtP):
                    V.memset(v[:, :, :], 0.0)
                link(l, V.memset(sbd[:, :, :], 0.0))

            def scaled(l, c, n, ends, split):
                V.tensor_copy(*ends)
                stt(At[:, :, 0:n], kkv[:, :, c], -1.0, e2[:, :, c], MUL, MUL)
                tt_(Rt[:, :, 0:n], r_[:, :, c], e1[:, :, c], MUL)
                tt_(Bt[:, :, 0:n], bv[:, :, c], e3[:, :, c], MUL)
                link(l, tt_(Kt_[:, :, 0:n], k_[:, :, c], e3[:, :, c], MUL))
                e, k = ends[0], split
                for o, i in ((Bp, Bt), (Kp, Kt_)):
                    tt_(o[:, :, 0:n].rearrange("p f (c n) -> p f c n", c=k),
                        i[:, :, 0:n].rearrange("p f (c n) -> p f c n", c=k),
                        e.unsqueeze(3).to_broadcast([P, 2, k, n // k]), MUL)
                for o, i in ((AtP, At), (RtP, Rt), (BtP, Bt)):
                    o = o.rearrange("p (f q) n -> p f q n", f=2)
                    for q in range(2):
                        r = slice(64 * q, 64 * q + 64)
                        m = V.tensor_copy(o[r, :, q, 0:n], i[r, :, 0:n])
                return m

            def flat(v):
                return v.rearrange("p h n -> p (h n)")

            def bank(b):
                return ps[:, b, :].rearrange("p (h n) -> p h n", h=NH)

            def rwkv_tiles(l):
                first = own[0]
                settled()
                with dve.Fori(0, NTT) as tt:
                    own[0] = first + tt * RW_LINKS
                    count = 0

                    def tlink(layer, ins):
                        nonlocal count
                        count += 1
                        link(layer, ins)

                    def tile_pe(n):
                        dve.wait_ge(rw_pe.sem, rw_pe.upto(l, n + tt * RW_PE))

                    def tile_act(n):
                        dve.wait_ge(rw_act.sem, rw_act.upto(l, n + tt * RW_ACT))

                    def masked(o, b, at):
                        return tt_(o, bank(b), across(cst[:, at:at + P], NH), MUL)

                    c = bass.ds(tt * P, P)
                    V.tensor_copy(stmp[:, :, :], v_[:, :, c])
                    ends = e1[:, :, c].rearrange("p f (c n) -> p f c n", c=2)[:, :, :, CH - 1]
                    scaled(l, c, P, (pend, ends), 2).then_inc(rw_dve.sem, 1)
                    count += 1
                    tile_pe(1)
                    masked(MA, 0, M16U)
                    masked(MB, 1, M16L)
                    masked(ET32, 1, E32L)
                    masked(E64, 1, E64L).then_inc(rw_dve.sem, 1)
                    dve.wait_ge(rw_dve.sem, rw_dve.upto(l, 2 + tt * RW_DVE))
                    tt_(ME, MA, across(cst[:, IDENT:IDENT + P], NH), ADD)
                    tile_pe(3)
                    V.tensor_copy(flat(MC), ps[:, 0, :]).then_inc(rw_dve.sem, 1)
                    masked(LakT, 2, SU64)
                    masked(MrbT, 3, LE64)
                    tile_pe(4)
                    tt_(flat(MF), flat(ME), ps[:, 0, :], ADD).then_inc(rw_dve.sem, 1)
                    tile_pe(5)
                    dve.wait_ge(rw_dve.sem, rw_dve.upto(l, 4 + tt * RW_DVE))
                    tt_(flat(ME), flat(MF), ps[:, 0, :], ADD).then_inc(rw_dve.sem, 1)
                    masked(MrkT, 3, LE64)
                    fill_merge(l, "gate_d", 0, tt, tlink)
                    tile_pe(6)
                    dve.wait_ge(rw_dve.sem, rw_dve.upto(l, 5 + tt * RW_DVE))
                    tt_(flat(MF), flat(ME), ps[:, 0, :], ADD).then_inc(rw_dve.sem, 1)
                    tile_pe(8)
                    dve.wait_ge(rw_dve.sem, rw_dve.upto(l, 6 + tt * RW_DVE))
                    tt_(flat(ME), flat(MF), ps[:, 7, :], ADD).then_inc(rw_dve.sem, 1)
                    tile_pe(10)
                    dve.wait_ge(rw_dve.sem, rw_dve.upto(l, 7 + tt * RW_DVE))
                    tt_(flat(MF), flat(ME), ps[:, 2, :], ADD).then_inc(rw_dve.sem, 1)
                    for ch in range(2):
                        rows = slice(CH * ch, CH * ch + CH)
                        tt_(stmp[:, :, :], sbd[:, :, :], over(pend[:, :, ch], P), MUL)
                        if ch == 0:
                            fill_merge(l, "gate_d", 1, tt, tlink)
                        tile_pe(12 + 3 * ch)
                        V.tensor_copy(sat[rows, :], ps[rows, 1, 0:256]).then_inc(rw_dve.sem, 1)
                        if ch == 0:
                            fill_merge(l, "gate_d", 2, tt, tlink)
                        tile_pe(13 + 3 * ch)
                        for q in range(2):
                            r = slice(64 * q, 64 * q + 64)
                            m = tt_(sbd[r, :, r], stmp[r, :, r],
                                    ps[r, 3, 0:256].rearrange("p (f n) -> p f n", f=2)[:, :, r], ADD)
                        m.then_inc(rw_dve.sem, 1)
                        dve.wait_ge(rw_dve.sem, rw_dve.upto(l, 10 + 2 * ch + tt * RW_DVE))
                    fill_merge(l, "gate_d", 3, tt, tlink)
                    tile_pe(17)
                    V.tensor_copy(yb[:, :, c], ps[:, 6, 256:512].rearrange("p (f n) -> p f n", f=2))\
                        .then_inc(rw_dve.sem, 1)
                    assert count == RW_LINKS, count
                own[0] = first + NTT * RW_LINKS

            def rwkv_sample(l):
                def small(v):
                    return v[0:TS, :, 0:TS]

                def sbank(b):
                    return ps[0:TS, b, 0:P].rearrange("p (h n) -> p h n", h=NH)

                def masked(o, b, at):
                    return tt_(small(o), sbank(b), across(cst[0:TS, at:at + TS], NH), MUL)

                ends = e1[:, :, TP:T].rearrange("p f (s t) -> p f s t", s=NSEQ)[:, :, :, TD - 1]
                scaled(l, slice(TP, T), TS, (pends, ends), NSEQ).then_inc(rs_dve.sem, 1)
                dve.wait_ge(rs_pe.sem, rs_pe.upto(l, 1))
                link(l, masked(MA, 0, S4U))
                masked(MB, 1, S4L)
                tt_(small(ME), small(MA), across(cst[0:TS, IDENT:IDENT + TS], NH), ADD)
                masked(LakT, 2, S4U)
                masked(MrbT, 3, LE4)
                masked(MrkT, 4, LE4).then_inc(rs_dve.sem, 1)
                dve.wait_ge(rs_pe.sem, rs_pe.upto(l, 2))
                V.tensor_copy(small(MD), sbank(0))
                V.tensor_copy(stmp[:, :, 0:TS], ps[:, 1, 0:2 * TS].rearrange("p (f n) -> p f n", f=2))\
                    .then_inc(rs_dve.sem, 1)
                dve.wait_ge(rs_pe.sem, rs_pe.upto(l, 3))
                tt_(small(MF), small(ME), sbank(0), ADD).then_inc(rs_dve.sem, 1)
                dve.wait_ge(rs_act.sem, rs_act.upto(l, 3))
                seqm = over(cst[0:TS, SEQM:SEQM + NSEQ], 256)
                tt_(sam[0:TS], across(sat[0:TS, :], NSEQ), seqm, MUL).then_inc(rs_dve.sem, 1)
                dve.wait_ge(rs_pe.sem, rs_pe.upto(l, 5))
                V.tensor_copy(yb[:, :, TP:T], ps[:, 7, 0:2 * TS].rearrange("p (f n) -> p f n", f=2))
                dve.wait_ge(rs_pe.sem, rs_pe.upto(l, 6))
                tt_(sam[0:TS], across(vt[0:TS, :], NSEQ), seqm, MUL).then_inc(rs_dve.sem, 1)
                st = lp[:, SWKV:SWKV + 2 * NSEQ * HD].rearrange("p (f s i) -> p f s i", f=2, s=NSEQ)
                link(l, tt_(st, st, pends.unsqueeze(3).to_broadcast([P, 2, NSEQ, HD]), MUL))
                dve.wait_ge(rs_pe.sem, rs_pe.upto(l, 7))
                tt_(st, st, ps[:, 3:5, :].rearrange("p f (s i) -> p f s i", s=NSEQ), ADD)\
                    .then_inc(wkv_ready.sem, 1)

            def group_norm(l):
                dve.wait_ge(wkv_ready.sem, wkv_ready.upto(l, 1))
                V.memset(pause_col(), 0.0).then_inc(gn_dve.sem, 1)
                dve.wait_ge(gn_pe.sem, gn_pe.upto(l, 1))
                for ft in range(2):
                    m = stt(halves(yb[:, ft, :]), pair(ft), -1.0 / HD, halves(yb[:, ft, :]), MUL, ADD)
                link(l, m)
                tt_(e2, yb, yb, MUL).then_inc(gn_dve.sem, 1)
                dve.wait_ge(gn_act.sem, gn_act.upto(l, 1))
                link(l, tt_(yb, yb, e2, MUL))
                for ft in range(2):
                    m = ts(yb[:, ft, :], yb[:, ft, :], col(LG + ft), MUL, col(LB + ft), ADD)
                link(l, m)
                link(l, tt_(yb, yb, bon, ADD))
                tt_(yb, yb, gg, MUL).then_inc(mix_done.sem, 1)
                V.memset(pause_col(), 0.0).then_inc(cache_used.sem, 4)

            V.memset(pause_col(), 0.0).then_inc(mod_done.sem, mod_done.credit)
            for sg in (h_done, x_done, in_act, in_dve, merge_done, fill_gate, fill_sum, cache_used, part, mix_done, stored, wkv_stored):
                V.memset(pause_col(), 0.0).then_inc(sg.sem, sg.credit)
            dve.wait_ge(start_loaded.sem, 48)
            with dve.Fori(0, DEPTH) as l:
                own[0] = 0
                dve.wait_ge(lp_loaded.sem, lp_loaded.upto(l, 1))
                settled()
                with dve.Fori(0, ADA_FIRST // R) as it:
                    for s in range(R):
                        keep_modulation(l, PART0["ada"] + s + 1, s, s, it, R)
                modulation_factors(l, ADA_FIRST, (0,), ())
                ffn(l, 0)
                norm(l, 1)
                for j in range(11):
                    if j < NBOTH:
                        dve.wait_ge(part.sem, part.upto(l, PART0["in"] + in_place(j)[1] + 2))
                        V.tensor_copy(halves(proj[:, 2 * IN_ORDER[j] + 1, :]), pair((2 * j + 1) % 4))\
                            .then_inc(in_dve.sem, 1)
                    if j < ADA_IN:
                        keep_modulation(l, PART0["in"] + in_place(j)[1] + 3, ADA_FIRST + FT + j, next_bank(j))
                dve.wait_ge(in_act.sem, in_act.upto(l, NBOTH))
                dve.wait_ge(in_dve.sem, in_dve.upto(l, NBOTH))
                modulation_factors(l, 36, (2,), (64,))
                dve.wait_ge(stored.sem, stored.upto(l, 0))
                conv(l)
                pooling(l)
                dve.wait_ge(in_act.sem, in_act.upto(l, in_act.per_layer))
                sh = proj[:, P_RWKV:P_RWKV + 8, :]
                V.tensor_copy(so_shift[:, :, 0:1], sh[:, :, TP - 1:TP])
                V.tensor_copy(so_shift[:, :, 1:9], sh[:, :, TP:T].rearrange(
                    "p f (s t) -> p f s t", s=NSEQ)[:, :, :, TD - 1]).then_inc(so_ready.sem, 1)
                qk_norm(l)
                attention(l)
                sample_attention(l)
                rwkv_pre(l)
                rwkv_tiles(l)
                rwkv_sample(l)
                group_norm(l)
                first = own[0]
                settled()
                with dve.Fori(0, 2) as g:
                    own[0] = first + g * 4
                    for q in range(4):
                        dve.wait_ge(part.sem, part.upto(l, PART0["gate_b"] + 2 * q + 2 + g * 8))
                        dve.wait_ge(gate_done.sem, gate_done.upto(l, q + 1 + g * 4))
                        mt = merged[:, q + g * 4, :]
                        dve.wait_ge(merge_done.sem, merge_done.upto(l, q + g * 4))
                        link(l, tt_(halves(ptmp[:, :]), halves(gt[:, q % 2, :]), pair(2 * (q % 2) + 1), MUL))
                        tt_(mt, mt, ptmp[:, :], ADD).then_inc(merge_done.sem, 1)
                own[0] = first + 2 * 4
                for m in range(KT):
                    dve.wait_ge(part.sem, part.upto(l, PART0["out"] + m + 1))
                    residual(l, m, m % 2, 40)
                ffn(l, 1)
                assert own[0] == VEC_LINKS, ("VEC_LINKS", own[0])


def kernel(**a):
    import concourse.bacc as bacc
    from concourse.bass_utils import run_bass_kernel_spmd

    a = {k: np.asarray(v) for k, v in a.items()}
    L = DEPTH

    def c(v):
        return np.ascontiguousarray(v)

    def feat(v):
        v = v.reshape(v.shape[:-1] + (-1, P))
        return np.moveaxis(v, (-1, -2), (0, 1))

    tokens = np.concatenate([a["x_prompt"][0], a["x_sample"].reshape(TS, D_MODEL)], 0)
    cond = np.concatenate([a["c_prompt"], a["c_sample"]], 0)
    packs = []
    for l in range(L):
        vecs = [a["ada_b"][l], a["norm_g"][l].reshape(-1), a["rwkv_mu"][l], a["conv_w"][l].reshape(-1),
                a["rwkv_w0"][l], a["rwkv_a0"][l], a["rwkv_k_k"][l], a["rwkv_k_a"][l], a["rwkv_r_k"][l],
                a["rwkv_lnx_g"][l], a["rwkv_lnx_b"][l], a["pool_scale"][l],
                np.tile(a["q_norm_g"][l], 2), np.tile(a["k_norm_g"][l], 2)]
        cols = [np.concatenate(vecs).reshape(128, P).T, np.broadcast_to(a["sb_bias"][l], (P, NH)),
                np.concatenate([a["rwkv_w2"][l], a["rwkv_a2"][l]], 0), a["rwkv_g2"][l]]
        bd = np.zeros((P, 2, P), np.float32)
        for g in range(4):
            r = slice(64 * (g % 2), 64 * (g % 2) + 64)
            bd[r, g // 2, r] = a["pool_w"][l, g]
        cols += [bd.reshape(P, -1), feat(a["state_conv"][l]).reshape(P, -1),
                 feat(a["state_shift"][l]).reshape(P, -1), feat(a["state_pool"][l]).reshape(P, -1)]
        w = a["state_wkv"][l].reshape(NSEQ, 2, 2, HD, HD).transpose(2, 4, 1, 0, 3)
        cols.append(w.reshape(P, -1))
        packs.append(np.concatenate(cols, 1))

    def panels(w, n):
        return c(w.reshape(L, KT, P, n, 256).transpose(0, 3, 2, 1, 4).reshape(L * n, P, PANEL))

    up = a["w_ffn_up"].reshape(L, 2, KT, P, 2, FT, P).transpose(0, 1, 5, 3, 2, 4, 6)
    down = a["w_ffn_down"].reshape(L, 2, 2, DOWN_K, P, KT, P).transpose(0, 1, 5, 2, 4, 3, 6)
    order = list(BRANCH_ORDER)
    gate = a["w_gate"][:, order].reshape(L, 4, KT, P, 4, 256).transpose(0, 1, 4, 3, 2, 5)
    branch = a["w_branch"][:, order].reshape(L, 4, 2, P, 4, 256).transpose(0, 1, 4, 3, 2, 5)
    keys = a["cache_k"].reshape(L * NPHYS, PAGE, 2, 2, HD).transpose(0, 3, 4, 2, 1)
    cache = np.concatenate([keys.reshape(L * NPHYS, P, 256), a["cache_v"].reshape(L * NPHYS, PAGE, 256)], 0)
    arrays = {
        "xT": c(feat(tokens)), "cT": c(feat(cond)), "constants": constants(), "params": c(np.stack(packs)),
        "page_table": c(a["page_table"].reshape(1, -1).astype(np.int32)),
        "w_ada": panels(a["ada_w"], 36), "w_up": c(up.reshape(L * 44, P, PANEL)),
        "w_down": c(down.reshape(L * 32, P, DOWN_K * P)), "w_in": panels(a["w_in"], 11)[(np.arange(L)[:, None] * 11 + IN_FROM).reshape(-1)],
        "w_gate": c(gate.reshape(L * 16, P, PANEL)), "w_branch": c(branch.reshape(L * 16, P, 512)),
        "w_out": panels(a["w_out"], 4), "cache": c(cache),
    }
    outs = {"o_y": (P, KT, T), "o_k": (L, P, 2, T), "o_v": (L, P, 2, T), "o_conv": (L, P, 2, 18),
            "o_shift": (L, P, 8, 9), "o_wkv": (L, P, 2, 9, HD), "o_pool": (L, P, 2, 9 * CTX)}

    nc = bacc.Bacc("TRN2", target_bir_lowering=False, num_devices=1)
    ins = [nc.dram_tensor(k, v.shape, mybir.dt.from_np(v.dtype), kind="ExternalInput").ap()
           for k, v in arrays.items()]
    outp = [nc.dram_tensor(k, s, F32, kind="ExternalOutput").ap() for k, s in outs.items()]
    build(nc, *ins, *outp)
    r = run_bass_kernel_spmd(nc, [arrays], core_ids=[0]).results[0]

    def rows(v):
        return c(v.transpose(2, 1, 0).reshape(v.shape[2], -1))

    def both(v, prompt, sample):
        t = np.stack([rows(v[l]) for l in range(L)])
        n = int(np.prod(prompt[:-1]))
        return c(t[:, :n].reshape((L,) + prompt)), c(t[:, n:].reshape((L,) + sample))

    yy = rows(r["o_y"])
    kp, ks = both(r["o_k"], (1, TP, D_BR), (NSEQ, TD, D_BR))
    vp, vs = both(r["o_v"], (1, TP, D_BR), (NSEQ, TD, D_BR))
    cp, cs = both(r["o_conv"], (1, 2, D_BR), (NSEQ, 2, D_BR))
    shp, shs = both(r["o_shift"], (1, D_MODEL), (NSEQ, D_MODEL))
    pp, pl = both(r["o_pool"], (1, CTX, D_BR), (NSEQ, CTX, D_BR))
    wkv = r["o_wkv"].reshape(L, 2, HD, 2, 9, HD).transpose(0, 4, 3, 1, 5, 2).reshape(L, 9, NH, HD, HD)
    return (c(yy[:TP].reshape(1, TP, D_MODEL)), c(yy[TP:].reshape(NSEQ, TD, D_MODEL)),
            kp.reshape(L, 1, TP, NH, HD), vp.reshape(L, 1, TP, NH, HD), cp, shp, c(wkv[:, 0:1]), pp,
            ks.reshape(L, NSEQ, TD, NH, HD), vs.reshape(L, NSEQ, TD, NH, HD), cs, shs, c(wkv[:, 1:]), pl)
```
